# Optimizing a Trainium2 kernel written in Bass

```python
import jax, jax.numpy as jnp
from jax import lax
import numpy as np

D_MODEL = 1024
BATCH = 1
SEQ = 1024
DEPTH = 2

N_MIXERS = 2
RMS_EPS = 1e-6

SB_HEADS = 8
SB_HEAD_DIM = D_MODEL // SB_HEADS
SB_WIDTH = SB_HEADS * SB_HEAD_DIM
Q_BLOCK = 128

HG_HEAD_K = 128
HG_HEADS = D_MODEL // HG_HEAD_K
HG_HEAD_V = D_MODEL // HG_HEADS
HG_KEY_WIDTH = HG_HEADS * HG_HEAD_K
HG_VALUE_WIDTH = HG_HEADS * HG_HEAD_V
CHUNK = 64

kernel_name = "hybrid_stickbreaking_hgrn2_trunk"

def rms_norm(x, gain):
    xf = x.astype(jnp.float32)
    y = xf * lax.rsqrt(jnp.mean(xf * xf, axis=-1, keepdims=True) + RMS_EPS)
    return (y * gain.astype(jnp.float32)).astype(x.dtype)

def split_heads(t, n_heads):
    b, s, _ = t.shape
    return t.reshape(b, s, n_heads, -1).transpose(0, 2, 1, 3)

def merge_heads(t):
    b, h, s, d = t.shape
    return t.transpose(0, 2, 1, 3).reshape(b, s, h * d)

def stick_breaking_attention(q, k, v):
    seq = q.shape[2]
    scale = q.shape[-1] ** -0.5
    outs = []
    for blk in range(seq // Q_BLOCK):
        start = blk * Q_BLOCK
        end = start + Q_BLOCK
        qb = q[:, :, start:end]
        kb = k[:, :, :end]
        vb = v[:, :, :end]
        z = jnp.einsum('bhtd,bhsd->bhts', qb, kb).astype(jnp.float32) * scale
        t_idx = start + jnp.arange(Q_BLOCK)[:, None]
        s_idx = jnp.arange(end)[None, :]
        causal = s_idx < t_idx
        log_beta = jax.nn.log_sigmoid(z)
        log_skip_j = jnp.where(causal, jax.nn.log_sigmoid(-z), 0.0)
        log_skip = lax.cumsum(log_skip_j, axis=3, reverse=True) - log_skip_j
        weights = jnp.where(causal, jnp.exp(log_beta + log_skip), 0.0)
        outs.append(jnp.einsum('bhts,bhsd->bhtd', weights.astype(vb.dtype), vb))
    return jnp.concatenate(outs, axis=2)

def hgrn2_chunkwise(q, log_f, k, i):
    b, h, s, dk = q.shape
    dv = i.shape[-1]
    n = s // CHUNK

    def to_chunks(a):
        return a.astype(jnp.float32).reshape(b, h, n, CHUNK, a.shape[-1]).transpose(2, 0, 1, 3, 4)

    qc, gc, kc, ic = to_chunks(q), to_chunks(log_f), to_chunks(k), to_chunks(i)
    incl = jnp.tril(jnp.ones((CHUNK, CHUNK), dtype=bool))[None, None, :, :, None]

    def step(state, xs):
        qb, gb, kb, ib = xs
        g_cum = jnp.cumsum(gb, axis=2)
        rel = g_cum[:, :, :, None, :] - g_cum[:, :, None, :, :]
        decay = jnp.exp(jnp.where(incl, rel, -jnp.inf))
        scores = jnp.einsum('bhtd,bhsd,bhtsd->bhts', qb, kb, decay)
        o_intra = jnp.einsum('bhts,bhsv->bhtv', scores, ib)
        o_inter = jnp.einsum('bhtd,bhdv->bhtv', qb * jnp.exp(g_cum), state)
        g_last = g_cum[:, :, -1:, :]
        new_state = (jnp.exp(g_last[:, :, 0, :])[..., None] * state
                     + jnp.einsum('bhsd,bhsv->bhdv', kb * jnp.exp(g_last - g_cum), ib))
        return new_state, o_intra + o_inter

    state0 = jnp.zeros((b, h, dk, dv), jnp.float32)
    _, oc = lax.scan(step, state0, (qc, gc, kc, ic))
    return oc.transpose(1, 2, 0, 3, 4).reshape(b, h, s, dv).astype(i.dtype)

def stick_breaking_layer(h, norm_gain, w_in, q_gain, k_gain, w_out):
    u = rms_norm(h, norm_gain)
    proj = u @ w_in
    q, k, v, gate = jnp.split(proj, 4, axis=-1)
    q = rms_norm(split_heads(q, SB_HEADS), q_gain)
    k = rms_norm(split_heads(k, SB_HEADS), k_gain)
    v = split_heads(v, SB_HEADS)
    o = merge_heads(stick_breaking_attention(q, k, v))
    return (o * jax.nn.silu(gate)) @ w_out

def hgrn2_layer(h, norm_gain, w_in, o_gain, w_out, lower_bound):
    u = rms_norm(h, norm_gain)
    proj = u @ w_in
    q, f_pre, i, gate = jnp.split(
        proj, [HG_KEY_WIDTH, 2 * HG_KEY_WIDTH, 2 * HG_KEY_WIDTH + HG_VALUE_WIDTH], axis=-1)
    q = split_heads(jax.nn.silu(q), HG_HEADS)
    f_pre = split_heads(f_pre, HG_HEADS).astype(jnp.float32)
    lb = lower_bound.astype(jnp.float32).reshape(HG_HEADS, 1, HG_HEAD_K)
    log_f = jnp.logaddexp(jnp.log(lb), jnp.log1p(-lb) + jax.nn.log_sigmoid(f_pre))
    k_in = -jnp.expm1(log_f)
    o = hgrn2_chunkwise(q, log_f, k_in, split_heads(i, HG_HEADS))
    o = merge_heads(rms_norm(o, o_gain))
    return (o * jax.nn.silu(gate)) @ w_out

def setup_inputs(seed: int = 0) -> dict:
    key = jax.random.key(seed)
    ks = jax.random.split(key, 12)
    n_a = (DEPTH + 1) // 2
    n_b = DEPTH // 2

    def normal(k, shape, scale):
        return jax.random.normal(k, shape, jnp.float32) * scale

    return {
        "x": normal(ks[0], (BATCH, SEQ, D_MODEL), 1.0),
        "sb_norm": 1.0 + normal(ks[1], (n_a, D_MODEL), 0.02),
        "sb_w_in": normal(ks[2], (n_a, D_MODEL, 4 * SB_WIDTH), D_MODEL ** -0.5),
        "sb_q_gain": 1.0 + normal(ks[3], (n_a, SB_HEAD_DIM), 0.02),
        "sb_k_gain": 1.0 + normal(ks[4], (n_a, SB_HEAD_DIM), 0.02),
        "sb_w_out": normal(ks[5], (n_a, SB_WIDTH, D_MODEL), SB_WIDTH ** -0.5),
        "hg_norm": 1.0 + normal(ks[6], (n_b, D_MODEL), 0.02),
        "hg_w_in": normal(ks[7], (n_b, D_MODEL, 2 * HG_KEY_WIDTH + 2 * HG_VALUE_WIDTH), D_MODEL ** -0.5),
        "hg_o_gain": 1.0 + normal(ks[8], (n_b, HG_HEAD_V), 0.02),
        "hg_w_out": normal(ks[9], (n_b, HG_VALUE_WIDTH, D_MODEL), HG_VALUE_WIDTH ** -0.5),
        "hg_lb_logits": normal(ks[10], (DEPTH, HG_KEY_WIDTH), 0.1),
    }

def reference(x, sb_norm, sb_w_in, sb_q_gain, sb_k_gain, sb_w_out,
              hg_norm, hg_w_in, hg_o_gain, hg_w_out, hg_lb_logits):
    lb_p = jax.nn.softmax(hg_lb_logits.astype(jnp.float32), axis=0)
    lb_table = jnp.cumsum(lb_p, axis=0) - lb_p[0]
    h = x
    for layer in range(DEPTH):
        j = layer // N_MIXERS
        if layer % N_MIXERS == 0:
            h = h + stick_breaking_layer(h, sb_norm[j], sb_w_in[j], sb_q_gain[j],
                                         sb_k_gain[j], sb_w_out[j])
        else:
            h = h + hgrn2_layer(h, hg_norm[j], hg_w_in[j], hg_o_gain[j], hg_w_out[j],
                                lb_table[layer])
    return h


_drawn_inputs = setup_inputs


def setup_inputs(seed=0):
    import zlib

    import numpy as np

    out = dict(_drawn_inputs(seed))
    spreads = {}
    factors = {'sb_norm': 4.118,
     'sb_q_gain': 8.0,
     'sb_k_gain': 8.0,
     'hg_norm': 3.879,
     'hg_o_gain': 5.51,
     'hg_lb_logits': 8.0}
    for name, (base, spread) in spreads.items():
        noise = np.random.default_rng([zlib.crc32(name.encode()), seed]).standard_normal(out[name].shape)
        drawn = base * np.exp(spread * noise) if base else spread * noise
        out[name] = __import__('jax').numpy.asarray(drawn.astype(out[name].dtype))
    for name, factor in factors.items():
        out[name] = (out[name] * factor).astype(out[name].dtype)
    return out
```

```python
from contextlib import ExitStack

import concourse.bass as bass
from concourse import mybir

ALU = mybir.AluOpType
ACT = mybir.ActivationFunctionType
AX_X = mybir.AxisListType.X
F32 = mybir.dt.float32
F32R = mybir.dt.float32r
BF16 = mybir.dt.bfloat16
I32 = mybir.dt.int32

P = 128
D_MODEL = 1024
SEQ = 1024
KT = D_MODEL // P
TILES = SEQ // P
HEADS = D_MODEL // P
HALF = 512
RMS_EPS = 1e-6
NEG = -1e30
LEVELS = [1, 2, 4, 8, 16, 32, 64]


def matmul_exact(pe, out, w_hi, w_lo, m_hi, m_lo, start, stop):
    pe.matmul(out, w_hi, m_hi, start=start, stop=False, skip_group_check=True)
    pe.matmul(out, w_hi, m_lo, start=False, stop=False, skip_group_check=True)
    return pe.matmul(out, w_lo, m_hi, start=False, stop=stop, skip_group_check=True)


def build_trunk(nc, x, sb_norm, sb_w_in, sb_q_gain, sb_k_gain, sb_w_out,
                hg_norm, hg_w_in, hg_o_gain, hg_w_out, hg_lb_logits, out):
    x = x.rearrange("b s d -> (b s) d")
    out = out.rearrange("b s d -> (b s) d")
    mixed = nc.dram_tensor("mixed_scratch", (2, HEADS, P, SEQ), F32).ap()
    h1 = nc.dram_tensor("h1_scratch", (SEQ, D_MODEL), F32).ap()

    with ExitStack() as ctx:
        def sb(name, shape, dt=F32, into=ctx):
            return into.enter_context(nc.sbuf_tensor(name, shape, dt))

        consts = {
            "ident": sb("ident", [P, P]),
            "ident_bf": sb("ident_bf", [P, P], BF16),
            "causal_neg": sb("causal_neg", [P, P], BF16),
            "ones_col": sb("ones_col", [P, 1]),
            "minus_half": sb("minus_half", [P, TILES]),
            "minus_one": sb("minus_one", [P, 1]),
            "head_eps": sb("head_eps", [P, TILES]),
            "level_mask": sb("level_mask", [P, len(LEVELS), P // 2]),
            "q_gain": sb("q_gain", [P, 1]),
            "k_gain": sb("k_gain", [P, 1]),
            "qk_gain": sb("qk_gain", [P, 1]),
            "o_gain": sb("o_gain", [P, 1]),
            "o_scale": sb("o_scale", [P, 1]),
            "logits": sb("logits", [P, 2, HEADS]),
            "logit_gap": sb("logit_gap", [P, HEADS]),
            "lower": sb("lower", [P, HEADS]),
            "one_minus_lower": sb("one_minus_lower", [P, HEADS]),
        }
        ut_hi = sb("ut_hi", [P, KT, SEQ], F32R)
        ut_lo = sb("ut_lo", [P, KT, SEQ], F32R)

        build_constants_and_norm(nc, consts, x, sb_norm, sb_q_gain, sb_k_gain, hg_o_gain,
                                 hg_lb_logits, ut_hi, ut_lo)
        build_attention(nc, consts, sb_w_in, ut_hi, ut_lo, mixed[0])
        build_output_projection(nc, "l0", consts, mixed[0], sb_w_out, x, h1, hg_norm, ut_hi, ut_lo)
        build_hgrn(nc, consts, hg_w_in, ut_hi, ut_lo, mixed[1])
        build_output_projection(nc, "l1", consts, mixed[1], hg_w_out, h1, out, None, ut_hi, ut_lo)


def build_constants_and_norm(nc, c, x, gain, q_gain, k_gain, o_gain, lb_logits, ut_hi, ut_lo):
    with ExitStack() as ctx:
        def sb(name, shape, dt=F32):
            return ctx.enter_context(nc.sbuf_tensor("n_" + name, shape, dt))

        def sem(name):
            return ctx.enter_context(nc.semaphore("n_" + name))

        gain_rows = sb("gain_rows", [P, D_MODEL])
        h_tile = [sb(f"h_tile{i}", [P, D_MODEL]) for i in range(2)]
        squares = sb("squares", [P, D_MODEL])
        sum_sq = [sb(f"sum_sq{i}", [P, 1]) for i in range(2)]
        mean_sq = [sb(f"mean_sq{i}", [P, 1]) for i in range(2)]
        inv_rms = [sb(f"inv_rms{i}", [P, 1]) for i in range(2)]
        normed = [sb(f"normed{i}", [P, D_MODEL]) for i in range(2)]
        turned = [ctx.enter_context(nc.psum_tensor(f"n_turned{i}", [P, 4, P], F32)) for i in range(4)]

        small_loaded = sem("small_loaded")
        gain_loaded = sem("gain_loaded")
        x_loaded = [sem(f"x_loaded{i}") for i in range(2)]
        pool_made = sem("pool_made")
        dve_made = sem("dve_made")
        act_made = sem("act_made")
        sum_ready = sem("sum_ready")
        mean_ready = sem("mean_ready")
        rms_ready = sem("rms_ready")
        normed_ready = sem("normed_ready")
        turned_ready = sem("turned_ready")
        hi_ready = sem("hi_ready")
        lo_ready = sem("lo_ready")

        block = ctx.enter_context(nc.Block())

        @block.sync
        def _(sp):
            for i in range(TILES):
                if i >= 2:
                    sp.wait_ge(normed_ready, i - 1)
                sp.dma_start(h_tile[i % 2][:, :], x[i * P:(i + 1) * P, :]).then_inc(x_loaded[i % 2], 16)
                if i == 0:
                    sp.dma_start(gain_rows[:, :], gain[0:1, :].to_broadcast([P, D_MODEL])).then_inc(gain_loaded, 16)
            sp.dma_start(c["q_gain"][:, :], q_gain.rearrange("a d -> d a"),
                         allow_slow_non_contiguous=True).then_inc(small_loaded, 16)
            sp.dma_start(c["k_gain"][:, :], k_gain.rearrange("a d -> d a"),
                         allow_slow_non_contiguous=True).then_inc(small_loaded, 16)
            sp.dma_start(c["o_gain"][:, :], o_gain.rearrange("a d -> d a"),
                         allow_slow_non_contiguous=True).then_inc(small_loaded, 16)
            for layer in range(2):
                sp.dma_start(c["logits"][:, layer, :],
                             lb_logits[layer].rearrange("(h d) -> d h", d=P),
                             allow_slow_non_contiguous=True).then_inc(small_loaded, 16)

        @block.gpsimd
        def _(pool):
            pool.memset(c["minus_half"][:, :], -0.5).then_inc(pool_made, 1)
            pool.memset(c["ident"][:, :], 0.0).then_inc(pool_made, 1)
            pool.memset(c["minus_one"][:, :], -1.0)
            pool.memset(c["head_eps"][:, :], RMS_EPS * P)
            pool.memset(c["ones_col"][:, :], 1.0).then_inc(pool_made, 1)
            pool.memset(c["causal_neg"][:, :], 0.0).then_inc(pool_made, 1)
            pool.memset(c["level_mask"][:, :, :], 1.0).then_inc(pool_made, 1)
            pool.wait_ge(pool_made, 5)
            pool.affine_select(out=c["ident"][:, :], in_=c["ident"][:, :], compare_op=ALU.not_equal, fill=1.0,
                               base=0, pattern=[[-1, P]], channel_multiplier=1).then_inc(pool_made, 1)
            pool.affine_select(out=c["causal_neg"][:, :], in_=c["causal_neg"][:, :], compare_op=ALU.is_gt, fill=NEG,
                               base=0, pattern=[[-1, P]], channel_multiplier=1).then_inc(pool_made, 1)
            for n, half in enumerate(LEVELS):
                mask = c["level_mask"][:, n, :].rearrange("p (b r) -> p b r", r=half)
                pool.affine_select(out=mask, in_=mask, compare_op=ALU.is_ge, fill=0.0, base=0,
                                   pattern=[[-2 * half, P // 2 // half], [0, half]],
                                   channel_multiplier=1).then_inc(pool_made, 1)
                pool.wait_ge(pool_made, 8 + 2 * n)
                pool.affine_select(out=mask, in_=mask, compare_op=ALU.is_gt, fill=0.0, base=half,
                                   pattern=[[2 * half, P // 2 // half], [0, half]],
                                   channel_multiplier=-1).then_inc(pool_made, 1)
            for i in range(TILES):
                pool.wait_ge(sum_ready, i + 1)
                pool.tensor_scalar(mean_sq[i % 2][:, :], sum_sq[i % 2][:, :], 1.0 / D_MODEL, RMS_EPS,
                                   ALU.mult, ALU.add).then_inc(mean_ready, 1)
                pool.wait_ge(mean_ready, i + 1)
                if i >= 2:
                    pool.wait_ge(normed_ready, i - 1)
                pool.tensor_tensor(inv_rms[i % 2][:, :], mean_sq[i % 2][:, :], c["minus_half"][:, 0:1],
                                   ALU.pow).then_inc(rms_ready, 1)

        @block.scalar
        def _(act):
            for i in range(TILES + 1):
                if i < TILES:
                    act.wait_ge(x_loaded[i % 2], 16 * (i // 2 + 1))
                    if i >= 1:
                        act.wait_ge(sum_ready, i)
                    if i >= 2:
                        act.wait_ge(mean_ready, i - 1)
                    act.activation(squares[:, :], h_tile[i % 2][:, :], ACT.Square,
                                   accum_out=sum_sq[i % 2][:, :]).then_inc(sum_ready, 1)
                if i >= 1:
                    j = i - 1
                    for half in range(2):
                        act.wait_ge(turned_ready, 2 * j + half + 1)
                        act.activation(ut_hi[:, 4 * half:4 * half + 4, j * P:(j + 1) * P],
                                       turned[(2 * j + half) % 4][:, :, :], ACT.Copy).then_inc(hi_ready, 1)
            act.wait_ge(dve_made, 3)
            act.activation(c["lower"][:, :], c["logit_gap"][:, :], ACT.Sigmoid).then_inc(act_made, 1)
            act.activation(c["one_minus_lower"][:, :], c["logit_gap"][:, :], ACT.Sigmoid,
                           scale=-1.0).then_inc(act_made, 1)

        @block.vector
        def _(dve):
            dve.wait_ge(pool_made, 7)
            dve.tensor_copy(c["ident_bf"][:, :], c["ident"][:, :]).then_inc(dve_made, 1)
            dve.wait_ge(gain_loaded, 16)
            for i in range(TILES + 1):
                if i < TILES:
                    dve.wait_ge(rms_ready, i + 1)
                    dve.wait_ge(x_loaded[i % 2], 16 * (i // 2 + 1))
                    if i >= 2:
                        dve.wait_ge(turned_ready, 2 * (i - 1))
                    dve.scalar_tensor_tensor(out=normed[i % 2][:, :], in0=h_tile[i % 2][:, :],
                                             scalar=inv_rms[i % 2][:, 0:1], in1=gain_rows[:, :],
                                             op0=ALU.mult, op1=ALU.mult).then_inc(normed_ready, 1)
                if i >= 1:
                    j = i - 1
                    for half in range(2):
                        dve.wait_ge(hi_ready, 2 * j + half + 1)
                        dve.tensor_tensor(ut_lo[:, 4 * half:4 * half + 4, j * P:(j + 1) * P],
                                          turned[(2 * j + half) % 4][:, :, :],
                                          ut_hi[:, 4 * half:4 * half + 4, j * P:(j + 1) * P].bitcast(F32),
                                          ALU.subtract).then_inc(lo_ready, 1)
            dve.wait_ge(small_loaded, 16 * 5)
            dve.scalar_tensor_tensor(out=c["qk_gain"][:, :], in0=c["q_gain"][:, :], scalar=float(P) ** 0.5,
                                     in1=c["k_gain"][:, :], op0=ALU.mult, op1=ALU.mult).then_inc(dve_made, 1)
            dve.tensor_scalar(c["o_scale"][:, :], c["o_gain"][:, :], float(P) ** 0.5, None,
                              ALU.mult)
            dve.tensor_tensor(c["logit_gap"][:, :], c["logits"][:, 1, :], c["logits"][:, 0, :],
                              ALU.subtract).then_inc(dve_made, 1)

        @block.tensor
        def _(pe):
            pe.wait_ge(pool_made, 7)
            for i in range(TILES):
                pe.wait_ge(normed_ready, i + 1)
                for half in range(2):
                    use = 2 * i + half
                    if use >= 4:
                        pe.wait_ge(lo_ready, use - 3)
                    for q in range(4):
                        kt = 4 * half + q
                        last = pe.transpose(turned[use % 4][:, q, :], normed[i % 2][:, kt * P:(kt + 1) * P],
                                            c["ident"][:, :])
                    last.then_inc(turned_ready, 1)


def build_attention(nc, c, w_in, ut_hi, ut_lo, mixed):
    Z_UNITS = [1, 1, 1, 1, 2, 2, 2, 2]
    ENDS = [sum(Z_UNITS[:i + 1]) for i in range(TILES)]
    UNITS = ENDS[-1]
    NAT, GATE = TILES, 2
    USES = NAT + GATE
    PAIRS = TILES // 2

    with ExitStack() as ctx:
        def sb(name, shape, dt=F32):
            return ctx.enter_context(nc.sbuf_tensor("a_" + name, shape, dt))

        def psum(name, shape):
            return ctx.enter_context(nc.psum_tensor("a_" + name, shape, F32))

        def sem(name):
            return ctx.enter_context(nc.semaphore("a_" + name))

        stage = [sb(f"stage{p}", [P, KT, P]) for p in range(4)]
        w_qkv_hi = sb("w_qkv_hi", [P, KT, 3, P], F32R)
        w_qkv_lo = sb("w_qkv_lo", [P, KT, 3, P], F32R)
        w_gate_hi = sb("w_gate_hi", [P, KT, P], F32R)
        w_gate_lo = sb("w_gate_lo", [P, KT, P], F32R)
        raw = [sb(f"raw{i}", [P, 3, P]) for i in range(4)]
        squares = [sb(f"squares{i}", [P, P]) for i in range(2)]
        sum_sq = [sb(f"sum_sq{i}", [P, 2]) for i in range(2)]
        mean_sq = [sb(f"mean_sq{i}", [P, 2]) for i in range(2)]
        inv_rms = [[sb(f"inv_rms{b}_{i}", [P, 3]) for i in range(TILES)] for b in range(2)]
        k_scaled = [sb(f"k_scaled{i}", [P, P]) for i in range(4)]
        qt_hi = [sb(f"qt_hi{b}", [P, SEQ], F32R) for b in range(2)]
        qt_lo = [sb(f"qt_lo{b}", [P, SEQ], F32R) for b in range(2)]
        kt_hi = [sb(f"kt_hi{b}", [P, SEQ], F32R) for b in range(2)]
        kt_lo = [sb(f"kt_lo{b}", [P, SEQ], F32R) for b in range(2)]
        v_hi = [sb(f"v_hi{b}", [P, TILES, P], F32R) for b in range(2)]
        v_lo = [sb(f"v_lo{b}", [P, TILES, P], F32R) for b in range(2)]
        gated = [sb(f"gated{b}", [P, SEQ]) for b in range(2)]
        beta = [sb(f"beta{i}", [P, SEQ]) for i in range(2)]
        skip = [sb(f"skip{i}", [P, SEQ + 1]) for i in range(2)]
        wt_hi = sb("wt_hi", [P, TILES, 2, P], F32R)
        wt_lo = sb("wt_lo", [P, TILES, 2, P], F32R)

        p_proj = [psum(f"p_proj{i}", [P, HALF]) for i in range(2)]
        p_z = [psum(f"p_z{i}", [P, HALF]) for i in range(3)]
        p_turn = [psum(f"p_turn{i}", [P, 4, P]) for i in range(2)]
        p_o = psum("p_o", [P, 2, P])

        w_loaded = [sem(f"w_loaded{p}") for p in range(4)]
        w_hi_ready = [sem(f"w_hi_ready{p}") for p in range(4)]
        w_ready = [sem(f"w_ready{p}") for p in range(4)]
        proj_done = sem("proj_done")
        raw_ready = sem("raw_ready")
        v_hi_ready = sem("v_hi_ready")
        v_ready = sem("v_ready")
        sums_ready = sem("sums_ready")
        mean_ready = sem("mean_ready")
        rms_ready = sem("rms_ready")
        k_ready = sem("k_ready")
        qk_turned = sem("qk_turned")
        qk_hi_ready = sem("qk_hi_ready")
        qk_ready = sem("qk_ready")
        gate_sigmoid = sem("gate_sigmoid")
        gate_ready = sem("gate_ready")
        z_done = sem("z_done")
        sigmoids_ready = sem("sigmoids_ready")
        scan_done = sem("scan_done")
        weights_ready = sem("weights_ready")
        weights_turned = sem("weights_turned")
        wt_hi_ready = sem("wt_hi_ready")
        wt_ready = sem("wt_ready")
        o_done = sem("o_done")
        o_gated = sem("o_gated")
        o_stored = sem("o_stored")
        skip_set = sem("skip_set")

        turn_of, turn_alone = {}, {}
        for i in range(USES):
            if 1 <= i <= TILES:
                for u in range(Z_UNITS[i - 1]):
                    turn_of[("w", ENDS[i - 1] - Z_UNITS[i - 1] + u)] = len(turn_of)
            if i >= 2 and i % 2 == 0:
                turn_of[("qk", i // 2 - 1)] = len(turn_of)
                turn_alone[("qk", i // 2 - 1)] = len(turn_alone)

        def heads(eng, step):
            step(-1, 1, False, True)
            step(0, 0, True, True)
            with eng.Fori(0, (HEADS - 4) // 2) as pair:
                step(pair * 2 + 1, 1, True, True)
                step(pair * 2 + 2, 0, True, True)
            step(HEADS - 3, 1, True, True)
            step(HEADS - 2, 0, True, True)
            step(HEADS - 1, 1, True, False)

        def known_first(h):
            return isinstance(h, int) and h <= 0

        block = ctx.enter_context(nc.Block())

        @block.sync
        def _(sp):
            def load(h, p):
                if not known_first(h):
                    sp.wait_ge(w_ready[p], h)
                columns = w_in[0, :, bass.ds(p * D_MODEL + h * P, P)]
                sp.dma_start(stage[p][:, :, :], columns.rearrange("(k p) c -> p k c", p=P)).then_inc(w_loaded[p], 16)

            def store(h, b):
                sp.wait_ge(o_gated, PAIRS * h + PAIRS)
                sp.dma_start(mixed[bass.ds(h, 1), :, :].rearrange("o p s -> p (o s)"),
                             gated[b][:, :]).then_inc(o_stored, 16)

            for h in range(3):
                for p in range(4):
                    load(h, p)
            store(0, 0)
            for p in range(4):
                load(3, p)
            with sp.Fori(0, 2) as pair:
                for b in (1, 0):
                    store(pair * 2 + 2 - b, b)
                    for p in range(4):
                        load(pair * 2 + 5 - b, p)
            for h in range(5, HEADS):
                store(h, h % 2)
            sp.wait_ge(o_stored, 16 * HEADS)

        @block.scalar
        def _(act):
            def split_hi(h, p):
                if not known_first(h):
                    act.wait_ge(proj_done, USES * (h - 1) + (NAT if p < 3 else USES))
                act.wait_ge(w_loaded[p], 16 * h + 16)
                dst = w_qkv_hi[:, :, p, :] if p < 3 else w_gate_hi[:, :, :]
                act.activation(dst, stage[p][:, :, :], ACT.Copy).then_inc(w_hi_ready[p], 1)

            def step(h, b, attends, projects):
                n, nb = h + 1, 1 - b
                for i in range(USES):
                    if attends and i < TILES:
                        for u in range(Z_UNITS[i]):
                            width = min(HALF, (i + 1) * P - u * HALF)
                            unit = ENDS[i] - Z_UNITS[i] + u
                            act.wait_ge(z_done, UNITS * h + unit + 1)
                            if u == 0:
                                act.wait_ge(rms_ready, TILES * h + i + 1)
                                if i >= 2:
                                    act.wait_ge(weights_turned, UNITS * h + ENDS[i - 2])
                                elif not known_first(h):
                                    act.wait_ge(weights_turned, UNITS * (h - 1) + ENDS[i + 6])
                                else:
                                    act.wait_ge(skip_set, 2)
                            cols = slice(u * HALF, u * HALF + width)
                            act.activation(skip[i % 2][:, cols], p_z[unit % 3][:, 0:width], ACT.Sigmoid,
                                           scale=inv_rms[b][i][:, 2:3])
                            act.activation(beta[i % 2][:, cols], p_z[unit % 3][:, 0:width], ACT.Sigmoid,
                                           scale=inv_rms[b][i][:, 0:1]).then_inc(sigmoids_ready, 1)
                    if not attends and i == 0:
                        for p in range(3):
                            split_hi(0, p)
                    if projects and i < NAT:
                        act.wait_ge(proj_done, USES * n + i + 1)
                        if i >= 4 or not known_first(n):
                            act.wait_ge(qk_turned, PAIRS * n + (i - 4) // 2 + 1)
                            act.wait_ge(v_ready, NAT * n + i - 3)
                        act.activation(raw[i % 4][:, :, :],
                                       p_proj[i % 2][:, 0:3 * P].rearrange("p (a b) -> p a b", a=3),
                                       ACT.Copy).then_inc(raw_ready, 1)
                    if projects and i == 3:
                        split_hi(n, 3)
                    if projects and i == 8 and not (isinstance(n, int) and n == HEADS - 1):
                        for p in range(3):
                            split_hi(n + 1, p)
                    if attends and 1 <= i <= TILES:
                        j = i - 1
                        for u in range(Z_UNITS[j]):
                            unit = ENDS[j] - Z_UNITS[j] + u
                            act.wait_ge(weights_turned, UNITS * h + unit + 1)
                            if not (known_first(h) and j < 2):
                                act.wait_ge(o_done, PAIRS * h + j // 2)
                            nb_blocks = min(4, j + 1 - 4 * u)
                            turn = turn_of[("w", unit)] % 2
                            act.activation(wt_hi[:, 4 * u:4 * u + nb_blocks, j % 2, :],
                                           p_turn[turn][:, 0:nb_blocks, :], ACT.Copy).then_inc(wt_hi_ready, 1)
                    if projects and i >= 2 and i % 2 == 0:
                        m = i // 2 - 1
                        act.wait_ge(qk_turned, PAIRS * n + m + 1)
                        if not (isinstance(n, int) and n < 2):
                            act.wait_ge(z_done, UNITS * (n - 1))
                        turn = (turn_of if attends else turn_alone)[("qk", m)] % 2
                        cols = slice(2 * m * P, (2 * m + 2) * P)
                        act.activation(qt_hi[nb][:, cols], p_turn[turn][:, 0:2, :].rearrange("p a b -> p (a b)"),
                                       ACT.Copy)
                        act.activation(kt_hi[nb][:, cols], p_turn[turn][:, 2:4, :].rearrange("p a b -> p (a b)"),
                                       ACT.Copy, scale=c["qk_gain"][:, 0:1]).then_inc(qk_hi_ready, 1)
                    if projects and i >= NAT:
                        half = i - NAT
                        act.wait_ge(proj_done, USES * n + i + 1)
                        if not (isinstance(n, int) and n < 2):
                            act.wait_ge(o_stored, 16 * (n - 1))
                        act.activation(gated[nb][:, half * HALF:(half + 1) * HALF], p_proj[i % 2][:, :],
                                       ACT.Sigmoid).then_inc(gate_sigmoid, 1)

            heads(act, step)

        @block.vector
        def _(dve):
            for i in range(2):
                dve.memset(skip[i][:, :], 1.0).then_inc(skip_set, 1)

            def split_lo(h, p):
                if not known_first(h):
                    dve.wait_ge(proj_done, USES * (h - 1) + (NAT if p < 3 else USES))
                dve.wait_ge(w_hi_ready[p], h + 1)
                hi = w_qkv_hi[:, :, p, :] if p < 3 else w_gate_hi[:, :, :]
                lo = w_qkv_lo[:, :, p, :] if p < 3 else w_gate_lo[:, :, :]
                dve.tensor_tensor(lo, stage[p][:, :, :], hi.bitcast(F32), ALU.subtract).then_inc(w_ready[p], 1)

            def step(h, b, attends, projects):
                n, nb = h + 1, 1 - b
                for i in range(USES):
                    if attends and i < TILES:
                        width = (i + 1) * P
                        dve.wait_ge(sigmoids_ready, UNITS * h + ENDS[i])
                        chain = skip[i % 2][:, 0:width][:, ::-1]
                        dve.tensor_tensor_scan(chain, chain, chain, 1.0, ALU.mult, ALU.min).then_inc(scan_done, 1)
                        dve.wait_ge(scan_done, TILES * h + i + 1)
                        dve.tensor_tensor(beta[i % 2][:, 0:width], beta[i % 2][:, 0:width],
                                          skip[i % 2][:, 1:width + 1], ALU.mult).then_inc(weights_ready, 1)
                    if not attends and i == 0:
                        for p in range(3):
                            split_lo(0, p)
                    if projects and i < NAT:
                        dve.wait_ge(raw_ready, NAT * n + i + 1)
                        if i >= 2 or not known_first(n):
                            dve.wait_ge(mean_ready, NAT * n + i - 1)
                        if i >= 1 or not known_first(n):
                            dve.wait_ge(sums_ready, 2 * (NAT * n + i))
                        for part in range(2):
                            dve.tensor_tensor_reduce(squares[part][:, :], raw[i % 4][:, part, :],
                                                     raw[i % 4][:, part, :], 1.0, 0.0, ALU.mult, ALU.add,
                                                     sum_sq[i % 2][:, part:part + 1]).then_inc(sums_ready, 1)
                        if not (isinstance(n, int) and n < 2):
                            dve.wait_ge(o_done, PAIRS * (n - 1))
                        dve.tensor_copy(v_hi[nb][:, i, :], raw[i % 4][:, 2, :]).then_inc(v_hi_ready, 1)
                        dve.wait_ge(v_hi_ready, NAT * n + i + 1)
                        dve.tensor_tensor(v_lo[nb][:, i, :], raw[i % 4][:, 2, :], v_hi[nb][:, i, :].bitcast(F32),
                                          ALU.subtract).then_inc(v_ready, 1)
                    if projects and i == 3:
                        split_lo(n, 3)
                    if projects and i == 8 and not (isinstance(n, int) and n == HEADS - 1):
                        for p in range(3):
                            split_lo(n + 1, p)
                    if attends and i >= 3 and i % 2 == 1:
                        g = (i - 3) // 2
                        dve.wait_ge(o_done, PAIRS * h + g + 1)
                        dve.wait_ge(gate_ready, GATE * h + GATE)
                        cols = slice(2 * g * P, (2 * g + 2) * P)
                        dve.tensor_tensor(gated[b][:, cols], gated[b][:, cols],
                                          p_o[:, :, :].rearrange("p a b -> p (a b)"),
                                          ALU.mult).then_inc(o_gated, 1)
                    if attends and 1 <= i <= TILES:
                        j = i - 1
                        for u in range(Z_UNITS[j]):
                            unit = ENDS[j] - Z_UNITS[j] + u
                            dve.wait_ge(wt_hi_ready, UNITS * h + unit + 1)
                            if not (known_first(h) and j < 2):
                                dve.wait_ge(o_done, PAIRS * h + j // 2)
                            nb_blocks = min(4, j + 1 - 4 * u)
                            turn = turn_of[("w", unit)] % 2
                            dve.tensor_tensor(wt_lo[:, 4 * u:4 * u + nb_blocks, j % 2, :],
                                              p_turn[turn][:, 0:nb_blocks, :],
                                              wt_hi[:, 4 * u:4 * u + nb_blocks, j % 2, :].bitcast(F32),
                                              ALU.subtract).then_inc(wt_ready, 1)
                    if projects and i >= 2 and i % 2 == 0:
                        m = i // 2 - 1
                        dve.wait_ge(qk_hi_ready, PAIRS * n + m + 1)
                        if not (isinstance(n, int) and n < 2):
                            dve.wait_ge(z_done, UNITS * (n - 1))
                        turn = (turn_of if attends else turn_alone)[("qk", m)] % 2
                        cols = slice(2 * m * P, (2 * m + 2) * P)
                        dve.tensor_tensor(qt_lo[nb][:, cols], p_turn[turn][:, 0:2, :].rearrange("p a b -> p (a b)"),
                                          qt_hi[nb][:, cols].bitcast(F32), ALU.subtract)
                        dve.scalar_tensor_tensor(out=kt_lo[nb][:, cols],
                                                 in0=p_turn[turn][:, 2:4, :].rearrange("p a b -> p (a b)"),
                                                 scalar=c["qk_gain"][:, 0:1], in1=kt_hi[nb][:, cols].bitcast(F32),
                                                 op0=ALU.mult, op1=ALU.subtract).then_inc(qk_ready, 1)
                    if projects and i >= NAT:
                        half = i - NAT
                        cols = slice(half * HALF, (half + 1) * HALF)
                        dve.wait_ge(gate_sigmoid, GATE * n + half + 1)
                        dve.tensor_tensor(gated[nb][:, cols], gated[nb][:, cols], p_proj[i % 2][:, :],
                                          ALU.mult).then_inc(gate_ready, 1)

            heads(dve, step)

        @block.gpsimd
        def _(pool):
            def step(h, b, attends, projects):
                n, nb = h + 1, 1 - b
                if not projects:
                    return
                for i in range(NAT):
                    rms = inv_rms[nb][i]
                    pool.wait_ge(sums_ready, 2 * (NAT * n + i) + 2)
                    if i >= 2 or not known_first(n):
                        pool.wait_ge(rms_ready, NAT * n + i - 1)
                    pool.tensor_tensor(mean_sq[i % 2][:, :], sum_sq[i % 2][:, :], c["head_eps"][:, 0:2],
                                       ALU.add).then_inc(mean_ready, 1)
                    pool.wait_ge(mean_ready, NAT * n + i + 1)
                    if not (isinstance(n, int) and n < 2):
                        pool.wait_ge(sigmoids_ready, UNITS * (n - 1))
                    pool.tensor_tensor(rms[:, 0:2], mean_sq[i % 2][:, :], c["minus_half"][:, 0:2],
                                       ALU.pow).then_inc(k_ready, 1)
                    pool.wait_ge(k_ready, 2 * (NAT * n + i) + 1)
                    pool.tensor_tensor(rms[:, 2:3], rms[:, 0:1], c["minus_one"][:, :], ALU.mult).then_inc(rms_ready, 1)
                    pool.wait_ge(raw_ready, NAT * n + i + 1)
                    if i >= 4 or not known_first(n):
                        pool.wait_ge(qk_turned, PAIRS * n + (i - 4) // 2 + 1)
                    pool.tensor_tensor(k_scaled[i % 4][:, :], raw[i % 4][:, 1, :], rms[:, 1:2].to_broadcast([P, P]),
                                       ALU.mult).then_inc(k_ready, 1)

            heads(pool, step)

        @block.tensor
        def _(pe):
            def bank_is_read(h, attends, kind, which):
                if not attends:
                    if which >= 2:
                        pe.wait_ge(qk_ready, PAIRS * (h + 1) + which - 1)
                    return
                at = turn_of[(kind, which)]
                if at < 2:
                    pe.wait_ge(qk_ready, PAIRS * (h + 1))
                    if not known_first(h):
                        pe.wait_ge(wt_ready, UNITS * h)
                    return
                before, w = next(key for key, value in turn_of.items() if value == at - 2)
                if before == "w":
                    pe.wait_ge(wt_ready, UNITS * h + w + 1)
                elif not (isinstance(h, int) and h == HEADS - 1):
                    pe.wait_ge(qk_ready, PAIRS * (h + 1) + w + 1)

            def step(h, b, attends, projects):
                n, nb = h + 1, 1 - b
                for i in range(USES):
                    if attends and i < TILES:
                        pe.wait_ge(qk_ready, PAIRS * h + i // 2 + 1)
                        rows = slice(i * P, (i + 1) * P)
                        for u in range(Z_UNITS[i]):
                            width = min(HALF, (i + 1) * P - u * HALF)
                            unit = ENDS[i] - Z_UNITS[i] + u
                            if unit >= 3 or not known_first(h):
                                pe.wait_ge(sigmoids_ready, UNITS * h + unit - 2)
                            z = p_z[unit % 3][:, 0:width]
                            cols = slice(u * HALF, u * HALF + width)
                            pe.matmul(z, qt_hi[b][:, rows], kt_hi[b][:, cols], start=True, stop=False,
                                      skip_group_check=True)
                            if u == Z_UNITS[i] - 1:
                                pe.matmul(p_z[unit % 3][:, width - P:width], c["ident_bf"][:, :],
                                          c["causal_neg"][:, :], start=False, stop=False, skip_group_check=True)
                            pe.matmul(z, qt_hi[b][:, rows], kt_lo[b][:, cols], start=False, stop=False,
                                      skip_group_check=True)
                            pe.matmul(z, qt_lo[b][:, rows], kt_hi[b][:, cols], start=False, stop=True,
                                      skip_group_check=True).then_inc(z_done, 1)
                    if projects:
                        if i >= 2:
                            pe.wait_ge(raw_ready, NAT * n + i - 1)
                        elif not known_first(n):
                            pe.wait_ge(gate_ready, GATE * (n - 1) + i + 1)
                        if i == 0:
                            for p in range(3):
                                pe.wait_ge(w_ready[p], n + 1)
                        if i == NAT:
                            pe.wait_ge(w_ready[3], n + 1)
                        for kt in range(KT):
                            if i < NAT:
                                rows = slice(i * P, (i + 1) * P)
                                last = matmul_exact(pe, p_proj[i % 2][:, 0:3 * P],
                                                    ut_hi[:, kt, rows], ut_lo[:, kt, rows],
                                                    w_qkv_hi[:, kt, :, :].rearrange("p a b -> p (a b)"),
                                                    w_qkv_lo[:, kt, :, :].rearrange("p a b -> p (a b)"),
                                                    kt == 0, kt == KT - 1)
                            else:
                                cols = slice((i - NAT) * HALF, (i - NAT + 1) * HALF)
                                last = matmul_exact(pe, p_proj[i % 2][:, :], w_gate_hi[:, kt, :],
                                                    w_gate_lo[:, kt, :], ut_hi[:, kt, cols], ut_lo[:, kt, cols],
                                                    kt == 0, kt == KT - 1)
                        last.then_inc(proj_done, 1)
                    if attends and i >= 3 and i % 2 == 1:
                        g = (i - 3) // 2
                        pe.wait_ge(wt_ready, UNITS * h + ENDS[2 * g + 1])
                        pe.wait_ge(v_ready, NAT * h + NAT)
                        if g >= 1 or not known_first(h):
                            pe.wait_ge(o_gated, PAIRS * h + g)
                        for s in range(2 * g + 2):
                            o = p_o[:, :, :] if s <= 2 * g else p_o[:, 1, :]
                            w_h = wt_hi[:, s, :, :] if s <= 2 * g else wt_hi[:, s, 1, :]
                            w_l = wt_lo[:, s, :, :] if s <= 2 * g else wt_lo[:, s, 1, :]
                            last = matmul_exact(pe, o, v_hi[b][:, s, :], v_lo[b][:, s, :], w_h, w_l,
                                                s == 0, s == 2 * g + 1)
                        last.then_inc(o_done, 1)
                    if attends and 1 <= i <= TILES:
                        j = i - 1
                        pe.wait_ge(weights_ready, TILES * h + j + 1)
                        for u in range(Z_UNITS[j]):
                            unit = ENDS[j] - Z_UNITS[j] + u
                            bank_is_read(h, attends, "w", unit)
                            for s in range(4 * u, min(4 * u + 4, j + 1)):
                                last = pe.transpose(p_turn[turn_of[("w", unit)] % 2][:, s - 4 * u, :],
                                                    beta[j % 2][:, s * P:(s + 1) * P], c["ident"][:, :])
                            last.then_inc(weights_turned, 1)
                    if projects and i >= 2 and i % 2 == 0:
                        m = i // 2 - 1
                        pe.wait_ge(k_ready, 2 * (NAT * n + 2 * m + 2))
                        bank_is_read(h, attends, "qk", m)
                        bank = p_turn[(turn_of if attends else turn_alone)[("qk", m)] % 2]
                        for t in range(2):
                            pe.transpose(bank[:, t, :], raw[(2 * m + t) % 4][:, 0, :], c["ident"][:, :])
                            last = pe.transpose(bank[:, 2 + t, :], k_scaled[(2 * m + t) % 4][:, :], c["ident"][:, :])
                        last.then_inc(qk_turned, 1)

            heads(pe, step)


def build_output_projection(nc, tag, c, mixed, w_out, residual, dst, gain, ut_hi, ut_lo):
    with ExitStack() as ctx:
        def sb(name, shape, dt=F32):
            return ctx.enter_context(nc.sbuf_tensor(f"{tag}_{name}", shape, dt))

        def sem(name):
            return ctx.enter_context(nc.semaphore(f"{tag}_{name}"))

        stage = [sb(f"stage{i}", [P, D_MODEL]) for i in range(4)]
        w_hi = sb("w_hi", [P, HEADS, D_MODEL], F32R)
        w_lo = sb("w_lo", [P, HEADS, D_MODEL], F32R)
        m_in = [sb(f"m_in{i}", [P, HEADS, P]) for i in range(2)]
        m_hi = [sb(f"m_hi{i}", [P, HEADS, P], F32R) for i in range(2)]
        m_lo = [sb(f"m_lo{i}", [P, HEADS, P], F32R) for i in range(2)]
        h_tile = [sb(f"h_tile{i}", [P, D_MODEL]) for i in range(2)]
        p_y = [ctx.enter_context(nc.psum_tensor(f"{tag}_p_y{i}", [P, HALF], F32)) for i in range(4)]
        if gain is not None:
            gain_rows = sb("gain_rows", [P, D_MODEL])
            squares = sb("squares", [P, D_MODEL])
            normed = sb("normed", [P, D_MODEL])
            sum_sq = [sb(f"sum_sq{i}", [P, 1]) for i in range(2)]
            mean_sq = [sb(f"mean_sq{i}", [P, 1]) for i in range(2)]
            inv_rms = [sb(f"inv_rms{i}", [P, 1]) for i in range(2)]
            turned = [ctx.enter_context(nc.psum_tensor(f"{tag}_turned{i}", [P, 4, P], F32)) for i in range(2)]

        w_loaded = [sem(f"w_loaded{i}") for i in range(4)]
        w_hi_ready = sem("w_hi_ready")
        w_ready = sem("w_ready")
        gain_loaded = sem("gain_loaded")
        m_loaded = [sem(f"m_loaded{i}") for i in range(2)]
        m_hi_ready = sem("m_hi_ready")
        m_ready = sem("m_ready")
        r_loaded = [sem(f"r_loaded{i}") for i in range(2)]
        y_done = sem("y_done")
        h_ready = sem("h_ready")
        stored = sem("stored")
        sum_ready = sem("sum_ready")
        mean_ready = sem("mean_ready")
        rms_ready = sem("rms_ready")
        normed_ready = sem("normed_ready")
        turned_ready = sem("turned_ready")
        hi_ready = sem("hi_ready")
        lo_ready = sem("lo_ready")

        block = ctx.enter_context(nc.Block())

        @block.sync
        def _(sp):
            def load_tile(i):
                if i >= 2:
                    sp.wait_ge(m_ready, i - 1)
                    sp.wait_ge(stored, 16 * (i - 1))
                    if gain is not None:
                        sp.wait_ge(normed_ready, i - 1)
                rows = slice(i * P, (i + 1) * P)
                sp.dma_start(m_in[i % 2][:, :, :], mixed[:, :, rows].rearrange("h p t -> p h t")
                             ).then_inc(m_loaded[i % 2], 16)
                sp.dma_start(h_tile[i % 2][:, :], residual[rows, :]).then_inc(r_loaded[i % 2], 16)

            def load_w(h):
                if h >= 4:
                    sp.wait_ge(w_ready, h - 3)
                sp.dma_start(stage[h % 4][:, :], w_out[0, h * P:(h + 1) * P, :]).then_inc(w_loaded[h % 4], 16)

            load_w(0)
            load_tile(0)
            for h in range(1, HEADS):
                load_w(h)
            load_tile(1)
            if gain is not None:
                sp.dma_start(gain_rows[:, :], gain[0:1, :].to_broadcast([P, D_MODEL])).then_inc(gain_loaded, 16)
            for i in range(TILES):
                sp.wait_ge(h_ready, 2 * i + 2)
                sp.dma_start(dst[i * P:(i + 1) * P, :], h_tile[i % 2][:, :]).then_inc(stored, 16)
                if i + 2 < TILES:
                    load_tile(i + 2)
            sp.wait_ge(stored, 16 * TILES)

        @block.scalar
        def _(act):
            def mixed_hi(i):
                act.wait_ge(m_loaded[i % 2], 16 * (i // 2 + 1))
                if i >= 2:
                    act.wait_ge(y_done, 2 * (i - 1))
                act.activation(m_hi[i % 2][:, :, :], m_in[i % 2][:, :, :], ACT.Copy).then_inc(m_hi_ready, 1)

            mixed_hi(0)
            for h in range(HEADS):
                act.wait_ge(w_loaded[h % 4], 16 * (h // 4 + 1))
                act.activation(w_hi[:, h, :], stage[h % 4][:, :], ACT.Copy).then_inc(w_hi_ready, 1)
            for i in range(TILES + 1):
                if i + 1 < TILES:
                    mixed_hi(i + 1)
                if gain is not None and i < TILES:
                    act.wait_ge(h_ready, 2 * i + 2)
                    if i >= 1:
                        act.wait_ge(sum_ready, i)
                    if i >= 2:
                        act.wait_ge(mean_ready, i - 1)
                    act.activation(squares[:, :], h_tile[i % 2][:, :], ACT.Square,
                                   accum_out=sum_sq[i % 2][:, :]).then_inc(sum_ready, 1)
                if gain is not None and i >= 1:
                    j = i - 1
                    for half in range(2):
                        act.wait_ge(turned_ready, 2 * j + half + 1)
                        act.activation(ut_hi[:, 4 * half:4 * half + 4, j * P:(j + 1) * P],
                                       turned[half][:, :, :], ACT.Copy).then_inc(hi_ready, 1)

        @block.vector
        def _(dve):
            def mixed_lo(i):
                dve.wait_ge(m_hi_ready, i + 1)
                if i >= 2:
                    dve.wait_ge(y_done, 2 * (i - 1))
                dve.tensor_tensor(m_lo[i % 2][:, :, :], m_in[i % 2][:, :, :], m_hi[i % 2][:, :, :].bitcast(F32),
                                  ALU.subtract).then_inc(m_ready, 1)

            mixed_lo(0)
            for h in range(HEADS):
                dve.wait_ge(w_hi_ready, h + 1)
                dve.tensor_tensor(w_lo[:, h, :], stage[h % 4][:, :], w_hi[:, h, :].bitcast(F32),
                                  ALU.subtract).then_inc(w_ready, 1)
            for i in range(TILES + 1):
                if i + 1 < TILES:
                    mixed_lo(i + 1)
                if i < TILES:
                    dve.wait_ge(r_loaded[i % 2], 16 * (i // 2 + 1))
                    for half in range(2):
                        cols = slice(half * HALF, (half + 1) * HALF)
                        dve.wait_ge(y_done, 2 * i + half + 1)
                        dve.tensor_tensor(h_tile[i % 2][:, cols], h_tile[i % 2][:, cols],
                                          p_y[(2 * i + half) % 4][:, :], ALU.add).then_inc(h_ready, 1)
                if gain is not None and i >= 1:
                    j = i - 1
                    for half in range(2):
                        dve.wait_ge(hi_ready, 2 * j + half + 1)
                        dve.tensor_tensor(ut_lo[:, 4 * half:4 * half + 4, j * P:(j + 1) * P], turned[half][:, :, :],
                                          ut_hi[:, 4 * half:4 * half + 4, j * P:(j + 1) * P].bitcast(F32),
                                          ALU.subtract).then_inc(lo_ready, 1)
                if gain is not None and i < TILES:
                    if i == 0:
                        dve.wait_ge(gain_loaded, 16)
                    dve.wait_ge(rms_ready, i + 1)
                    dve.wait_ge(h_ready, 2 * i + 2)
                    if i >= 1:
                        dve.wait_ge(turned_ready, 2 * i)
                    dve.scalar_tensor_tensor(out=normed[:, :], in0=h_tile[i % 2][:, :],
                                             scalar=inv_rms[i % 2][:, 0:1], in1=gain_rows[:, :],
                                             op0=ALU.mult, op1=ALU.mult).then_inc(normed_ready, 1)

        @block.gpsimd
        def _(pool):
            if gain is None:
                return
            for i in range(TILES):
                pool.wait_ge(sum_ready, i + 1)
                pool.tensor_scalar(mean_sq[i % 2][:, :], sum_sq[i % 2][:, :], 1.0 / D_MODEL, RMS_EPS,
                                   ALU.mult, ALU.add).then_inc(mean_ready, 1)
                pool.wait_ge(mean_ready, i + 1)
                if i >= 2:
                    pool.wait_ge(normed_ready, i - 1)
                pool.tensor_tensor(inv_rms[i % 2][:, :], mean_sq[i % 2][:, :], c["minus_half"][:, 0:1],
                                   ALU.pow).then_inc(rms_ready, 1)

        @block.tensor
        def _(pe):
            for i in range(TILES + 1):
                if i < TILES:
                    pe.wait_ge(m_ready, i + 1)
                    for half in range(2):
                        use = 2 * i + half
                        if use >= 4:
                            pe.wait_ge(h_ready, use - 3)
                        for h in range(HEADS):
                            if use == 0:
                                pe.wait_ge(w_ready, h + 1)
                            cols = slice(half * HALF, (half + 1) * HALF)
                            last = matmul_exact(pe, p_y[use % 4][:, :], m_hi[i % 2][:, h, :], m_lo[i % 2][:, h, :],
                                                w_hi[:, h, cols], w_lo[:, h, cols], h == 0, h == HEADS - 1)
                        last.then_inc(y_done, 1)
                if gain is not None and i >= 1:
                    j = i - 1
                    pe.wait_ge(normed_ready, j + 1)
                    for half in range(2):
                        if j >= 1:
                            pe.wait_ge(lo_ready, 2 * (j - 1) + half + 1)
                        for q in range(4):
                            kt = 4 * half + q
                            last = pe.transpose(turned[half][:, q, :], normed[:, kt * P:(kt + 1) * P],
                                                c["ident"][:, :])
                        last.then_inc(turned_ready, 1)


def build_hgrn(nc, c, w_in, ut_hi, ut_lo, mixed):
    L = len(LEVELS)
    HALVES = SEQ // 2
    USES = 8

    with ExitStack() as ctx:
        def sb(name, shape, dt=F32):
            return ctx.enter_context(nc.sbuf_tensor("g_" + name, shape, dt))

        def psum(name, shape):
            return ctx.enter_context(nc.psum_tensor("g_" + name, shape, F32))

        def sem(name):
            return ctx.enter_context(nc.semaphore("g_" + name))

        stage = [sb(f"stage{p}", [P, KT, P]) for p in range(4)]
        w_qf_hi = sb("w_qf_hi", [P, KT, 2, P], F32R)
        w_qf_lo = sb("w_qf_lo", [P, KT, 2, P], F32R)
        w_ig_hi = sb("w_ig_hi", [P, KT, 2, P], F32R)
        w_ig_lo = sb("w_ig_lo", [P, KT, 2, P], F32R)
        q = [sb(f"q{b}", [P, SEQ]) for b in range(2)]
        k = [sb(f"k{b}", [P, SEQ]) for b in range(2)]
        prefix = [sb(f"prefix{b}", [P, SEQ]) for b in range(2)]
        suffix = sb("suffix", [P, SEQ])
        value = [sb(f"value{b}", [P, TILES, P]) for b in range(2)]
        gate = [sb(f"gate{b}", [P, TILES, P]) for b in range(2)]
        q_right = [sb(f"q_right{i}", [P, HALVES]) for i in range(3)]
        k_left = [sb(f"k_left{i}", [P, SEQ]) for i in range(3)]
        scores = sb("scores", [P, TILES, P])
        q_chunk = sb("q_chunk", [P, SEQ])
        k_chunk = sb("k_chunk", [P, SEQ])
        qk = sb("qk", [P, SEQ])
        self_score = sb("self_score", [P, TILES])
        k_turned = sb("k_turned", [P, TILES, P])
        state = sb("state", [P, TILES, P])
        o = sb("o", [P, TILES, P])
        squares = sb("squares", [P, P])
        sum_sq = sb("sum_sq", [P, TILES])
        sum_eps = sb("sum_eps", [P, TILES])
        inv_rms = sb("inv_rms", [P, TILES])
        out_turned = sb("out_turned", [P, SEQ])

        p_proj = [psum(f"p_proj{i}", [P, HALF]) for i in range(2)]
        p_level = [psum(f"p_level{i}", [P, HALF]) for i in range(2)]
        p_misc = [psum(f"p_misc{i}", [P, 4, P]) for i in range(4)]

        w_loaded = [sem(f"w_loaded{p}") for p in range(4)]
        w_hi_ready = [sem(f"w_hi_ready{p}") for p in range(4)]
        w_ready = [sem(f"w_ready{p}") for p in range(4)]
        proj_done = sem("proj_done")
        q_sigmoid = sem("q_sigmoid")
        q_ready = sem("q_ready")
        f_sigmoid = sem("f_sigmoid")
        fk_ready = sem("fk_ready")
        ig_copied = sem("ig_copied")
        gate_ready = sem("gate_ready")
        zeroed = sem("zeroed")
        k_prepared = sem("k_prepared")
        prepared = sem("prepared")
        doubled = sem("doubled")
        level_done = sem("level_done")
        level_placed = sem("level_placed")
        chunk_ready = sem("chunk_ready")
        self_done = sem("self_done")
        self_ready = sem("self_ready")
        k_turned_done = sem("k_turned_done")
        k_turned_ready = sem("k_turned_ready")
        update_done = sem("update_done")
        state_ready = sem("state_ready")
        o_done = sem("o_done")
        o_ready = sem("o_ready")
        sums_ready = sem("sums_ready")
        eps_added = sem("eps_added")
        rms_ready = sem("rms_ready")
        o_gated = sem("o_gated")
        o_turned = sem("o_turned")
        out_ready = sem("out_ready")
        out_stored = sem("out_stored")

        def heads(eng, step):
            step(-1, 1, False, False, True)
            step(0, 0, False, True, True)
            with eng.Fori(0, (HEADS - 4) // 2) as pair:
                step(pair * 2 + 1, 1, True, True, True)
                step(pair * 2 + 2, 0, True, True, True)
            step(HEADS - 3, 1, True, True, True)
            step(HEADS - 2, 0, True, True, True)
            step(HEADS - 1, 1, True, True, False)
            step(HEADS, 0, True, False, False)

        def known_first(h):
            return isinstance(h, int) and h <= 0

        block = ctx.enter_context(nc.Block())

        @block.sync
        def _(sp):
            def load(h, p):
                if not known_first(h):
                    sp.wait_ge(w_ready[p], h)
                columns = w_in[0, :, bass.ds(p * D_MODEL + h * P, P)]
                sp.dma_start(stage[p][:, :, :], columns.rearrange("(k p) c -> p k c", p=P)).then_inc(w_loaded[p], 16)

            def store(h):
                sp.wait_ge(out_ready, 2 * h + 2)
                sp.dma_start(mixed[bass.ds(h, 1), :, :].rearrange("o p s -> p (o s)"),
                             out_turned[:, :]).then_inc(out_stored, 16)

            for h in range(3):
                for p in range(4):
                    load(h, p)
            with sp.Fori(0, HEADS - 3) as h:
                store(h)
                for p in range(4):
                    load(h + 3, p)
            for h in range(HEADS - 3, HEADS):
                store(h)
            sp.wait_ge(out_stored, 16 * HEADS)

        @block.scalar
        def _(act):
            def split_hi(h, p):
                if not known_first(h):
                    act.wait_ge(proj_done, USES * (h - 1) + (4 if p < 2 else USES))
                act.wait_ge(w_loaded[p], 16 * h + 16)
                dst = (w_qf_hi if p < 2 else w_ig_hi)[:, :, p % 2, :]
                act.activation(dst, stage[p][:, :, :], ACT.Copy).then_inc(w_hi_ready[p], 1)

            def step(h, b, follows, mixes, projects):
                n, nb = h + 1, 1 - b
                early = isinstance(n, int) and n < 2
                last_head = isinstance(n, int) and n == HEADS - 1
                for i in range(USES):
                    if projects and i == 0:
                        if known_first(n):
                            split_hi(0, 0)
                            split_hi(0, 1)
                        split_hi(n, 2)
                        split_hi(n, 3)
                    if projects and i == 4 and not last_head:
                        split_hi(n + 1, 0)
                        split_hi(n + 1, 1)
                    if projects:
                        act.wait_ge(proj_done, USES * n + i + 1)
                        cols = slice((i % 2) * HALF, (i % 2 + 1) * HALF)
                        if i == 0 and not early:
                            act.wait_ge(state_ready, (TILES - 1) * (n - 1))
                            act.wait_ge(o_gated, n - 1)
                            act.wait_ge(chunk_ready, n - 1)
                        if i < 2:
                            act.activation(q[nb][:, cols], p_proj[i % 2][:, :], ACT.Sigmoid).then_inc(q_sigmoid, 1)
                        elif i < 4:
                            act.activation(prefix[nb][:, cols], p_proj[i % 2][:, :], ACT.Sigmoid)
                            act.activation(k[nb][:, cols], p_proj[i % 2][:, :], ACT.Sigmoid,
                                           scale=-1.0).then_inc(f_sigmoid, 1)
                        else:
                            both = p_proj[i % 2][:, :].rearrange("p (t a v) -> p t a v", t=2, a=2)
                            tiles = slice(2 * (i - 4), 2 * (i - 4) + 2)
                            act.activation(value[nb][:, tiles, :], both[:, :, 0, :], ACT.Copy)
                            act.activation(gate[nb][:, tiles, :], both[:, :, 1, :],
                                           ACT.Sigmoid).then_inc(ig_copied, 1)
                    if follows and i == 0:
                        for u in range(2):
                            act.wait_ge(o_turned, 2 * (h - 1) + u + 1)
                            if u == 0 and not (isinstance(h, int) and h == 1):
                                act.wait_ge(out_stored, 16 * (h - 1))
                            act.activation(out_turned[:, u * HALF:(u + 1) * HALF],
                                           p_misc[2 + u][:, :, :].rearrange("p a b -> p (a b)"), ACT.Copy,
                                           scale=c["o_scale"][:, 0:1]).then_inc(out_ready, 1)
                    if mixes and i == 4:
                        for u in range(2):
                            act.wait_ge(k_turned_done, 2 * h + u + 1)
                            if not known_first(h):
                                act.wait_ge(update_done, 2 * h)
                            act.activation(k_turned[:, 4 * u:4 * u + 4, :], p_misc[u][:, :, :],
                                           ACT.Copy).then_inc(k_turned_ready, 1)

            heads(act, step)

        @block.vector
        def _(dve):
            dve.memset(scores[:, :, :], 0.0).then_inc(zeroed, 1)
            dve.memset(suffix[:, :], 1.0).then_inc(zeroed, 1)
            for i in range(3):
                dve.memset(k_left[i][:, :], 0.0).then_inc(zeroed, 1)

            def split_lo(h, p):
                if not known_first(h):
                    dve.wait_ge(proj_done, USES * (h - 1) + (4 if p < 2 else USES))
                dve.wait_ge(w_hi_ready[p], h + 1)
                hi = (w_qf_hi if p < 2 else w_ig_hi)[:, :, p % 2, :]
                lo = (w_qf_lo if p < 2 else w_ig_lo)[:, :, p % 2, :]
                dve.tensor_tensor(lo, stage[p][:, :, :], hi.bitcast(F32), ALU.subtract).then_inc(w_ready[p], 1)

            def by_halves(t, half):
                return t[:, :].rearrange("p (b two r) -> p b two r", two=2, r=half)

            def prepare(h, b, level):
                half = LEVELS[level]
                blocks = SEQ // (2 * half)
                pre, suf = by_halves(prefix[b], half), by_halves(suffix, half)
                if level == 0:
                    dve.wait_ge(fk_ready, 2 * h + 2)
                    dve.wait_ge(q_ready, 2 * h + 2)
                    if known_first(h):
                        dve.wait_ge(zeroed, 5)
                    else:
                        dve.wait_ge(chunk_ready, h)
                        dve.wait_ge(state_ready, (TILES - 1) * h)
                else:
                    dve.wait_ge(doubled, 2 * (L * h + level) - 1)
                if level >= 3:
                    dve.wait_ge(level_done, L * h + level - 2)
                elif not known_first(h):
                    dve.wait_ge(level_done, L * h)
                q_out = q_right[level % 3][:, :].rearrange("p (b r) -> p b r", r=half)
                k_out = by_halves(k_left[level % 3], half)[:, :, 0, :]
                k_in = by_halves(k[b], half)[:, :, 0, :]
                if level == 0:
                    dve.tensor_copy(k_out, k_in).then_inc(k_prepared, 1)
                else:
                    dve.tensor_tensor(k_out, k_in, suf[:, :, 0, :], ALU.mult).then_inc(k_prepared, 1)
                    dve.wait_ge(doubled, 2 * (L * h + level))
                dve.tensor_tensor(q_out, by_halves(q[b], half)[:, :, 1, :], pre[:, :, 1, :],
                                  ALU.mult).then_inc(prepared, 1)
                dve.wait_ge(k_prepared, L * h + level + 1)
                if level == 0:
                    dve.tensor_copy(suf[:, :, 0, :], pre[:, :, 1, :])
                    dve.memset(suf[:, :, 1, :], 1.0).then_inc(doubled, 1)
                else:
                    dve.tensor_tensor(suf[:, :, 0, :], suf[:, :, 0, :],
                                      pre[:, :, 1, half - 1:half].to_broadcast([P, blocks, half]),
                                      ALU.mult).then_inc(doubled, 1)
                dve.wait_ge(prepared, L * h + level + 1)
                dve.wait_ge(doubled, 2 * (L * h + level) + 1)
                dve.tensor_tensor(pre[:, :, 1, :], pre[:, :, 1, :],
                                  pre[:, :, 0, half - 1:half].to_broadcast([P, blocks, half]),
                                  ALU.mult).then_inc(doubled, 1)

            def place(h, level):
                half = LEVELS[level]
                blocks = P // (2 * half)
                dve.wait_ge(zeroed, 5)
                if level < L - 1:
                    dve.wait_ge(level_done, L * h + level + 1)
                if level == 0 and not known_first(h):
                    dve.wait_ge(o_done, 2 * h)
                if 1 <= level < L - 1:
                    dve.wait_ge(level_placed, L * h + level)
                dst = scores[:, :, :].rearrange("p m (b two r) -> p m b two r", two=2, r=half)[:, :, :, 1, :]
                mask = c["level_mask"][:, level, :].bitcast(I32).rearrange("p (b r) -> p b r", r=half)
                dve.copy_predicated(dst, mask.unsqueeze(1).to_broadcast([P, TILES, blocks, half]),
                                    p_level[level % 2][:, :].rearrange("p (m b r) -> p m b r", m=TILES, r=half)
                                    ).then_inc(level_placed, 1)

            def chunk_operands(h, b):
                dve.wait_ge(doubled, 2 * L * (h + 1))
                if not known_first(h):
                    dve.wait_ge(o_done, 2 * h)
                    dve.wait_ge(k_turned_done, 2 * h)
                    dve.wait_ge(self_done, h)
                dve.tensor_tensor(k_chunk[:, :], k[b][:, :], suffix[:, :], ALU.mult)
                dve.tensor_tensor(qk[:, :], q[b][:, :], k[b][:, :], ALU.mult)
                dve.tensor_tensor(q_chunk[:, :], q[b][:, :], prefix[b][:, :], ALU.mult).then_inc(chunk_ready, 1)

            def states(h, b):
                for m in range(TILES - 1):
                    bank = p_misc[2 + m // 4][:, m % 4, :]
                    dve.wait_ge(update_done, 2 * h + m // 4 + 1)
                    if m == 0:
                        if not known_first(h):
                            dve.wait_ge(o_done, 2 * h)
                        dve.tensor_copy(state[:, 1, :], bank).then_inc(state_ready, 1)
                    else:
                        dve.wait_ge(state_ready, (TILES - 1) * h + m)
                        dve.scalar_tensor_tensor(out=state[:, m + 1, :], in0=state[:, m, :],
                                                 scalar=prefix[b][:, m * P + P - 1:m * P + P], in1=bank,
                                                 op0=ALU.mult, op1=ALU.add).then_inc(state_ready, 1)

            def outputs(h, b):
                dve.wait_ge(self_ready, h + 1)
                if not known_first(h):
                    dve.wait_ge(o_turned, 2 * h)
                for m in range(TILES):
                    dve.wait_ge(o_done, 2 * h + m // 4 + 1)
                    dve.scalar_tensor_tensor(out=o[:, m, :], in0=value[b][:, m, :], scalar=self_score[:, m:m + 1],
                                             in1=p_misc[m // 4][:, m % 4, :], op0=ALU.mult,
                                             op1=ALU.add).then_inc(o_ready, 1)
                if not known_first(h):
                    dve.wait_ge(eps_added, h)
                for m in range(TILES):
                    dve.wait_ge(o_ready, TILES * h + m + 1)
                    if m > 0 or not known_first(h):
                        dve.wait_ge(sums_ready, TILES * h + m)
                    dve.tensor_tensor_reduce(squares[:, :], o[:, m, :], o[:, m, :], 1.0, 0.0, ALU.mult, ALU.add,
                                             sum_sq[:, m:m + 1]).then_inc(sums_ready, 1)

            def gate_outputs(h, b):
                dve.wait_ge(rms_ready, h + 1)
                dve.wait_ge(gate_ready, 4 * h + 4)
                for m in range(TILES):
                    ins = dve.scalar_tensor_tensor(out=o[:, m, :], in0=o[:, m, :], scalar=inv_rms[:, m:m + 1],
                                                   in1=gate[b][:, m, :], op0=ALU.mult, op1=ALU.mult)
                ins.then_inc(o_gated, 1)

            def step(h, b, follows, mixes, projects):
                n, nb = h + 1, 1 - b
                last_head = isinstance(n, int) and n == HEADS - 1
                for i in range(USES):
                    if mixes and i == 0:
                        prepare(h, b, 0)
                    if follows and i == 0:
                        gate_outputs(h - 1, 1 - b)
                    if mixes and i == 0:
                        prepare(h, b, 1)
                        prepare(h, b, 2)
                    if projects and i == 0:
                        if known_first(n):
                            split_lo(0, 0)
                            split_lo(0, 1)
                        split_lo(n, 2)
                        split_lo(n, 3)
                    if projects and i == 4 and not last_head:
                        split_lo(n + 1, 0)
                        split_lo(n + 1, 1)
                    if projects:
                        cols = slice((i % 2) * HALF, (i % 2 + 1) * HALF)
                        if i < 2:
                            dve.wait_ge(q_sigmoid, 2 * n + i + 1)
                            dve.tensor_tensor(q[nb][:, cols], q[nb][:, cols], p_proj[i % 2][:, :],
                                              ALU.mult).then_inc(q_ready, 1)
                        elif i < 4:
                            dve.wait_ge(f_sigmoid, 2 * n + i - 1)
                            scale = c["one_minus_lower"][:, bass.ds(n, 1)]
                            dve.tensor_scalar(prefix[nb][:, cols], prefix[nb][:, cols], scale,
                                              c["lower"][:, bass.ds(n, 1)], ALU.mult, ALU.add)
                            dve.tensor_scalar(k[nb][:, cols], k[nb][:, cols], scale, None,
                                              ALU.mult).then_inc(fk_ready, 1)
                        else:
                            dve.wait_ge(ig_copied, 4 * n + i - 3)
                            tiles = slice(2 * (i - 4), 2 * (i - 4) + 2)
                            both = p_proj[i % 2][:, :].rearrange("p (t a v) -> p t a v", t=2, a=2)
                            dve.tensor_tensor(gate[nb][:, tiles, :], gate[nb][:, tiles, :], both[:, :, 1, :],
                                              ALU.mult).then_inc(gate_ready, 1)
                    if mixes and i == 0:
                        place(h, 0)
                        place(h, 1)
                        prepare(h, b, 3)
                        prepare(h, b, 4)
                    if mixes and i == 1:
                        place(h, 2)
                        place(h, 3)
                        prepare(h, b, 5)
                        prepare(h, b, 6)
                    if mixes and i == 2:
                        place(h, 4)
                        place(h, 5)
                        chunk_operands(h, b)
                    if mixes and i == 3:
                        dve.wait_ge(self_done, h + 1)
                        dve.wait_ge(level_done, L * h + L)
                        dve.wait_ge(level_placed, L * h + L - 1)
                        if not known_first(h):
                            dve.wait_ge(o_ready, TILES * h)
                        dve.tensor_copy(self_score[:, :], p_level[1][:, 0:TILES]).then_inc(self_ready, 1)
                        place(h, L - 1)
                    if mixes and i == 5:
                        states(h, b)
                    if mixes and i == 6:
                        outputs(h, b)

            heads(dve, step)

        @block.gpsimd
        def _(pool):
            def step(h, b, follows, mixes, projects):
                if not mixes:
                    return
                pool.wait_ge(sums_ready, TILES * h + TILES)
                if not known_first(h):
                    pool.wait_ge(rms_ready, h)
                pool.tensor_tensor(sum_eps[:, :], sum_sq[:, :], c["head_eps"][:, :], ALU.add).then_inc(eps_added, 1)
                pool.wait_ge(eps_added, h + 1)
                if not known_first(h):
                    pool.wait_ge(o_gated, h)
                pool.tensor_tensor(inv_rms[:, :], sum_eps[:, :], c["minus_half"][:, :], ALU.pow).then_inc(rms_ready, 1)

            heads(pool, step)

        @block.tensor
        def _(pe):
            def multiply_level(h, level):
                pe.wait_ge(prepared, L * h + level + 1)
                if level >= 2:
                    pe.wait_ge(level_placed, L * h + level - 1)
                elif level == 0 and not known_first(h):
                    pe.wait_ge(level_placed, L * h)
                elif level == 1 and not known_first(h):
                    pe.wait_ge(self_ready, h)
                for m in range(TILES):
                    last = pe.matmul(p_level[level % 2][:, m * (P // 2):(m + 1) * (P // 2)],
                                     k_left[level % 3][:, m * P:(m + 1) * P],
                                     q_right[level % 3][:, m * (P // 2):(m + 1) * (P // 2)], start=True, stop=True)
                last.then_inc(level_done, 1)

            def step(h, b, follows, mixes, projects):
                n, nb = h + 1, 1 - b
                for i in range(USES):
                    if projects:
                        if i in (0, 1) and not known_first(n):
                            pe.wait_ge(gate_ready, 4 * (n - 1) + 3 + i)
                        if i in (2, 3):
                            pe.wait_ge(q_ready, 2 * n + i - 1)
                        if i in (4, 5):
                            pe.wait_ge(f_sigmoid, 2 * n + i - 3)
                        if i in (6, 7):
                            pe.wait_ge(gate_ready, 4 * n + i - 5)
                        if i in (0, 2):
                            pe.wait_ge(w_ready[i // 2], n + 1)
                        if i == 4:
                            pe.wait_ge(w_ready[2], n + 1)
                            pe.wait_ge(w_ready[3], n + 1)
                        if i < 4:
                            cols = slice((i % 2) * HALF, (i % 2 + 1) * HALF)
                            for kt in range(KT):
                                last = matmul_exact(pe, p_proj[i % 2][:, :], w_qf_hi[:, kt, i // 2, :],
                                                    w_qf_lo[:, kt, i // 2, :], ut_hi[:, kt, cols],
                                                    ut_lo[:, kt, cols], kt == 0, kt == KT - 1)
                        else:
                            for t in range(2):
                                tile = 2 * (i - 4) + t
                                rows = slice(tile * P, (tile + 1) * P)
                                for kt in range(KT):
                                    last = matmul_exact(pe, p_proj[i % 2][:, t * 2 * P:(t + 1) * 2 * P],
                                                        ut_hi[:, kt, rows], ut_lo[:, kt, rows],
                                                        w_ig_hi[:, kt, :, :].rearrange("p a b -> p (a b)"),
                                                        w_ig_lo[:, kt, :, :].rearrange("p a b -> p (a b)"),
                                                        kt == 0, kt == KT - 1)
                        last.then_inc(proj_done, 1)
                    if follows and i == 0:
                        pe.wait_ge(o_gated, h)
                        for u in range(2):
                            pe.wait_ge(state_ready, (TILES - 1) * h)
                            for m in range(4):
                                last = pe.transpose(p_misc[2 + u][:, m, :], o[:, 4 * u + m, :], c["ident"][:, :])
                            last.then_inc(o_turned, 1)
                    if not mixes:
                        continue
                    if i < 3:
                        multiply_level(h, 2 * i)
                        multiply_level(h, 2 * i + 1)
                    if i == 3:
                        multiply_level(h, L - 1)
                        pe.wait_ge(chunk_ready, h + 1)
                        pe.wait_ge(level_placed, L * h + L - 1)
                        for m in range(TILES):
                            last = pe.matmul(p_level[1][:, m:m + 1], qk[:, m * P:(m + 1) * P],
                                             c["ones_col"][:, :], start=True, stop=True)
                        last.then_inc(self_done, 1)
                    if i == 4:
                        if not known_first(h):
                            pe.wait_ge(o_ready, TILES * h)
                        for u in range(2):
                            for m in range(4):
                                last = pe.transpose(p_misc[u][:, m, :],
                                                    k_chunk[:, (4 * u + m) * P:(4 * u + m + 1) * P],
                                                    c["ident"][:, :])
                            last.then_inc(k_turned_done, 1)
                    if i == 5:
                        if not known_first(h):
                            pe.wait_ge(out_ready, 2 * h)
                        for u in range(2):
                            pe.wait_ge(k_turned_ready, 2 * h + u + 1)
                            for m in range(4 * u, min(4 * u + 4, TILES - 1)):
                                last = pe.matmul(p_misc[2 + u][:, m % 4, :], k_turned[:, m, :], value[b][:, m, :],
                                                 start=True, stop=True)
                            last.then_inc(update_done, 1)
                    if i == 6:
                        pe.wait_ge(level_placed, L * h + L)
                        for u in range(2):
                            for m in range(4 * u, 4 * u + 4):
                                dst = p_misc[u][:, m % 4, :]
                                last = pe.matmul(dst, scores[:, m, :], value[b][:, m, :], start=True, stop=(m == 0))
                                if m > 0:
                                    pe.wait_ge(state_ready, (TILES - 1) * h + m)
                                    last = pe.matmul(dst, q_chunk[:, m * P:(m + 1) * P], state[:, m, :],
                                                     start=False, stop=True)
                            last.then_inc(o_done, 1)

            heads(pe, step)


_INS = ["x", "sb_norm", "sb_w_in", "sb_q_gain", "sb_k_gain", "sb_w_out",
        "hg_norm", "hg_w_in", "hg_o_gain", "hg_w_out", "hg_lb_logits"]


def kernel(**inputs):
    import numpy as _np
    import concourse.bacc as _bacc
    from concourse import mybir as _mybir
    from concourse.bass_utils import run_bass_kernel_spmd as _run

    nc = _bacc.Bacc("TRN2", target_bir_lowering=False, num_devices=1, dynamic_dma_scratch_size=1024)
    arrays, args = {}, []
    for name in _INS:
        a = _np.ascontiguousarray(inputs[name])
        arrays[f"in_{name}_dram"] = a
        args.append(nc.dram_tensor(f"in_{name}_dram", a.shape, _mybir.dt.from_np(a.dtype), kind="ExternalInput").ap())
    result = nc.dram_tensor("out_0_dram", inputs["x"].shape, _mybir.dt.float32, kind="ExternalOutput").ap()
    build_trunk(nc, *args, result)
    r = _run(nc, [arrays], core_ids=[0])
    return r.results[0]["out_0_dram"]
```

```python
from contextlib import ExitStack

import concourse.bass as bass
from concourse import mybir

ALU = mybir.AluOpType
ACT = mybir.ActivationFunctionType
AX_X = mybir.AxisListType.X
F32 = mybir.dt.float32
F32R = mybir.dt.float32r
BF16 = mybir.dt.bfloat16
I32 = mybir.dt.int32

P = 128
D_MODEL = 1024
SEQ = 1024
KT = D_MODEL // P
TILES = SEQ // P
HEADS = D_MODEL // P
HALF = 512
RMS_EPS = 1e-6
NEG = -1e30
LEVELS = [1, 2, 4, 8, 16, 32, 64]


def matmul_exact(pe, out, w_hi, w_lo, m_hi, m_lo, start, stop):
    pe.matmul(out, w_hi, m_hi, start=start, stop=False, skip_group_check=True)
    pe.matmul(out, w_hi, m_lo, start=False, stop=False, skip_group_check=True)
    return pe.matmul(out, w_lo, m_hi, start=False, stop=stop, skip_group_check=True)


def build_trunk(nc, x, sb_norm, sb_w_in, sb_q_gain, sb_k_gain, sb_w_out,
                hg_norm, hg_w_in, hg_o_gain, hg_w_out, hg_lb_logits, out):
    x = x.rearrange("b s d -> (b s) d")
    out = out.rearrange("b s d -> (b s) d")
    mixed = nc.dram_tensor("mixed_scratch", (2, HEADS, P, SEQ), F32).ap()
    h1 = nc.dram_tensor("h1_scratch", (SEQ, D_MODEL), F32).ap()

    with ExitStack() as ctx:
        def sb(name, shape, dt=F32, into=ctx):
            return into.enter_context(nc.sbuf_tensor(name, shape, dt))

        consts = {
            "ident": sb("ident", [P, P]),
            "ident_bf": sb("ident_bf", [P, P], BF16),
            "causal_neg": sb("causal_neg", [P, P], BF16),
            "ones_col": sb("ones_col", [P, 1]),
            "minus_half": sb("minus_half", [P, TILES]),
            "minus_one": sb("minus_one", [P, 1]),
            "head_eps": sb("head_eps", [P, TILES]),
            "level_mask": sb("level_mask", [P, len(LEVELS), P // 2]),
            "q_gain": sb("q_gain", [P, 1]),
            "k_gain": sb("k_gain", [P, 1]),
            "qk_gain": sb("qk_gain", [P, 1]),
            "o_gain": sb("o_gain", [P, 1]),
            "o_scale": sb("o_scale", [P, 1]),
            "logits": sb("logits", [P, 2, HEADS]),
            "logit_gap": sb("logit_gap", [P, HEADS]),
            "lower": sb("lower", [P, HEADS]),
            "one_minus_lower": sb("one_minus_lower", [P, HEADS]),
        }
        stage = [sb(f"stage{i}", [P, KT, P]) for i in range(4)]
        m_in = [sb(f"m_in{i}", [P, HEADS, P]) for i in range(2)]

        def link(tag):
            def sem(name):
                return ctx.enter_context(nc.semaphore(f"{tag}_{name}"))
            return {"w_loaded": [sem(f"w_loaded{i}") for i in range(4)],
                    "stored": sem("mixed_stored"),
                    "m_loaded": [sem(f"m_loaded{i}") for i in range(2)]}

        links = [link("l0"), link("l1")]
        hg_w_loaded = [ctx.enter_context(nc.semaphore(f"g_w_loaded{i}")) for i in range(4)]

        with ExitStack() as first_layer:
            ut_hi = sb("ut_hi", [P, KT, SEQ], F32R, first_layer)
            ut_lo = sb("ut_lo", [P, KT, SEQ], F32R, first_layer)
            small_inputs = {"q_gain": sb_q_gain, "k_gain": sb_k_gain, "o_gain": hg_o_gain, "logits": hg_lb_logits}
            build_attention(nc, consts, small_inputs, x, sb_norm, stage, m_in, links[0], sb_w_in, sb_w_out,
                            ut_hi, ut_lo, mixed[0])
            next_hi = ctx.enter_context(nc.sbuf_tensor("next_hi", [P, KT, SEQ], F32R, side="right"))
            next_lo = ctx.enter_context(nc.sbuf_tensor("next_lo", [P, KT, SEQ], F32R, side="right"))
            build_output_projection(nc, "l0", consts, m_in, links[0], mixed[0], ut_hi, ut_lo, x, h1,
                                    hg_norm, next_hi, next_lo, (stage, hg_w_in, hg_w_loaded))
        build_hgrn(nc, consts, stage, m_in, links[1], hg_w_loaded, hg_w_in, hg_w_out, next_hi, next_lo, mixed[1])
        build_output_projection(nc, "l1", consts, m_in, links[1], mixed[1], next_hi, next_lo, h1, out,
                                None, None, None, None)


def load_columns(sp, stage, w_in, h, p):
    columns = w_in[0, :, bass.ds(p * D_MODEL + h * P, P)]
    return sp.dma_start(stage[p][:, :, :], columns.rearrange("(k p) c -> p k c", p=P))


def load_w_out(sp, stage, w_out, r):
    return sp.dma_start(stage[r % 4][:, :, :].rearrange("p k c -> p (k c)"), w_out[0, r * P:(r + 1) * P, :])


def load_mixed(sp, m_in, mixed, i, heads):
    return sp.dma_start(m_in[i % 2][:, heads, :],
                        mixed[heads, :, i * P:(i + 1) * P].rearrange("h p t -> p h t"))


def build_attention(nc, c, small_inputs, x, gain, stage, m_in, link, w_in, w_out, ut_hi, ut_lo, mixed):
    Z_UNITS = [1, 1, 1, 1, 2, 2, 2, 2]
    ENDS = [sum(Z_UNITS[:i + 1]) for i in range(TILES)]
    UNITS = ENDS[-1]
    NAT, GATE = TILES, 2
    USES = NAT + GATE
    PAIRS = TILES // 2
    W_OUT_AT = {0: [0, 1], 1: [2, 3], 3: [4], 4: [5], 5: [6], 6: [7]}

    with ExitStack() as ctx:
        def sb(name, shape, dt=F32):
            return ctx.enter_context(nc.sbuf_tensor("a_" + name, shape, dt))

        def psum(name, shape):
            return ctx.enter_context(nc.psum_tensor("a_" + name, shape, F32))

        def sem(name):
            return ctx.enter_context(nc.semaphore("a_" + name))

        w_qkv_hi = sb("w_qkv_hi", [P, KT, 3, P], F32R)
        w_qkv_lo = sb("w_qkv_lo", [P, KT, 3, P], F32R)
        w_gate_hi = sb("w_gate_hi", [P, KT, P], F32R)
        w_gate_lo = sb("w_gate_lo", [P, KT, P], F32R)
        raw = [sb(f"raw{i}", [P, 3, P]) for i in range(4)]
        squares = [sb(f"squares{i}", [P, P]) for i in range(2)]
        sum_sq = [sb(f"sum_sq{i}", [P, 2]) for i in range(2)]
        mean_sq = [sb(f"mean_sq{i}", [P, 2]) for i in range(2)]
        inv_rms = [[sb(f"inv_rms{b}_{i}", [P, 3]) for i in range(TILES)] for b in range(2)]
        k_scaled = [sb(f"k_scaled{i}", [P, P]) for i in range(4)]
        qt_hi = [sb(f"qt_hi{b}", [P, SEQ], F32R) for b in range(2)]
        qt_lo = [sb(f"qt_lo{b}", [P, SEQ], F32R) for b in range(2)]
        kt_hi = [sb(f"kt_hi{b}", [P, SEQ], F32R) for b in range(2)]
        kt_lo = [sb(f"kt_lo{b}", [P, SEQ], F32R) for b in range(2)]
        v_hi = [sb(f"v_hi{b}", [P, TILES, P], F32R) for b in range(2)]
        v_lo = [sb(f"v_lo{b}", [P, TILES, P], F32R) for b in range(2)]
        gated = [sb(f"gated{b}", [P, SEQ]) for b in range(2)]
        beta = [sb(f"beta{i}", [P, SEQ]) for i in range(2)]
        skip = [sb(f"skip{i}", [P, SEQ + 1]) for i in range(2)]
        wt_hi = sb("wt_hi", [P, TILES, 2, P], F32R)
        wt_lo = sb("wt_lo", [P, TILES, 2, P], F32R)

        x_tile = beta
        normed = skip
        x_squares = m_in[0][:, :, :].rearrange("p a b -> p (a b)")
        gain_rows = m_in[1][:, :, :].rearrange("p a b -> p (a b)")
        x_sum_sq = [sb(f"x_sum_sq{i}", [P, 1]) for i in range(2)]
        x_mean_sq = [sb(f"x_mean_sq{i}", [P, 1]) for i in range(2)]
        x_inv_rms = [sb(f"x_inv_rms{i}", [P, 1]) for i in range(2)]

        p_proj = [psum(f"p_proj{i}", [P, HALF]) for i in range(2)]
        p_z = [psum(f"p_z{i}", [P, HALF]) for i in range(3)]
        p_turn = [psum(f"p_turn{i}", [P, 4, P]) for i in range(2)]
        p_o = psum("p_o", [P, 2, P])

        w_loaded = [sem(f"w_loaded{p}") for p in range(4)]
        w_out_hi_ready = sem("w_out_hi_ready")
        w_out_ready = sem("w_out_ready")
        w_hi_ready = [sem(f"w_hi_ready{p}") for p in range(4)]
        w_ready = [sem(f"w_ready{p}") for p in range(4)]
        proj_done = sem("proj_done")
        raw_ready = sem("raw_ready")
        v_hi_ready = sem("v_hi_ready")
        v_ready = sem("v_ready")
        sums_ready = sem("sums_ready")
        mean_ready = sem("mean_ready")
        rms_ready = sem("rms_ready")
        k_ready = sem("k_ready")
        qk_turned = sem("qk_turned")
        qk_hi_ready = sem("qk_hi_ready")
        qk_ready = sem("qk_ready")
        gate_sigmoid = sem("gate_sigmoid")
        gate_ready = sem("gate_ready")
        z_done = sem("z_done")
        sigmoids_ready = sem("sigmoids_ready")
        scan_done = sem("scan_done")
        weights_ready = sem("weights_ready")
        weights_turned = sem("weights_turned")
        wt_hi_ready = sem("wt_hi_ready")
        wt_ready = sem("wt_ready")
        o_done = sem("o_done")
        o_gated = sem("o_gated")
        o_stored = link["stored"]
        skip_set = sem("skip_set")
        pool_made = sem("pool_made")
        dve_made = sem("dve_made")
        act_made = sem("act_made")
        gain_loaded = sem("gain_loaded")
        qk_gains_loaded = sem("qk_gains_loaded")
        small_loaded = sem("small_loaded")
        x_loaded = [sem(f"x_loaded{i}") for i in range(2)]
        x_sum_ready = sem("x_sum_ready")
        x_mean_ready = sem("x_mean_ready")
        x_rms_ready = sem("x_rms_ready")
        normed_ready = sem("normed_ready")
        x_turned = sem("x_turned")
        ut_hi_ready = sem("ut_hi_ready")
        ut_ready = sem("ut_ready")

        turn_of, turn_alone = {}, {}
        for i in range(USES):
            if i >= 3 and i % 2 == 1:
                turn_of[("qk", (i - 3) // 2)] = len(turn_of)
                turn_alone[("qk", (i - 3) // 2)] = len(turn_alone)
            if 1 <= i <= TILES:
                for u in range(Z_UNITS[i - 1]):
                    turn_of[("w", ENDS[i - 1] - Z_UNITS[i - 1] + u)] = len(turn_of)

        def heads(eng, step):
            step(-1, 1, False, True)
            step(0, 0, True, True)
            with eng.Fori(0, (HEADS - 4) // 2) as pair:
                step(pair * 2 + 1, 1, True, True)
                step(pair * 2 + 2, 0, True, True)
            step(HEADS - 3, 1, True, True)
            step(HEADS - 2, 0, True, True)
            step(HEADS - 1, 1, True, False)

        def known_first(h):
            return isinstance(h, int) and h <= 0

        block = ctx.enter_context(nc.Block())

        @block.sync
        def _(sp):
            def load_out(r):
                if r < 4:
                    sp.wait_ge(w_ready[r], HEADS)
                else:
                    sp.wait_ge(w_out_ready, r - 3)
                load_w_out(sp, stage, w_out, r).then_inc(link["w_loaded"][r % 4], 16)

            def load_mixed_early(i):
                sp.wait_ge(o_stored, 16 * (HEADS - 1))
                load_mixed(sp, m_in, mixed, i, slice(0, HEADS - 1)).then_inc(link["m_loaded"][i], 16)

            def load(h, p):
                if not known_first(h):
                    sp.wait_ge(w_ready[p], h)
                load_columns(sp, stage, w_in, h, p).then_inc(w_loaded[p], 16)

            def store(h, b):
                sp.wait_ge(o_gated, PAIRS * h + PAIRS)
                sp.dma_start(mixed[bass.ds(h, 1), :, :].rearrange("o p s -> p (o s)"),
                             gated[b][:, :]).then_inc(o_stored, 16)

            def load_x(i):
                if i >= 2:
                    sp.wait_ge(normed_ready, i - 1)
                sp.dma_start(x_tile[i % 2][:, :], x[i * P:(i + 1) * P, :]).then_inc(x_loaded[i % 2], 16)

            load_x(0)
            sp.dma_start(gain_rows, gain[0:1, :].to_broadcast([P, D_MODEL])).then_inc(gain_loaded, 16)
            for p in range(3):
                load(0, p)
            load_x(1)
            for name in ("q_gain", "k_gain"):
                sp.dma_start(c[name][:, :], small_inputs[name].rearrange("a d -> d a"),
                             allow_slow_non_contiguous=True).then_inc(qk_gains_loaded, 16)
            load_x(2)
            load(0, 3)
            load_x(3)
            for p in range(3):
                load(1, p)
            for i in range(4, TILES):
                load_x(i)
            load(1, 3)
            sp.dma_start(c["o_gain"][:, :], small_inputs["o_gain"].rearrange("a d -> d a"),
                         allow_slow_non_contiguous=True).then_inc(small_loaded, 16)
            for layer in range(2):
                sp.dma_start(c["logits"][:, layer, :],
                             small_inputs["logits"][layer].rearrange("(h d) -> d h", d=P),
                             allow_slow_non_contiguous=True).then_inc(small_loaded, 16)
            for p in range(4):
                load(2, p)
            store(0, 0)
            for p in range(4):
                load(3, p)
            with sp.Fori(0, 2) as pair:
                for b in (1, 0):
                    store(pair * 2 + 2 - b, b)
                    for p in range(4):
                        load(pair * 2 + 5 - b, p)
            store(HEADS - 3, 1)
            for r in range(4):
                load_out(r)
            store(HEADS - 2, 0)
            load_out(4)
            load_out(5)
            for i in range(2):
                load_mixed_early(i)
            load_out(6)
            load_out(7)
            store(HEADS - 1, 1)

        @block.scalar
        def _(act):
            def split_hi(h, p):
                if not known_first(h):
                    act.wait_ge(proj_done, USES * (h - 1) + (NAT if p < 3 else USES))
                act.wait_ge(w_loaded[p], 16 * h + 16)
                dst = w_qkv_hi[:, :, p, :] if p < 3 else w_gate_hi[:, :, :]
                act.activation(dst, stage[p][:, :, :], ACT.Copy).then_inc(w_hi_ready[p], 1)

            def square_x(i):
                act.wait_ge(x_loaded[i % 2], 16 * (i // 2 + 1))
                if i >= 1:
                    act.wait_ge(x_sum_ready, i)
                if i >= 2:
                    act.wait_ge(x_mean_ready, i - 1)
                act.activation(x_squares, x_tile[i % 2][:, :], ACT.Square,
                               accum_out=x_sum_sq[i % 2][:, :]).then_inc(x_sum_ready, 1)

            def stream_hi(i):
                for half in range(2):
                    use = 2 * i + half
                    act.wait_ge(x_turned, use + 1)
                    act.activation(ut_hi[:, 4 * half:4 * half + 4, i * P:(i + 1) * P],
                                   p_z[use % 3][:, :].rearrange("p (a b) -> p a b", a=4),
                                   ACT.Copy).then_inc(ut_hi_ready, 1)

            def step(h, b, attends, projects):
                n, nb = h + 1, 1 - b
                for i in range(USES):
                    if known_first(h) and attends and i == 0:
                        act.wait_ge(normed_ready, TILES)
                        act.wait_ge(x_turned, 2 * TILES)
                    if known_first(n) and i + 1 < TILES:
                        stream_hi(i + 1)
                    if known_first(n) and i + 2 < TILES:
                        square_x(i + 2)
                    if attends and i < TILES:
                        for u in range(Z_UNITS[i]):
                            width = min(HALF, (i + 1) * P - u * HALF)
                            unit = ENDS[i] - Z_UNITS[i] + u
                            act.wait_ge(z_done, UNITS * h + unit + 1)
                            if u == 0:
                                act.wait_ge(rms_ready, TILES * h + i + 1)
                                if i >= 2:
                                    act.wait_ge(weights_turned, UNITS * h + ENDS[i - 2])
                                elif not known_first(h):
                                    act.wait_ge(weights_turned, UNITS * (h - 1) + ENDS[i + 6])
                            cols = slice(u * HALF, u * HALF + width)
                            act.activation(skip[i % 2][:, cols], p_z[unit % 3][:, 0:width], ACT.Sigmoid,
                                           scale=inv_rms[b][i][:, 2:3])
                            act.activation(beta[i % 2][:, cols], p_z[unit % 3][:, 0:width], ACT.Sigmoid,
                                           scale=inv_rms[b][i][:, 0:1]).then_inc(sigmoids_ready, 1)
                    if projects and i >= 3 and i % 2 == 1:
                        m = (i - 3) // 2
                        act.wait_ge(qk_turned, PAIRS * n + m + 1)
                        if known_first(n) and m == 0:
                            act.wait_ge(dve_made, 1)
                        if not (isinstance(n, int) and n < 2):
                            act.wait_ge(z_done, UNITS * (n - 1))
                        turn = (turn_of if attends else turn_alone)[("qk", m)] % 2
                        cols = slice(2 * m * P, (2 * m + 2) * P)
                        act.activation(qt_hi[nb][:, cols], p_turn[turn][:, 0:2, :].rearrange("p a b -> p (a b)"),
                                       ACT.Copy)
                        act.activation(kt_hi[nb][:, cols], p_turn[turn][:, 2:4, :].rearrange("p a b -> p (a b)"),
                                       ACT.Copy, scale=c["qk_gain"][:, 0:1]).then_inc(qk_hi_ready, 1)
                    if projects and i < NAT:
                        act.wait_ge(proj_done, USES * n + i + 1)
                        if i >= 4 or not known_first(n):
                            act.wait_ge(qk_turned, PAIRS * n + (i - 4) // 2 + 1)
                            act.wait_ge(v_ready, NAT * n + i - 3)
                        act.activation(raw[i % 4][:, :, :],
                                       p_proj[i % 2][:, 0:3 * P].rearrange("p (a b) -> p a b", a=3),
                                       ACT.Copy).then_inc(raw_ready, 1)
                    if projects and i == 3:
                        split_hi(n, 3)
                    if projects and i == 8 and not (isinstance(n, int) and n == HEADS - 1):
                        for p in range(3):
                            split_hi(n + 1, p)
                    if attends and 1 <= i <= TILES:
                        j = i - 1
                        for u in range(Z_UNITS[j]):
                            unit = ENDS[j] - Z_UNITS[j] + u
                            act.wait_ge(weights_turned, UNITS * h + unit + 1)
                            if not (known_first(h) and j < 2):
                                act.wait_ge(o_done, PAIRS * h + j // 2)
                            nb_blocks = min(4, j + 1 - 4 * u)
                            turn = turn_of[("w", unit)] % 2
                            act.activation(wt_hi[:, 4 * u:4 * u + nb_blocks, j % 2, :],
                                           p_turn[turn][:, 0:nb_blocks, :], ACT.Copy).then_inc(wt_hi_ready, 1)
                    if known_first(n) and i == NAT:
                        act.wait_ge(dve_made, 3)
                        act.activation(c["lower"][:, :], c["logit_gap"][:, :], ACT.Sigmoid).then_inc(act_made, 1)
                        act.activation(c["one_minus_lower"][:, :], c["logit_gap"][:, :], ACT.Sigmoid,
                                       scale=-1.0).then_inc(act_made, 1)
                    if projects and i >= NAT:
                        half = i - NAT
                        act.wait_ge(proj_done, USES * n + i + 1)
                        if not (isinstance(n, int) and n < 2):
                            act.wait_ge(o_stored, 16 * (n - 1))
                        act.activation(gated[nb][:, half * HALF:(half + 1) * HALF], p_proj[i % 2][:, :],
                                       ACT.Sigmoid).then_inc(gate_sigmoid, 1)

            square_x(0)
            split_hi(0, 0)
            stream_hi(0)
            split_hi(0, 1)
            split_hi(0, 2)
            square_x(1)
            heads(act, step)

        @block.vector
        def _(dve):
            def split_w_out_hi(r):
                dve.wait_ge(proj_done, USES * HEADS)
                dve.wait_ge(link["w_loaded"][r % 4], 16 * (r // 4) + 16)
                dve.tensor_copy(ut_hi[:, r, :], stage[r % 4][:, :, :].rearrange("p k c -> p (k c)")
                                ).then_inc(w_out_hi_ready, 1)

            def split_lo(h, p):
                if not known_first(h):
                    dve.wait_ge(proj_done, USES * (h - 1) + (NAT if p < 3 else USES))
                dve.wait_ge(w_hi_ready[p], h + 1)
                hi = w_qkv_hi[:, :, p, :] if p < 3 else w_gate_hi[:, :, :]
                lo = w_qkv_lo[:, :, p, :] if p < 3 else w_gate_lo[:, :, :]
                dve.tensor_tensor(lo, stage[p][:, :, :], hi.bitcast(F32), ALU.subtract).then_inc(w_ready[p], 1)

            def norm_x(i):
                if i == 0:
                    dve.wait_ge(gain_loaded, 16)
                dve.wait_ge(x_rms_ready, i + 1)
                dve.wait_ge(x_loaded[i % 2], 16 * (i // 2 + 1))
                if i >= 2:
                    dve.wait_ge(x_turned, 2 * (i - 1))
                dve.scalar_tensor_tensor(out=normed[i % 2][:, 0:D_MODEL], in0=x_tile[i % 2][:, :],
                                         scalar=x_inv_rms[i % 2][:, 0:1], in1=gain_rows,
                                         op0=ALU.mult, op1=ALU.mult).then_inc(normed_ready, 1)

            def stream_lo(i):
                for half in range(2):
                    use = 2 * i + half
                    dve.wait_ge(ut_hi_ready, use + 1)
                    part = (slice(None), slice(4 * half, 4 * half + 4), slice(i * P, (i + 1) * P))
                    dve.tensor_tensor(ut_lo[part], p_z[use % 3][:, :].rearrange("p (a b) -> p a b", a=4),
                                      ut_hi[part].bitcast(F32), ALU.subtract).then_inc(ut_ready, 1)

            def step(h, b, attends, projects):
                n, nb = h + 1, 1 - b
                for i in range(USES):
                    if known_first(n) and i + 1 < TILES:
                        stream_lo(i + 1)
                    if known_first(n) and i + 2 < TILES:
                        norm_x(i + 2)
                    if known_first(n) and i == 1:
                        dve.wait_ge(qk_gains_loaded, 16 * 2)
                        dve.scalar_tensor_tensor(out=c["qk_gain"][:, :], in0=c["q_gain"][:, :],
                                                 scalar=float(P) ** 0.5, in1=c["k_gain"][:, :],
                                                 op0=ALU.mult, op1=ALU.mult).then_inc(dve_made, 1)
                        dve.wait_ge(pool_made, 4)
                        dve.tensor_copy(c["ident_bf"][:, :], c["ident"][:, :]).then_inc(dve_made, 1)
                    if known_first(n) and i == NAT:
                        dve.wait_ge(small_loaded, 16 * 3)
                        dve.tensor_scalar(c["o_scale"][:, :], c["o_gain"][:, :], float(P) ** 0.5, None,
                                          ALU.mult)
                        dve.tensor_tensor(c["logit_gap"][:, :], c["logits"][:, 1, :], c["logits"][:, 0, :],
                                          ALU.subtract).then_inc(dve_made, 1)
                    if attends and i < TILES:
                        width = (i + 1) * P
                        if known_first(h) and i == 0:
                            dve.wait_ge(skip_set, 2)
                        dve.wait_ge(sigmoids_ready, UNITS * h + ENDS[i])
                        chain = skip[i % 2][:, 0:width][:, ::-1]
                        dve.tensor_tensor_scan(chain, chain, chain, 1.0, ALU.mult, ALU.min).then_inc(scan_done, 1)
                        dve.wait_ge(scan_done, TILES * h + i + 1)
                        dve.tensor_tensor(beta[i % 2][:, 0:width], beta[i % 2][:, 0:width],
                                          skip[i % 2][:, 1:width + 1], ALU.mult).then_inc(weights_ready, 1)
                    if projects and i >= 3 and i % 2 == 1:
                        m = (i - 3) // 2
                        dve.wait_ge(qk_hi_ready, PAIRS * n + m + 1)
                        if not (isinstance(n, int) and n < 2):
                            dve.wait_ge(z_done, UNITS * (n - 1))
                        turn = (turn_of if attends else turn_alone)[("qk", m)] % 2
                        cols = slice(2 * m * P, (2 * m + 2) * P)
                        dve.tensor_tensor(qt_lo[nb][:, cols], p_turn[turn][:, 0:2, :].rearrange("p a b -> p (a b)"),
                                          qt_hi[nb][:, cols].bitcast(F32), ALU.subtract)
                        dve.scalar_tensor_tensor(out=kt_lo[nb][:, cols],
                                                 in0=p_turn[turn][:, 2:4, :].rearrange("p a b -> p (a b)"),
                                                 scalar=c["qk_gain"][:, 0:1], in1=kt_hi[nb][:, cols].bitcast(F32),
                                                 op0=ALU.mult, op1=ALU.subtract).then_inc(qk_ready, 1)
                    if projects and i < NAT:
                        dve.wait_ge(raw_ready, NAT * n + i + 1)
                        if i >= 2 or not known_first(n):
                            dve.wait_ge(mean_ready, NAT * n + i - 1)
                        if i >= 1 or not known_first(n):
                            dve.wait_ge(sums_ready, 2 * (NAT * n + i))
                        for part in range(2):
                            dve.tensor_tensor_reduce(squares[part][:, :], raw[i % 4][:, part, :],
                                                     raw[i % 4][:, part, :], 1.0, 0.0, ALU.mult, ALU.add,
                                                     sum_sq[i % 2][:, part:part + 1]).then_inc(sums_ready, 1)
                        if not (isinstance(n, int) and n < 2):
                            dve.wait_ge(o_done, PAIRS * (n - 1))
                        dve.tensor_copy(v_hi[nb][:, i, :], raw[i % 4][:, 2, :]).then_inc(v_hi_ready, 1)
                        dve.wait_ge(v_hi_ready, NAT * n + i + 1)
                        dve.tensor_tensor(v_lo[nb][:, i, :], raw[i % 4][:, 2, :], v_hi[nb][:, i, :].bitcast(F32),
                                          ALU.subtract).then_inc(v_ready, 1)
                    if projects and i == 3:
                        split_lo(n, 3)
                    if projects and i == 8 and not (isinstance(n, int) and n == HEADS - 1):
                        for p in range(3):
                            split_lo(n + 1, p)
                    if not projects:
                        for r in W_OUT_AT.get(i, []):
                            split_w_out_hi(r)
                    if attends and i >= 3 and i % 2 == 1:
                        g = (i - 3) // 2
                        dve.wait_ge(o_done, PAIRS * h + g + 1)
                        dve.wait_ge(gate_ready, GATE * h + GATE)
                        cols = slice(2 * g * P, (2 * g + 2) * P)
                        dve.tensor_tensor(gated[b][:, cols], gated[b][:, cols],
                                          p_o[:, :, :].rearrange("p a b -> p (a b)"),
                                          ALU.mult).then_inc(o_gated, 1)
                    if attends and 1 <= i <= TILES:
                        j = i - 1
                        for u in range(Z_UNITS[j]):
                            unit = ENDS[j] - Z_UNITS[j] + u
                            dve.wait_ge(wt_hi_ready, UNITS * h + unit + 1)
                            if not (known_first(h) and j < 2):
                                dve.wait_ge(o_done, PAIRS * h + j // 2)
                            nb_blocks = min(4, j + 1 - 4 * u)
                            turn = turn_of[("w", unit)] % 2
                            dve.tensor_tensor(wt_lo[:, 4 * u:4 * u + nb_blocks, j % 2, :],
                                              p_turn[turn][:, 0:nb_blocks, :],
                                              wt_hi[:, 4 * u:4 * u + nb_blocks, j % 2, :].bitcast(F32),
                                              ALU.subtract).then_inc(wt_ready, 1)
                    if projects and i >= NAT:
                        half = i - NAT
                        cols = slice(half * HALF, (half + 1) * HALF)
                        dve.wait_ge(gate_sigmoid, GATE * n + half + 1)
                        dve.tensor_tensor(gated[nb][:, cols], gated[nb][:, cols], p_proj[i % 2][:, :],
                                          ALU.mult).then_inc(gate_ready, 1)

            norm_x(0)
            split_lo(0, 0)
            stream_lo(0)
            split_lo(0, 1)
            split_lo(0, 2)
            norm_x(1)
            heads(dve, step)

        @block.gpsimd
        def _(pool):
            def rms_of_x(i):
                pool.wait_ge(x_sum_ready, i + 1)
                pool.tensor_scalar(x_mean_sq[i % 2][:, :], x_sum_sq[i % 2][:, :], 1.0 / D_MODEL, RMS_EPS,
                                   ALU.mult, ALU.add).then_inc(x_mean_ready, 1)
                pool.wait_ge(x_mean_ready, i + 1)
                if i >= 2:
                    pool.wait_ge(normed_ready, i - 1)
                pool.tensor_tensor(x_inv_rms[i % 2][:, :], x_mean_sq[i % 2][:, :], c["minus_half"][:, 0:1],
                                   ALU.pow).then_inc(x_rms_ready, 1)

            pool.memset(c["minus_half"][:, :], -0.5).then_inc(pool_made, 1)
            pool.memset(c["ident"][:, :], 0.0).then_inc(pool_made, 1)
            pool.memset(c["causal_neg"][:, :], 0.0).then_inc(pool_made, 1)
            pool.wait_ge(pool_made, 3)
            pool.affine_select(out=c["ident"][:, :], in_=c["ident"][:, :], compare_op=ALU.not_equal, fill=1.0,
                               base=0, pattern=[[-1, P]], channel_multiplier=1).then_inc(pool_made, 1)
            rms_of_x(0)
            pool.affine_select(out=c["causal_neg"][:, :], in_=c["causal_neg"][:, :], compare_op=ALU.is_gt, fill=NEG,
                               base=0, pattern=[[-1, P]], channel_multiplier=1).then_inc(pool_made, 1)
            pool.memset(c["minus_one"][:, :], -1.0)
            pool.memset(c["head_eps"][:, :], RMS_EPS * P)
            pool.memset(c["ones_col"][:, :], 1.0).then_inc(pool_made, 1)
            for i in range(2):
                pool.memset(skip[i][:, SEQ:SEQ + 1], 1.0).then_inc(skip_set, 1)
            rms_of_x(1)

            def step(h, b, attends, projects):
                n, nb = h + 1, 1 - b
                if not projects:
                    for r in range(HEADS):
                        pool.wait_ge(w_out_hi_ready, r + 1)
                        pool.tensor_tensor(ut_lo[:, r, :], stage[r % 4][:, :, :].rearrange("p k c -> p (k c)"),
                                           ut_hi[:, r, :].bitcast(F32), ALU.subtract).then_inc(w_out_ready, 1)
                    return
                for i in range(NAT):
                    if known_first(n) and i + 2 < TILES:
                        rms_of_x(i + 2)
                    rms = inv_rms[nb][i]
                    pool.wait_ge(sums_ready, 2 * (NAT * n + i) + 2)
                    if i >= 2 or not known_first(n):
                        pool.wait_ge(rms_ready, NAT * n + i - 1)
                    pool.tensor_tensor(mean_sq[i % 2][:, :], sum_sq[i % 2][:, :], c["head_eps"][:, 0:2],
                                       ALU.add).then_inc(mean_ready, 1)
                    pool.wait_ge(mean_ready, NAT * n + i + 1)
                    if not (isinstance(n, int) and n < 2):
                        pool.wait_ge(sigmoids_ready, UNITS * (n - 1))
                    pool.tensor_tensor(rms[:, 0:2], mean_sq[i % 2][:, :], c["minus_half"][:, 0:2],
                                       ALU.pow).then_inc(k_ready, 1)
                    pool.wait_ge(k_ready, 2 * (NAT * n + i) + 1)
                    pool.tensor_tensor(rms[:, 2:3], rms[:, 0:1], c["minus_one"][:, :], ALU.mult).then_inc(rms_ready, 1)
                    pool.wait_ge(raw_ready, NAT * n + i + 1)
                    if i >= 4 or not known_first(n):
                        pool.wait_ge(qk_turned, PAIRS * n + (i - 4) // 2 + 1)
                    pool.tensor_tensor(k_scaled[i % 4][:, :], raw[i % 4][:, 1, :], rms[:, 1:2].to_broadcast([P, P]),
                                       ALU.mult).then_inc(k_ready, 1)

            heads(pool, step)

        @block.tensor
        def _(pe):
            def bank_is_read(h, attends, kind, which):
                if not attends:
                    if which >= 2:
                        pe.wait_ge(qk_ready, PAIRS * (h + 1) + which - 1)
                    return
                at = turn_of[(kind, which)]
                if at < 2:
                    pe.wait_ge(qk_ready, PAIRS * (h + 1))
                    if not known_first(h):
                        pe.wait_ge(wt_ready, UNITS * h)
                    return
                before, w = next(key for key, value in turn_of.items() if value == at - 2)
                if before == "w":
                    pe.wait_ge(wt_ready, UNITS * h + w + 1)
                elif not (isinstance(h, int) and h == HEADS - 1):
                    pe.wait_ge(qk_ready, PAIRS * (h + 1) + w + 1)

            def turn_x(i):
                pe.wait_ge(normed_ready, i + 1)
                for half in range(2):
                    use = 2 * i + half
                    if use >= 3:
                        pe.wait_ge(ut_ready, use - 2)
                    for q in range(4):
                        kt = 4 * half + q
                        last = pe.transpose(p_z[use % 3][:, q * P:(q + 1) * P], normed[i % 2][:, kt * P:(kt + 1) * P],
                                            c["ident"][:, :])
                    last.then_inc(x_turned, 1)

            def turn_qk(h, m, attends):
                n = h + 1
                pe.wait_ge(k_ready, 2 * (NAT * n + 2 * m + 2))
                bank_is_read(h, attends, "qk", m)
                bank = p_turn[(turn_of if attends else turn_alone)[("qk", m)] % 2]
                for t in range(2):
                    pe.transpose(bank[:, t, :], raw[(2 * m + t) % 4][:, 0, :], c["ident"][:, :])
                    last = pe.transpose(bank[:, 2 + t, :], k_scaled[(2 * m + t) % 4][:, :], c["ident"][:, :])
                last.then_inc(qk_turned, 1)

            def step(h, b, attends, projects):
                n, nb = h + 1, 1 - b
                for i in range(USES):
                    if known_first(h) and attends and i == 0:
                        pe.wait_ge(ut_ready, 2 * TILES)
                        pe.wait_ge(dve_made, 2)
                        pe.wait_ge(pool_made, 6)
                    if attends and i < TILES:
                        pe.wait_ge(qk_ready, PAIRS * h + i // 2 + 1)
                        rows = slice(i * P, (i + 1) * P)
                        for u in range(Z_UNITS[i]):
                            width = min(HALF, (i + 1) * P - u * HALF)
                            unit = ENDS[i] - Z_UNITS[i] + u
                            if unit >= 3 or not known_first(h):
                                pe.wait_ge(sigmoids_ready, UNITS * h + unit - 2)
                            z = p_z[unit % 3][:, 0:width]
                            cols = slice(u * HALF, u * HALF + width)
                            pe.matmul(z, qt_hi[b][:, rows], kt_hi[b][:, cols], start=True, stop=False,
                                      skip_group_check=True)
                            if u == Z_UNITS[i] - 1:
                                pe.matmul(p_z[unit % 3][:, width - P:width], c["ident_bf"][:, :],
                                          c["causal_neg"][:, :], start=False, stop=False, skip_group_check=True)
                            pe.matmul(z, qt_hi[b][:, rows], kt_lo[b][:, cols], start=False, stop=False,
                                      skip_group_check=True)
                            pe.matmul(z, qt_lo[b][:, rows], kt_hi[b][:, cols], start=False, stop=True,
                                      skip_group_check=True).then_inc(z_done, 1)
                    if projects:
                        if i >= 2:
                            pe.wait_ge(raw_ready, NAT * n + i - 1)
                        elif not known_first(n):
                            pe.wait_ge(gate_ready, GATE * (n - 1) + i + 1)
                        if i == 0:
                            for p in range(3):
                                pe.wait_ge(w_ready[p], n + 1)
                        if i == NAT:
                            pe.wait_ge(w_ready[3], n + 1)
                        if known_first(n) and i < TILES:
                            pe.wait_ge(ut_ready, 2 * i + 2)
                        for kt in range(KT):
                            if i >= 3 and i % 2 == 1 and kt == 2:
                                turn_qk(h, (i - 3) // 2, attends)
                            if known_first(n) and i + 1 < TILES and kt == KT // 2:
                                turn_x(i + 1)
                            if i < NAT:
                                rows = slice(i * P, (i + 1) * P)
                                last = matmul_exact(pe, p_proj[i % 2][:, 0:3 * P],
                                                    ut_hi[:, kt, rows], ut_lo[:, kt, rows],
                                                    w_qkv_hi[:, kt, :, :].rearrange("p a b -> p (a b)"),
                                                    w_qkv_lo[:, kt, :, :].rearrange("p a b -> p (a b)"),
                                                    kt == 0, kt == KT - 1)
                            else:
                                cols = slice((i - NAT) * HALF, (i - NAT + 1) * HALF)
                                last = matmul_exact(pe, p_proj[i % 2][:, :], w_gate_hi[:, kt, :],
                                                    w_gate_lo[:, kt, :], ut_hi[:, kt, cols], ut_lo[:, kt, cols],
                                                    kt == 0, kt == KT - 1)
                        last.then_inc(proj_done, 1)
                    if attends and i >= 3 and i % 2 == 1:
                        g = (i - 3) // 2
                        pe.wait_ge(wt_ready, UNITS * h + ENDS[2 * g + 1])
                        pe.wait_ge(v_ready, NAT * h + NAT)
                        if g >= 1 or not known_first(h):
                            pe.wait_ge(o_gated, PAIRS * h + g)
                        for s in range(2 * g + 2):
                            o = p_o[:, :, :] if s <= 2 * g else p_o[:, 1, :]
                            w_h = wt_hi[:, s, :, :] if s <= 2 * g else wt_hi[:, s, 1, :]
                            w_l = wt_lo[:, s, :, :] if s <= 2 * g else wt_lo[:, s, 1, :]
                            last = matmul_exact(pe, o, v_hi[b][:, s, :], v_lo[b][:, s, :], w_h, w_l,
                                                s == 0, s == 2 * g + 1)
                        last.then_inc(o_done, 1)
                    if attends and 1 <= i <= TILES:
                        j = i - 1
                        pe.wait_ge(weights_ready, TILES * h + j + 1)
                        for u in range(Z_UNITS[j]):
                            unit = ENDS[j] - Z_UNITS[j] + u
                            bank_is_read(h, attends, "w", unit)
                            for s in range(4 * u, min(4 * u + 4, j + 1)):
                                last = pe.transpose(p_turn[turn_of[("w", unit)] % 2][:, s - 4 * u, :],
                                                    beta[j % 2][:, s * P:(s + 1) * P], c["ident"][:, :])
                            last.then_inc(weights_turned, 1)

            pe.wait_ge(pool_made, 4)
            turn_x(0)
            heads(pe, step)


def build_output_projection(nc, tag, c, m_in, link, mixed, w_hi, w_lo, residual, dst, gain, ut_hi, ut_lo,
                            next_weights):
    FIRST_OF_PART = [0, 2, HEADS - 1]
    PARTS = [slice(a, b) for a, b in zip(FIRST_OF_PART, FIRST_OF_PART[1:] + [HEADS])]
    with ExitStack() as ctx:
        def sb(name, shape, dt=F32):
            return ctx.enter_context(nc.sbuf_tensor(f"{tag}_{name}", shape, dt))

        def sem(name):
            return ctx.enter_context(nc.semaphore(f"{tag}_{name}"))

        m_hi = [sb(f"m_hi{i}", [P, HEADS, P], F32R) for i in range(2)]
        m_lo = [sb(f"m_lo{i}", [P, HEADS, P], F32R) for i in range(2)]
        h_tile = [sb(f"h_tile{i}", [P, D_MODEL]) for i in range(2)]
        p_y = [ctx.enter_context(nc.psum_tensor(f"{tag}_p_y{i}", [P, HALF], F32)) for i in range(4)]
        if gain is not None:
            gain_rows = sb("gain_rows", [P, D_MODEL])
            squares = sb("squares", [P, D_MODEL])
            normed = sb("normed", [P, D_MODEL])
            sum_sq = [sb(f"sum_sq{i}", [P, 1]) for i in range(2)]
            mean_sq = [sb(f"mean_sq{i}", [P, 1]) for i in range(2)]
            inv_rms = [sb(f"inv_rms{i}", [P, 1]) for i in range(2)]
            turned = [ctx.enter_context(nc.psum_tensor(f"{tag}_turned{i}", [P, 4, P], F32)) for i in range(2)]

        gain_loaded = sem("gain_loaded")
        m_loaded = link["m_loaded"]
        last_loaded = [sem(f"last_loaded{i}") for i in range(2)]
        m_hi_ready = sem("m_hi_ready")
        m_ready = sem("m_ready")
        r_loaded = [sem(f"r_loaded{i}") for i in range(2)]
        y_done = sem("y_done")
        h_ready = sem("h_ready")
        stored = sem("stored")
        sum_ready = sem("sum_ready")
        mean_ready = sem("mean_ready")
        rms_ready = sem("rms_ready")
        normed_ready = sem("normed_ready")
        turned_ready = sem("turned_ready")
        hi_ready = sem("hi_ready")
        lo_ready = sem("lo_ready")

        block = ctx.enter_context(nc.Block())

        @block.sync
        def _(sp):
            def load_residual(i):
                if i >= 2:
                    sp.wait_ge(stored, 16 * (i - 1))
                    if gain is not None:
                        sp.wait_ge(normed_ready, i - 1)
                sp.dma_start(h_tile[i % 2][:, :], residual[i * P:(i + 1) * P, :]).then_inc(r_loaded[i % 2], 16)

            sp.wait_ge(link["stored"], 16 * HEADS)
            for i in range(2):
                load_mixed(sp, m_in, mixed, i, slice(HEADS - 1, HEADS)).then_inc(last_loaded[i], 16)
            for i in range(2):
                load_residual(i)
            if gain is not None:
                sp.dma_start(gain_rows[:, :], gain[0:1, :].to_broadcast([P, D_MODEL])).then_inc(gain_loaded, 16)
            if next_weights is not None:
                stage, w_in, w_loaded = next_weights
                for p in range(4):
                    load_columns(sp, stage, w_in, 0, p).then_inc(w_loaded[p], 16)
            for i in range(TILES):
                if i + 2 < TILES:
                    sp.wait_ge(m_ready, len(PARTS) * (i + 1))
                    load_mixed(sp, m_in, mixed, i + 2, slice(0, HEADS)).then_inc(m_loaded[i % 2], 16)
                sp.wait_ge(h_ready, 2 * i + 2)
                sp.dma_start(dst[i * P:(i + 1) * P, :], h_tile[i % 2][:, :]).then_inc(stored, 16)
                if i + 2 < TILES:
                    load_residual(i + 2)
            sp.wait_ge(stored, 16 * TILES)

        @block.scalar
        def _(act):
            def mixed_hi(i):
                if i >= 2:
                    act.wait_ge(y_done, 2 * (i - 1))
                act.wait_ge(m_loaded[i % 2], 16 * (i // 2 + 1))
                for part, heads in enumerate(PARTS):
                    if i < 2 and part == len(PARTS) - 1:
                        act.wait_ge(last_loaded[i], 16)
                    act.activation(m_hi[i % 2][:, heads, :], m_in[i % 2][:, heads, :],
                                   ACT.Copy).then_inc(m_hi_ready, 1)

            mixed_hi(0)
            for i in range(TILES + 1):
                if i + 1 < TILES:
                    mixed_hi(i + 1)
                if gain is not None and i < TILES:
                    act.wait_ge(h_ready, 2 * i + 2)
                    if i >= 1:
                        act.wait_ge(sum_ready, i)
                    if i >= 2:
                        act.wait_ge(mean_ready, i - 1)
                    act.activation(squares[:, :], h_tile[i % 2][:, :], ACT.Square,
                                   accum_out=sum_sq[i % 2][:, :]).then_inc(sum_ready, 1)
                if gain is not None and i >= 1:
                    j = i - 1
                    for half in range(2):
                        act.wait_ge(turned_ready, 2 * j + half + 1)
                        act.activation(ut_hi[:, 4 * half:4 * half + 4, j * P:(j + 1) * P],
                                       turned[half][:, :, :], ACT.Copy).then_inc(hi_ready, 1)

        @block.vector
        def _(dve):
            def mixed_lo(i):
                if i >= 2:
                    dve.wait_ge(y_done, 2 * (i - 1))
                for part, heads in enumerate(PARTS):
                    dve.wait_ge(m_hi_ready, len(PARTS) * i + part + 1)
                    dve.tensor_tensor(m_lo[i % 2][:, heads, :], m_in[i % 2][:, heads, :],
                                      m_hi[i % 2][:, heads, :].bitcast(F32), ALU.subtract).then_inc(m_ready, 1)

            mixed_lo(0)
            for i in range(TILES + 1):
                if i + 1 < TILES:
                    mixed_lo(i + 1)
                if i < TILES:
                    dve.wait_ge(r_loaded[i % 2], 16 * (i // 2 + 1))
                    for half in range(2):
                        cols = slice(half * HALF, (half + 1) * HALF)
                        dve.wait_ge(y_done, 2 * i + half + 1)
                        dve.tensor_tensor(h_tile[i % 2][:, cols], h_tile[i % 2][:, cols],
                                          p_y[(2 * i + half) % 4][:, :], ALU.add).then_inc(h_ready, 1)
                if gain is not None and i >= 1:
                    j = i - 1
                    for half in range(2):
                        dve.wait_ge(hi_ready, 2 * j + half + 1)
                        dve.tensor_tensor(ut_lo[:, 4 * half:4 * half + 4, j * P:(j + 1) * P], turned[half][:, :, :],
                                          ut_hi[:, 4 * half:4 * half + 4, j * P:(j + 1) * P].bitcast(F32),
                                          ALU.subtract).then_inc(lo_ready, 1)
                if gain is not None and i < TILES:
                    if i == 0:
                        dve.wait_ge(gain_loaded, 16)
                    dve.wait_ge(rms_ready, i + 1)
                    dve.wait_ge(h_ready, 2 * i + 2)
                    if i >= 1:
                        dve.wait_ge(turned_ready, 2 * i)
                    dve.scalar_tensor_tensor(out=normed[:, :], in0=h_tile[i % 2][:, :],
                                             scalar=inv_rms[i % 2][:, 0:1], in1=gain_rows[:, :],
                                             op0=ALU.mult, op1=ALU.mult).then_inc(normed_ready, 1)

        @block.gpsimd
        def _(pool):
            if gain is None:
                return
            for i in range(TILES):
                pool.wait_ge(sum_ready, i + 1)
                pool.tensor_scalar(mean_sq[i % 2][:, :], sum_sq[i % 2][:, :], 1.0 / D_MODEL, RMS_EPS,
                                   ALU.mult, ALU.add).then_inc(mean_ready, 1)
                pool.wait_ge(mean_ready, i + 1)
                if i >= 2:
                    pool.wait_ge(normed_ready, i - 1)
                pool.tensor_tensor(inv_rms[i % 2][:, :], mean_sq[i % 2][:, :], c["minus_half"][:, 0:1],
                                   ALU.pow).then_inc(rms_ready, 1)

        @block.tensor
        def _(pe):
            for i in range(TILES + 1):
                if i < TILES:
                    for half in range(2):
                        use = 2 * i + half
                        if use >= 4:
                            pe.wait_ge(h_ready, use - 3)
                        for h in range(HEADS):
                            if half == 0 and h in FIRST_OF_PART:
                                pe.wait_ge(m_ready, len(PARTS) * i + FIRST_OF_PART.index(h) + 1)
                            cols = slice(half * HALF, (half + 1) * HALF)
                            last = matmul_exact(pe, p_y[use % 4][:, :], m_hi[i % 2][:, h, :], m_lo[i % 2][:, h, :],
                                                w_hi[:, h, cols], w_lo[:, h, cols], h == 0, h == HEADS - 1)
                        last.then_inc(y_done, 1)
                if gain is not None and i >= 1:
                    j = i - 1
                    pe.wait_ge(normed_ready, j + 1)
                    for half in range(2):
                        if j >= 1:
                            pe.wait_ge(lo_ready, 2 * (j - 1) + half + 1)
                        for q in range(4):
                            kt = 4 * half + q
                            last = pe.transpose(turned[half][:, q, :], normed[:, kt * P:(kt + 1) * P],
                                                c["ident"][:, :])
                        last.then_inc(turned_ready, 1)


def build_hgrn(nc, c, stage, m_in, link, w_loaded, w_in, w_out, ut_hi, ut_lo, mixed):
    L = len(LEVELS)
    MASKED = L - 1
    W_OUT_AT = {0: [0, 1], 1: [2, 3], 2: [4], 3: [5], 4: [6], 5: [7]}
    HALVES = SEQ // 2
    USES = 8

    with ExitStack() as ctx:
        def sb(name, shape, dt=F32):
            return ctx.enter_context(nc.sbuf_tensor("g_" + name, shape, dt))

        def psum(name, shape):
            return ctx.enter_context(nc.psum_tensor("g_" + name, shape, F32))

        def sem(name):
            return ctx.enter_context(nc.semaphore("g_" + name))

        w_qf_hi = sb("w_qf_hi", [P, KT, 2, P], F32R)
        w_qf_lo = sb("w_qf_lo", [P, KT, 2, P], F32R)
        w_ig_hi = sb("w_ig_hi", [P, KT, 2, P], F32R)
        w_ig_lo = sb("w_ig_lo", [P, KT, 2, P], F32R)
        q = [sb(f"q{b}", [P, SEQ]) for b in range(2)]
        k = [sb(f"k{b}", [P, SEQ]) for b in range(2)]
        prefix = [sb(f"prefix{b}", [P, SEQ]) for b in range(2)]
        suffix = sb("suffix", [P, SEQ])
        value = [sb(f"value{b}", [P, TILES, P]) for b in range(2)]
        gate = [sb(f"gate{b}", [P, TILES, P]) for b in range(2)]
        q_right = [sb(f"q_right{i}", [P, HALVES]) for i in range(2)]
        k_left = [sb(f"k_left{i}", [P, SEQ]) for i in range(2)]
        scores = [sb(f"scores{b}", [P, TILES, P]) for b in range(2)]
        q_chunk = sb("q_chunk", [P, SEQ])
        k_chunk = sb("k_chunk", [P, SEQ])
        qk = sb("qk", [P, SEQ])
        self_score = sb("self_score", [P, TILES])
        k_turned = sb("k_turned", [P, TILES, P])
        state = sb("state", [P, TILES, P])
        o = sb("o", [P, TILES, P])
        squares = [sb(f"squares{i}", [P, P]) for i in range(2)]
        sum_sq = sb("sum_sq", [P, TILES])
        sum_eps = sb("sum_eps", [P, TILES])
        inv_rms = sb("inv_rms", [P, TILES])
        out_turned = sb("out_turned", [P, SEQ])
        waits_taken = sb("waits_taken", [P, 1])

        p_proj = [psum(f"p_proj{i}", [P, HALF]) for i in range(2)]
        p_level = [psum(f"p_level{i}", [P, HALF]) for i in range(2)]
        p_misc = [psum(f"p_misc{i}", [P, 4, P]) for i in range(4)]

        w_out_hi_ready = sem("w_out_hi_ready")
        w_out_ready = sem("w_out_ready")
        w_hi_ready = [sem(f"w_hi_ready{p}") for p in range(4)]
        w_ready = [sem(f"w_ready{p}") for p in range(4)]
        proj_done = sem("proj_done")
        q_sigmoid = sem("q_sigmoid")
        q_ready = sem("q_ready")
        f_sigmoid = sem("f_sigmoid")
        fk_ready = sem("fk_ready")
        ig_copied = sem("ig_copied")
        gate_ready = sem("gate_ready")
        zeroed = sem("zeroed")
        masks_made = sem("masks_made")
        k_prepared = sem("k_prepared")
        prepared = sem("prepared")
        doubled = sem("doubled")
        level_done = sem("level_done")
        level_placed = sem("level_placed")
        last_placed = sem("last_placed")
        chunk_ready = sem("chunk_ready")
        self_done = sem("self_done")
        self_ready = sem("self_ready")
        k_turned_done = sem("k_turned_done")
        k_turned_ready = sem("k_turned_ready")
        update_done = sem("update_done")
        state_ready = sem("state_ready")
        o_done = sem("o_done")
        o_ready = sem("o_ready")
        sums_ready = sem("sums_ready")
        eps_added = sem("eps_added")
        rms_ready = sem("rms_ready")
        o_gated = sem("o_gated")
        o_turned = sem("o_turned")
        out_ready = sem("out_ready")
        out_stored = link["stored"]

        def heads(eng, step):
            step(-1, 1, False, True)
            step(0, 0, True, True)
            with eng.Fori(0, (HEADS - 4) // 2) as pair:
                step(pair * 2 + 1, 1, True, True)
                step(pair * 2 + 2, 0, True, True)
            step(HEADS - 3, 1, True, True)
            step(HEADS - 2, 0, True, True)
            step(HEADS - 1, 1, True, False)

        def known_first(h):
            return isinstance(h, int) and h <= 0

        block = ctx.enter_context(nc.Block())

        @block.sync
        def _(sp):
            def load_out(r):
                if r < 4:
                    sp.wait_ge(w_ready[r], HEADS)
                else:
                    sp.wait_ge(w_out_ready, r - 3)
                load_w_out(sp, stage, w_out, r).then_inc(link["w_loaded"][r % 4], 16)

            def load_mixed_early(i):
                sp.wait_ge(out_stored, 16 * (HEADS - 1))
                load_mixed(sp, m_in, mixed, i, slice(0, HEADS - 1)).then_inc(link["m_loaded"][i], 16)

            def load(h, p):
                if not known_first(h):
                    sp.wait_ge(w_ready[p], h)
                load_columns(sp, stage, w_in, h, p).then_inc(w_loaded[p], 16)

            def store(h):
                sp.wait_ge(out_ready, 2 * h + 2)
                sp.dma_start(mixed[bass.ds(h, 1), :, :].rearrange("o p s -> p (o s)"),
                             out_turned[:, :]).then_inc(out_stored, 16)

            for h in range(1, 3):
                for p in range(4):
                    load(h, p)
            with sp.Fori(0, HEADS - 3) as h:
                store(h)
                for p in range(4):
                    load(h + 3, p)
            store(HEADS - 3)
            for r in range(4):
                load_out(r)
            store(HEADS - 2)
            load_out(4)
            load_out(5)
            for i in range(2):
                load_mixed_early(i)
            load_out(6)
            load_out(7)
            store(HEADS - 1)

        @block.scalar
        def _(act):
            def split_w_out_hi(r):
                act.wait_ge(proj_done, USES * HEADS)
                act.wait_ge(link["w_loaded"][r % 4], 16 * (r // 4) + 16)
                act.activation(ut_hi[:, r, :], stage[r % 4][:, :, :].rearrange("p k c -> p (k c)"),
                               ACT.Copy).then_inc(w_out_hi_ready, 1)

            def split_hi(h, p):
                if not known_first(h):
                    act.wait_ge(proj_done, USES * (h - 1) + (4 if p < 2 else USES))
                act.wait_ge(w_loaded[p], 16 * h + 16)
                dst = (w_qf_hi if p < 2 else w_ig_hi)[:, :, p % 2, :]
                act.activation(dst, stage[p][:, :, :], ACT.Copy).then_inc(w_hi_ready[p], 1)

            def step(h, b, mixes, projects):
                n, nb = h + 1, 1 - b
                early = isinstance(n, int) and n < 2
                last_head = isinstance(n, int) and n == HEADS - 1
                for i in range(USES):
                    if projects and i == 0 and known_first(n):
                        split_hi(0, 0)
                        split_hi(0, 1)
                    if projects and i in (1, 2):
                        split_hi(n, i + 1)
                    if projects and i in (4, 5) and not last_head:
                        split_hi(n + 1, i - 4)
                    if mixes and i == 3:
                        act.wait_ge(level_placed, MASKED * h + MASKED)
                        act.wait_ge(level_done, L * h + L)
                        act.activation(scores[b][0:P // 2, :, P // 2:P],
                                       p_level[0][0:P // 2, :].rearrange("p (m t) -> p m t", m=TILES),
                                       ACT.Copy).then_inc(last_placed, 1)
                    if mixes and i == 4:
                        for u in range(2):
                            act.wait_ge(k_turned_done, 2 * h + u + 1)
                            if not known_first(h):
                                act.wait_ge(update_done, 2 * h)
                            act.activation(k_turned[:, 4 * u:4 * u + 4, :], p_misc[u][:, :, :],
                                           ACT.Copy).then_inc(k_turned_ready, 1)
                    if not projects:
                        for r in W_OUT_AT.get(i, []):
                            split_w_out_hi(r)
                    if mixes and i == 6:
                        for m in range(TILES):
                            act.wait_ge(o_ready, TILES * h + m + 1)
                            if m >= 2 or not known_first(h):
                                act.wait_ge(sums_ready, TILES * h + m - 1)
                            if m == 0 and not known_first(h):
                                act.wait_ge(eps_added, h)
                            act.activation(squares[m % 2][:, :], o[:, m, :], ACT.Square,
                                           accum_out=sum_sq[:, m:m + 1]).then_inc(sums_ready, 1)
                    if projects:
                        act.wait_ge(proj_done, USES * n + i + 1)
                        cols = slice((i % 2) * HALF, (i % 2 + 1) * HALF)
                        if i == 0 and not early:
                            act.wait_ge(state_ready, (TILES - 1) * (n - 1))
                            act.wait_ge(o_gated, n - 1)
                            act.wait_ge(chunk_ready, n - 1)
                        if i < 2:
                            act.activation(q[nb][:, cols], p_proj[i % 2][:, :], ACT.Sigmoid).then_inc(q_sigmoid, 1)
                        elif i < 4:
                            act.activation(prefix[nb][:, cols], p_proj[i % 2][:, :], ACT.Sigmoid)
                            act.activation(k[nb][:, cols], p_proj[i % 2][:, :], ACT.Sigmoid,
                                           scale=-1.0).then_inc(f_sigmoid, 1)
                        else:
                            both = p_proj[i % 2][:, :].rearrange("p (t a v) -> p t a v", t=2, a=2)
                            tiles = slice(2 * (i - 4), 2 * (i - 4) + 2)
                            act.activation(value[nb][:, tiles, :], both[:, :, 0, :], ACT.Copy)
                            act.activation(gate[nb][:, tiles, :], both[:, :, 1, :],
                                           ACT.Sigmoid).then_inc(ig_copied, 1)
                    if mixes and i == 7:
                        for u in range(2):
                            act.wait_ge(o_turned, 2 * h + u + 1)
                            if u == 0 and not known_first(h):
                                act.wait_ge(out_stored, 16 * h)
                            act.activation(out_turned[:, u * HALF:(u + 1) * HALF],
                                           p_misc[2 + u][:, :, :].rearrange("p a b -> p (a b)"), ACT.Copy,
                                           scale=c["o_scale"][:, 0:1]).then_inc(out_ready, 1)

            heads(act, step)

        @block.vector
        def _(dve):

            def split_lo(h, p):
                if not known_first(h):
                    dve.wait_ge(proj_done, USES * (h - 1) + (4 if p < 2 else USES))
                dve.wait_ge(w_hi_ready[p], h + 1)
                hi = (w_qf_hi if p < 2 else w_ig_hi)[:, :, p % 2, :]
                lo = (w_qf_lo if p < 2 else w_ig_lo)[:, :, p % 2, :]
                dve.tensor_tensor(lo, stage[p][:, :, :], hi.bitcast(F32), ALU.subtract).then_inc(w_ready[p], 1)

            def by_halves(t, half):
                return t[:, :].rearrange("p (b two r) -> p b two r", two=2, r=half)

            def prepare(h, b, level):
                half = LEVELS[level]
                blocks = SEQ // (2 * half)
                pre, suf = by_halves(prefix[b], half), by_halves(suffix, half)
                if level == 0:
                    dve.wait_ge(fk_ready, 2 * h + 2)
                    dve.wait_ge(q_ready, 2 * h + 2)
                    if known_first(h):
                        dve.wait_ge(zeroed, 5)
                    else:
                        dve.wait_ge(chunk_ready, h)
                else:
                    dve.wait_ge(doubled, 2 * (L * h + level) - 1)
                if level >= 2:
                    dve.wait_ge(level_done, L * h + level - 1)
                elif not known_first(h):
                    dve.wait_ge(level_done, L * h)
                q_out = q_right[level % 2][:, :].rearrange("p (b r) -> p b r", r=half)
                k_out = by_halves(k_left[level % 2], half)[:, :, 0, :]
                k_in = by_halves(k[b], half)[:, :, 0, :]
                if level == 0:
                    dve.tensor_copy(k_out, k_in).then_inc(k_prepared, 1)
                else:
                    dve.tensor_tensor(k_out, k_in, suf[:, :, 0, :], ALU.mult).then_inc(k_prepared, 1)
                    dve.wait_ge(doubled, 2 * (L * h + level))
                dve.tensor_tensor(q_out, by_halves(q[b], half)[:, :, 1, :], pre[:, :, 1, :],
                                  ALU.mult).then_inc(prepared, 1)
                dve.wait_ge(k_prepared, L * h + level + 1)
                if level == 0:
                    dve.tensor_copy(suf[:, :, 0, :], pre[:, :, 1, :])
                    dve.memset(suf[:, :, 1, :], 1.0).then_inc(doubled, 1)
                else:
                    dve.tensor_tensor(suf[:, :, 0, :], suf[:, :, 0, :],
                                      pre[:, :, 1, half - 1:half].to_broadcast([P, blocks, half]),
                                      ALU.mult).then_inc(doubled, 1)
                dve.wait_ge(prepared, L * h + level + 1)
                dve.wait_ge(doubled, 2 * (L * h + level) + 1)
                dve.tensor_tensor(pre[:, :, 1, :], pre[:, :, 1, :],
                                  pre[:, :, 0, half - 1:half].to_broadcast([P, blocks, half]),
                                  ALU.mult).then_inc(doubled, 1)

            def place(h, b, level):
                half = LEVELS[level]
                blocks = P // (2 * half)
                dve.wait_ge(level_done, L * h + level + 1)
                if level == 0 and not (isinstance(h, int) and h < 2):
                    dve.wait_ge(o_done, 2 * (h - 1))
                if level >= 1:
                    dve.wait_ge(level_placed, MASKED * h + level)
                dve.memset(waits_taken[:, :], 0.0)
                dve.wait_ge(masks_made, 1 + 2 * L)
                dst = scores[b][:, :, :].rearrange("p m (b two r) -> p m b two r", two=2, r=half)[:, :, :, 1, :]
                mask = c["level_mask"][:, level, :].bitcast(I32).rearrange("p (b r) -> p b r", r=half)
                dve.copy_predicated(dst, mask.unsqueeze(1).to_broadcast([P, TILES, blocks, half]),
                                    p_level[level % 2][:, :].rearrange("p (m b r) -> p m b r", m=TILES, r=half)
                                    ).then_inc(level_placed, 1)

            def chunk_operands(h, b):
                dve.wait_ge(doubled, 2 * L * (h + 1))
                if not known_first(h):
                    dve.wait_ge(o_done, 2 * h)
                    dve.wait_ge(k_turned_done, 2 * h)
                    dve.wait_ge(self_done, h)
                dve.tensor_tensor(k_chunk[:, :], k[b][:, :], suffix[:, :], ALU.mult)
                dve.tensor_tensor(qk[:, :], q[b][:, :], k[b][:, :], ALU.mult)
                dve.tensor_tensor(q_chunk[:, :], q[b][:, :], prefix[b][:, :], ALU.mult).then_inc(chunk_ready, 1)

            def states(h, b):
                for m in range(TILES - 1):
                    bank = p_misc[2 + m // 4][:, m % 4, :]
                    dve.wait_ge(update_done, 2 * h + m // 4 + 1)
                    if m == 0:
                        if not known_first(h):
                            dve.wait_ge(o_done, 2 * h)
                        dve.tensor_copy(state[:, 1, :], bank).then_inc(state_ready, 1)
                    else:
                        dve.wait_ge(state_ready, (TILES - 1) * h + m)
                        dve.scalar_tensor_tensor(out=state[:, m + 1, :], in0=state[:, m, :],
                                                 scalar=prefix[b][:, m * P + P - 1:m * P + P], in1=bank,
                                                 op0=ALU.mult, op1=ALU.add).then_inc(state_ready, 1)

            def outputs(h, b):
                dve.wait_ge(self_ready, h + 1)
                if not known_first(h):
                    dve.wait_ge(o_turned, 2 * h)
                for m in range(TILES):
                    dve.wait_ge(o_done, 2 * h + m // 4 + 1)
                    dve.scalar_tensor_tensor(out=o[:, m, :], in0=value[b][:, m, :], scalar=self_score[:, m:m + 1],
                                             in1=p_misc[m // 4][:, m % 4, :], op0=ALU.mult,
                                             op1=ALU.add).then_inc(o_ready, 1)

            def gate_outputs(h, b):
                dve.wait_ge(rms_ready, h + 1)
                dve.wait_ge(gate_ready, 4 * h + 4)
                for m in range(TILES):
                    ins = dve.scalar_tensor_tensor(out=o[:, m, :], in0=o[:, m, :], scalar=inv_rms[:, m:m + 1],
                                                   in1=gate[b][:, m, :], op0=ALU.mult, op1=ALU.mult)
                ins.then_inc(o_gated, 1)

            def step(h, b, mixes, projects):
                n, nb = h + 1, 1 - b
                last_head = isinstance(n, int) and n == HEADS - 1
                for i in range(USES):
                    if mixes and i < 3:
                        prepare(h, b, 4 + i)
                        place(h, b, 3 + i)
                    if mixes and i == 3:
                        chunk_operands(h, b)
                    if mixes and i == 4:
                        dve.wait_ge(self_done, h + 1)
                        if not known_first(h):
                            dve.wait_ge(o_ready, TILES * h)
                        dve.tensor_copy(self_score[:, :], p_level[1][:, 0:TILES]).then_inc(self_ready, 1)
                    if projects and i >= 4:
                        prepare(n, nb, i - 4)
                    if mixes and i == 5:
                        states(h, b)
                    if mixes and i == 6:
                        outputs(h, b)
                    if projects and i >= 5:
                        place(n, nb, i - 5)
                    if mixes and i == 7:
                        gate_outputs(h, b)
                    if projects and i == 0 and known_first(n):
                        split_lo(0, 0)
                        split_lo(0, 1)
                    if projects and i in (1, 2):
                        split_lo(n, i + 1)
                    if projects and i in (4, 5) and not last_head:
                        split_lo(n + 1, i - 4)
                    if projects:
                        cols = slice((i % 2) * HALF, (i % 2 + 1) * HALF)
                        if i < 2:
                            dve.wait_ge(q_sigmoid, 2 * n + i + 1)
                            dve.tensor_tensor(q[nb][:, cols], q[nb][:, cols], p_proj[i % 2][:, :],
                                              ALU.mult).then_inc(q_ready, 1)
                        elif i < 4:
                            dve.wait_ge(f_sigmoid, 2 * n + i - 1)
                            scale = c["one_minus_lower"][:, bass.ds(n, 1)]
                            dve.tensor_scalar(prefix[nb][:, cols], prefix[nb][:, cols], scale,
                                              c["lower"][:, bass.ds(n, 1)], ALU.mult, ALU.add)
                            dve.tensor_scalar(k[nb][:, cols], k[nb][:, cols], scale, None,
                                              ALU.mult).then_inc(fk_ready, 1)
                        else:
                            dve.wait_ge(ig_copied, 4 * n + i - 3)
                            tiles = slice(2 * (i - 4), 2 * (i - 4) + 2)
                            both = p_proj[i % 2][:, :].rearrange("p (t a v) -> p t a v", t=2, a=2)
                            dve.tensor_tensor(gate[nb][:, tiles, :], gate[nb][:, tiles, :], both[:, :, 1, :],
                                              ALU.mult).then_inc(gate_ready, 1)

            heads(dve, step)

        @block.gpsimd
        def _(pool):
            pool.memset(suffix[:, :], 1.0).then_inc(zeroed, 1)
            for i in range(2):
                pool.memset(k_left[i][:, :], 0.0).then_inc(zeroed, 1)
                pool.memset(scores[i][:, :, :], 0.0).then_inc(zeroed, 1)
            pool.memset(c["level_mask"][:, :, :], 1.0).then_inc(masks_made, 1)
            pool.wait_ge(masks_made, 1)
            for n, half in enumerate(LEVELS):
                mask = c["level_mask"][:, n, :].rearrange("p (b r) -> p b r", r=half)
                pool.affine_select(out=mask, in_=mask, compare_op=ALU.is_ge, fill=0.0, base=0,
                                   pattern=[[-2 * half, P // 2 // half], [0, half]],
                                   channel_multiplier=1).then_inc(masks_made, 1)
                pool.wait_ge(masks_made, 2 + 2 * n)
                pool.affine_select(out=mask, in_=mask, compare_op=ALU.is_gt, fill=0.0, base=half,
                                   pattern=[[2 * half, P // 2 // half], [0, half]],
                                   channel_multiplier=-1).then_inc(masks_made, 1)

            def step(h, b, mixes, projects):
                if not mixes:
                    return
                if not projects:
                    for r in range(HEADS):
                        pool.wait_ge(w_out_hi_ready, r + 1)
                        pool.tensor_tensor(ut_lo[:, r, :], stage[r % 4][:, :, :].rearrange("p k c -> p (k c)"),
                                           ut_hi[:, r, :].bitcast(F32), ALU.subtract).then_inc(w_out_ready, 1)
                pool.wait_ge(sums_ready, TILES * h + TILES)
                if not known_first(h):
                    pool.wait_ge(rms_ready, h)
                pool.tensor_tensor(sum_eps[:, :], sum_sq[:, :], c["head_eps"][:, :], ALU.add).then_inc(eps_added, 1)
                pool.wait_ge(eps_added, h + 1)
                if not known_first(h):
                    pool.wait_ge(o_gated, h)
                pool.tensor_tensor(inv_rms[:, :], sum_eps[:, :], c["minus_half"][:, :], ALU.pow).then_inc(rms_ready, 1)

            heads(pool, step)

        @block.tensor
        def _(pe):
            def multiply_level(h, level):
                pe.wait_ge(prepared, L * h + level + 1)
                if level >= 2:
                    pe.wait_ge(level_placed, MASKED * h + level - 1)
                elif level == 0 and not known_first(h):
                    pe.wait_ge(last_placed, h)
                elif level == 1 and not known_first(h):
                    pe.wait_ge(self_ready, h)
                rows = P if level < L - 1 else P // 2
                for m in range(TILES):
                    last = pe.matmul(p_level[level % 2][0:rows, m * (P // 2):(m + 1) * (P // 2)],
                                     k_left[level % 2][:, m * P:m * P + rows],
                                     q_right[level % 2][:, m * (P // 2):(m + 1) * (P // 2)], start=True, stop=True)
                last.then_inc(level_done, 1)

            def step(h, b, mixes, projects):
                n, nb = h + 1, 1 - b
                for i in range(USES):
                    if projects:
                        if i in (0, 1) and not known_first(n):
                            pe.wait_ge(gate_ready, 4 * (n - 1) + 3 + i)
                        if i in (2, 3):
                            pe.wait_ge(q_ready, 2 * n + i - 1)
                        if i in (4, 5):
                            pe.wait_ge(f_sigmoid, 2 * n + i - 3)
                        if i in (6, 7):
                            pe.wait_ge(gate_ready, 4 * n + i - 5)
                        if i in (0, 2):
                            pe.wait_ge(w_ready[i // 2], n + 1)
                        if i == 4:
                            pe.wait_ge(w_ready[2], n + 1)
                            pe.wait_ge(w_ready[3], n + 1)
                        if i < 4:
                            cols = slice((i % 2) * HALF, (i % 2 + 1) * HALF)
                            for kt in range(KT):
                                last = matmul_exact(pe, p_proj[i % 2][:, :], w_qf_hi[:, kt, i // 2, :],
                                                    w_qf_lo[:, kt, i // 2, :], ut_hi[:, kt, cols],
                                                    ut_lo[:, kt, cols], kt == 0, kt == KT - 1)
                        else:
                            for t in range(2):
                                tile = 2 * (i - 4) + t
                                rows = slice(tile * P, (tile + 1) * P)
                                for kt in range(KT):
                                    last = matmul_exact(pe, p_proj[i % 2][:, t * 2 * P:(t + 1) * 2 * P],
                                                        ut_hi[:, kt, rows], ut_lo[:, kt, rows],
                                                        w_ig_hi[:, kt, :, :].rearrange("p a b -> p (a b)"),
                                                        w_ig_lo[:, kt, :, :].rearrange("p a b -> p (a b)"),
                                                        kt == 0, kt == KT - 1)
                        last.then_inc(proj_done, 1)
                    if mixes and i < 3:
                        multiply_level(h, 4 + i)
                    if mixes and i == 3:
                        pe.wait_ge(chunk_ready, h + 1)
                        pe.wait_ge(level_placed, MASKED * h + MASKED)
                        for m in range(TILES):
                            last = pe.matmul(p_level[1][:, m:m + 1], qk[:, m * P:(m + 1) * P],
                                             c["ones_col"][:, :], start=True, stop=True)
                        last.then_inc(self_done, 1)
                        if not known_first(h):
                            pe.wait_ge(o_ready, TILES * h)
                        for u in range(2):
                            for m in range(4):
                                last = pe.transpose(p_misc[u][:, m, :],
                                                    k_chunk[:, (4 * u + m) * P:(4 * u + m + 1) * P],
                                                    c["ident"][:, :])
                            last.then_inc(k_turned_done, 1)
                    if projects and i >= 4:
                        multiply_level(n, i - 4)
                    if mixes and i == 4:
                        if not known_first(h):
                            pe.wait_ge(out_ready, 2 * h)
                        for u in range(2):
                            pe.wait_ge(k_turned_ready, 2 * h + u + 1)
                            for m in range(4 * u, min(4 * u + 4, TILES - 1)):
                                last = pe.matmul(p_misc[2 + u][:, m % 4, :], k_turned[:, m, :], value[b][:, m, :],
                                                 start=True, stop=True)
                            last.then_inc(update_done, 1)
                    if mixes and i == 5:
                        pe.wait_ge(last_placed, h + 1)
                        for u in range(2):
                            for m in range(4 * u, 4 * u + 4):
                                dst = p_misc[u][:, m % 4, :]
                                last = pe.matmul(dst, scores[b][:, m, :], value[b][:, m, :], start=True,
                                                 stop=(m == 0))
                                if m > 0:
                                    pe.wait_ge(state_ready, (TILES - 1) * h + m)
                                    last = pe.matmul(dst, q_chunk[:, m * P:(m + 1) * P], state[:, m, :],
                                                     start=False, stop=True)
                            last.then_inc(o_done, 1)
                    if mixes and i == 7:
                        pe.wait_ge(o_gated, h + 1)
                        for u in range(2):
                            pe.wait_ge(state_ready, (TILES - 1) * (h + 1))
                            for m in range(4):
                                last = pe.transpose(p_misc[2 + u][:, m, :], o[:, 4 * u + m, :], c["ident"][:, :])
                            last.then_inc(o_turned, 1)

            heads(pe, step)


_INS = ["x", "sb_norm", "sb_w_in", "sb_q_gain", "sb_k_gain", "sb_w_out",
        "hg_norm", "hg_w_in", "hg_o_gain", "hg_w_out", "hg_lb_logits"]


def kernel(**inputs):
    import numpy as _np
    import concourse.bacc as _bacc
    from concourse import mybir as _mybir
    from concourse.bass_utils import run_bass_kernel_spmd as _run

    nc = _bacc.Bacc("TRN2", target_bir_lowering=False, num_devices=1, dynamic_dma_scratch_size=1024)
    arrays, args = {}, []
    for name in _INS:
        a = _np.ascontiguousarray(inputs[name])
        arrays[f"in_{name}_dram"] = a
        args.append(nc.dram_tensor(f"in_{name}_dram", a.shape, _mybir.dt.from_np(a.dtype), kind="ExternalInput").ap())
    result = nc.dram_tensor("out_0_dram", inputs["x"].shape, _mybir.dt.float32, kind="ExternalOutput").ap()
    build_trunk(nc, *args, result)
    r = _run(nc, [arrays], core_ids=[0])
    return r.results[0]["out_0_dram"]
```

```python
from contextlib import ExitStack

import concourse.bass as bass
from concourse import mybir

ALU = mybir.AluOpType
ACT = mybir.ActivationFunctionType
F32 = mybir.dt.float32
F32R = mybir.dt.float32r
BF16 = mybir.dt.bfloat16
I32 = mybir.dt.int32

P = 128
D_MODEL = 1024
SEQ = 1024
KT = D_MODEL // P
TILES = SEQ // P
HEADS = D_MODEL // P
HALF = 512
RMS_EPS = 1e-6
NEG = -1e30
LEVELS = [1, 2, 4, 8, 16, 32, 64]


def matmul_exact(pe, out, w_hi, w_lo, m_hi, m_lo, start, stop):
    pe.matmul(out, w_hi, m_hi, start=start, stop=False, skip_group_check=True)
    pe.matmul(out, w_hi, m_lo, start=False, stop=False, skip_group_check=True)
    return pe.matmul(out, w_lo, m_hi, start=False, stop=stop, skip_group_check=True)


def build_trunk(nc, x, sb_norm, sb_w_in, sb_q_gain, sb_k_gain, sb_w_out,
                hg_norm, hg_w_in, hg_o_gain, hg_w_out, hg_lb_logits, out):
    x = x.rearrange("b s d -> (b s) d")
    out = out.rearrange("b s d -> (b s) d")
    mixed = nc.dram_tensor("mixed_scratch", (2, HEADS, P, SEQ), F32).ap()
    h1 = nc.dram_tensor("h1_scratch", (SEQ, D_MODEL), F32).ap()

    with ExitStack() as ctx:
        def sb(name, shape, dt=F32, into=ctx):
            return into.enter_context(nc.sbuf_tensor(name, shape, dt))

        consts = {
            "ident": sb("ident", [P, P]),
            "ident_bf": sb("ident_bf", [P, P], BF16),
            "causal_neg": sb("causal_neg", [P, P], BF16),
            "ones_col": sb("ones_col", [P, 1]),
            "minus_half": sb("minus_half", [P, TILES]),
            "minus_one": sb("minus_one", [P, 1]),
            "head_eps": sb("head_eps", [P, TILES]),
            "level_mask": sb("level_mask", [P, len(LEVELS), P // 2]),
            "q_gain": sb("q_gain", [P, 1]),
            "k_gain": sb("k_gain", [P, 1]),
            "qk_gain": sb("qk_gain", [P, 1]),
            "o_gain": sb("o_gain", [P, 1]),
            "o_scale": sb("o_scale", [P, 1]),
            "logits": sb("logits", [P, 2, HEADS]),
            "logit_gap": sb("logit_gap", [P, HEADS]),
            "lower": sb("lower", [P, HEADS]),
            "one_minus_lower": sb("one_minus_lower", [P, HEADS]),
        }
        stage = [sb(f"stage{i}", [P, KT, P]) for i in range(4)]
        m_in = [sb(f"m_in{i}", [P, HEADS, P]) for i in range(2)]

        def link(tag):
            def sem(name):
                return ctx.enter_context(nc.semaphore(f"{tag}_{name}"))
            return {"w_loaded": [sem(f"w_loaded{i}") for i in range(4)],
                    "stored": sem("mixed_stored"),
                    "m_loaded": [sem(f"m_loaded{i}") for i in range(2)],
                    "m_hi_ready": sem("m_hi_ready"),
                    "m_ready": sem("m_ready")}

        links = [link("l0"), link("l1")]
        p_proj = [ctx.enter_context(nc.psum_tensor(f"p_proj{i}", [P, 4, P], F32)) for i in range(2)]
        hg_w = {name: [ctx.enter_context(nc.semaphore(f"g_{name}{i}")) for i in range(4)]
                for name in ("w_loaded", "w_hi_ready", "w_ready")}

        with ExitStack() as first_layer:
            ut_hi = sb("ut_hi", [P, KT, SEQ], F32R, first_layer)
            ut_lo = sb("ut_lo", [P, KT, SEQ], F32R, first_layer)
            w_qkv_hi = sb("w_qkv_hi", [P, KT, 3, P], F32R, first_layer)
            w_qkv_lo = sb("w_qkv_lo", [P, KT, 3, P], F32R, first_layer)
            small_inputs = {"q_gain": sb_q_gain, "k_gain": sb_k_gain, "o_gain": hg_o_gain, "logits": hg_lb_logits}
            build_attention(nc, consts, small_inputs, x, sb_norm, stage, m_in, links[0], sb_w_in, sb_w_out,
                            ut_hi, ut_lo, w_qkv_hi, w_qkv_lo, p_proj, mixed[0])
            next_hi = ctx.enter_context(nc.sbuf_tensor("next_hi", [P, KT, SEQ], F32R, side="right"))
            next_lo = ctx.enter_context(nc.sbuf_tensor("next_lo", [P, KT, SEQ], F32R, side="right"))
            w_qf_hi = ctx.enter_context(nc.sbuf_tensor("w_qf_hi", [P, KT, 2, P], F32R, side="right"))
            w_qf_lo = ctx.enter_context(nc.sbuf_tensor("w_qf_lo", [P, KT, 2, P], F32R, side="right"))
            build_output_projection(nc, "l0", consts, m_in, links[0], mixed[0], ut_hi, ut_lo, x, h1,
                                    w_qkv_hi, w_qkv_lo, p_proj,
                                    hg_norm, next_hi, next_lo, (stage, hg_w_in, hg_w, w_qf_hi, w_qf_lo))
        build_hgrn(nc, consts, stage, m_in, links[1], hg_w, hg_w_in, hg_w_out, next_hi, next_lo,
                   w_qf_hi, w_qf_lo, p_proj, mixed[1])
        build_output_projection(nc, "l1", consts, m_in, links[1], mixed[1], next_hi, next_lo, h1, out,
                                w_qf_hi, w_qf_lo, p_proj,
                                None, None, None, None)


def split_mixed_hi(act, m_in, m_hi, link, i):
    act.wait_ge(link["m_loaded"][i], 16)
    act.activation(m_hi[:, 0:HEADS - 1, i, :], m_in[i][:, 0:HEADS - 1, :], ACT.Copy).then_inc(link["m_hi_ready"], 1)


def split_mixed_lo(dve, m_in, m_hi, m_lo, link, i):
    dve.wait_ge(link["m_hi_ready"], i + 1)
    dve.tensor_tensor(m_lo[:, 0:HEADS - 1, i, :], m_in[i][:, 0:HEADS - 1, :],
                      m_hi[:, 0:HEADS - 1, i, :].bitcast(F32), ALU.subtract).then_inc(link["m_ready"], 1)


def start_output_tile(pe, p_proj, m_hi, m_lo, w_hi, w_lo, m_ready, w_ready, rows):
    pe.wait_ge(m_ready, 1)
    for h in rows:
        pe.wait_ge(w_ready, h + 1)
        for half in range(2):
            cols = slice(half * HALF, (half + 1) * HALF)
            matmul_exact(pe, p_proj[half][:, :, :].rearrange("p a b -> p (a b)"), m_hi[:, h, 0, :], m_lo[:, h, 0, :],
                         w_hi[:, h, cols], w_lo[:, h, cols], h == 0, False)


def load_columns(sp, stage, w_in, h, p):
    columns = w_in[0, :, bass.ds(p * D_MODEL + h * P, P)]
    return sp.dma_start(stage[p][:, :, :], columns.rearrange("(k p) c -> p k c", p=P))


def load_w_out(sp, stage, w_out, r):
    return sp.dma_start(stage[r % 4][:, :, :].rearrange("p k c -> p (k c)"), w_out[0, r * P:(r + 1) * P, :])


def load_mixed(sp, m_in, mixed, i, heads):
    return sp.dma_start(m_in[i % 2][:, heads, :],
                        mixed[heads, :, i * P:(i + 1) * P].rearrange("h p t -> p h t"))


def build_attention(nc, c, small_inputs, x, gain, stage, m_in, link, w_in, w_out, ut_hi, ut_lo,
                    w_qkv_hi, w_qkv_lo, p_proj, mixed):
    Z_UNITS = [1, 1, 1, 1, 2, 2, 2, 2]
    ENDS = [sum(Z_UNITS[:i + 1]) for i in range(TILES)]
    UNITS = ENDS[-1]
    NAT, GATE = TILES, 2
    USES = NAT + GATE
    PAIRS = TILES // 2
    W_OUT_AT = {0: [0, 1], 1: [2, 3], 3: [4], 4: [5], 5: [6], 6: [7]}
    M_AT = [4, 6]
    START_AT = {6: [0], 7: [1], 8: [2, 3, 4], 9: [5, 6]}

    with ExitStack() as ctx:
        def sb(name, shape, dt=F32):
            return ctx.enter_context(nc.sbuf_tensor("a_" + name, shape, dt))

        def psum(name, shape):
            return ctx.enter_context(nc.psum_tensor("a_" + name, shape, F32))

        def sem(name):
            return ctx.enter_context(nc.semaphore("a_" + name))

        w_gate_hi = sb("w_gate_hi", [P, KT, P], F32R)
        w_gate_lo = sb("w_gate_lo", [P, KT, P], F32R)
        raw = [sb(f"raw{i}", [P, 3, P]) for i in range(4)]
        squares = [sb(f"squares{i}", [P, P]) for i in range(2)]
        sum_sq = [sb(f"sum_sq{i}", [P, 2]) for i in range(2)]
        mean_sq = [sb(f"mean_sq{i}", [P, 2]) for i in range(2)]
        inv_rms = [[sb(f"inv_rms{b}_{i}", [P, 3]) for i in range(TILES)] for b in range(2)]
        k_scaled = [sb(f"k_scaled{i}", [P, P]) for i in range(4)]
        qt_hi = [sb(f"qt_hi{b}", [P, SEQ], F32R) for b in range(2)]
        qt_lo = [sb(f"qt_lo{b}", [P, SEQ], F32R) for b in range(2)]
        kt_hi = [sb(f"kt_hi{b}", [P, SEQ], F32R) for b in range(2)]
        kt_lo = [sb(f"kt_lo{b}", [P, SEQ], F32R) for b in range(2)]
        v_hi = [sb(f"v_hi{b}", [P, TILES, P], F32R) for b in range(2)]
        v_lo = [sb(f"v_lo{b}", [P, TILES, P], F32R) for b in range(2)]
        gated = [sb(f"gated{b}", [P, SEQ]) for b in range(2)]
        beta = [sb(f"beta{i}", [P, SEQ]) for i in range(2)]
        skip = [sb(f"skip{i}", [P, SEQ + 1]) for i in range(2)]
        wt_hi = sb("wt_hi", [P, TILES, 2, P], F32R)
        wt_lo = sb("wt_lo", [P, TILES, 2, P], F32R)

        x_tile = beta
        normed = skip
        x_squares = m_in[0][:, :, :].rearrange("p a b -> p (a b)")
        gain_rows = m_in[1][:, :, :].rearrange("p a b -> p (a b)")
        x_sum_sq = [sb(f"x_sum_sq{i}", [P, 1]) for i in range(2)]
        x_mean_sq = [sb(f"x_mean_sq{i}", [P, 1]) for i in range(2)]
        x_inv_rms = [sb(f"x_inv_rms{i}", [P, 1]) for i in range(2)]

        p_wide = [bank[:, :, :].rearrange("p a b -> p (a b)") for bank in p_proj]
        p_z = [psum(f"p_z{i}", [P, HALF]) for i in range(3)]
        p_turn = [psum(f"p_turn{i}", [P, 4, P]) for i in range(2)]
        p_o = psum("p_o", [P, 2, P])

        w_loaded = [sem(f"w_loaded{p}") for p in range(4)]
        w_out_hi_ready = sem("w_out_hi_ready")
        w_out_ready = sem("w_out_ready")
        w_hi_ready = [sem(f"w_hi_ready{p}") for p in range(4)]
        w_ready = [sem(f"w_ready{p}") for p in range(4)]
        proj_done = sem("proj_done")
        raw_ready = sem("raw_ready")
        v_hi_ready = sem("v_hi_ready")
        v_ready = sem("v_ready")
        sums_ready = sem("sums_ready")
        mean_ready = sem("mean_ready")
        rms_ready = sem("rms_ready")
        k_ready = sem("k_ready")
        qk_turned = sem("qk_turned")
        qk_hi_ready = sem("qk_hi_ready")
        qk_ready = sem("qk_ready")
        gate_sigmoid = sem("gate_sigmoid")
        gate_ready = sem("gate_ready")
        z_done = sem("z_done")
        sigmoids_ready = sem("sigmoids_ready")
        scan_done = sem("scan_done")
        weights_ready = sem("weights_ready")
        weights_turned = sem("weights_turned")
        wt_hi_ready = sem("wt_hi_ready")
        wt_ready = sem("wt_ready")
        o_done = sem("o_done")
        o_gated = sem("o_gated")
        o_stored = link["stored"]
        skip_set = sem("skip_set")
        pool_made = sem("pool_made")
        dve_made = sem("dve_made")
        act_made = sem("act_made")
        gain_loaded = sem("gain_loaded")
        qk_gains_loaded = sem("qk_gains_loaded")
        small_loaded = sem("small_loaded")
        x_loaded = [sem(f"x_loaded{i}") for i in range(2)]
        x_sum_ready = sem("x_sum_ready")
        x_mean_ready = sem("x_mean_ready")
        x_rms_ready = sem("x_rms_ready")
        normed_ready = sem("normed_ready")
        x_turned = sem("x_turned")
        ut_hi_ready = sem("ut_hi_ready")
        ut_ready = sem("ut_ready")

        turn_of, turn_alone = {}, {}
        for i in range(USES):
            if i >= 3 and i % 2 == 1:
                turn_of[("qk", (i - 3) // 2)] = len(turn_of)
                turn_alone[("qk", (i - 3) // 2)] = len(turn_alone)
            if 1 <= i <= TILES:
                for u in range(Z_UNITS[i - 1]):
                    turn_of[("w", ENDS[i - 1] - Z_UNITS[i - 1] + u)] = len(turn_of)

        def w_bank(unit, projects):
            return p_turn[(turn_of[("w", unit)] if projects else unit) % 2]

        def heads(eng, step):
            step(-1, 1, False, True)
            step(0, 0, True, True)
            with eng.Fori(0, (HEADS - 4) // 2) as pair:
                step(pair * 2 + 1, 1, True, True)
                step(pair * 2 + 2, 0, True, True)
            step(HEADS - 3, 1, True, True)
            step(HEADS - 2, 0, True, True)
            step(HEADS - 1, 1, True, False)

        def known_first(h):
            return isinstance(h, int) and h <= 0

        block = ctx.enter_context(nc.Block())

        @block.sync
        def _(sp):
            def load_out(r):
                if r < 4:
                    sp.wait_ge(w_ready[r], HEADS)
                else:
                    sp.wait_ge(w_out_ready, r - 3)
                load_w_out(sp, stage, w_out, r).then_inc(link["w_loaded"][r % 4], 16)

            def load_mixed_early(i):
                sp.wait_ge(o_stored, 16 * (HEADS - 1))
                load_mixed(sp, m_in, mixed, i, slice(0, HEADS - 1)).then_inc(link["m_loaded"][i], 16)

            def load(h, p):
                if not known_first(h):
                    sp.wait_ge(w_ready[p], h)
                load_columns(sp, stage, w_in, h, p).then_inc(w_loaded[p], 16)

            def store(h, b):
                sp.wait_ge(o_gated, PAIRS * h + PAIRS)
                sp.dma_start(mixed[bass.ds(h, 1), :, :].rearrange("o p s -> p (o s)"),
                             gated[b][:, :]).then_inc(o_stored, 16)

            def load_x(i):
                if i >= 2:
                    sp.wait_ge(normed_ready, i - 1)
                sp.dma_start(x_tile[i % 2][:, :], x[i * P:(i + 1) * P, :]).then_inc(x_loaded[i % 2], 16)

            load_x(0)
            sp.dma_start(gain_rows, gain[0:1, :].to_broadcast([P, D_MODEL])).then_inc(gain_loaded, 16)
            for p in range(3):
                load(0, p)
            load_x(1)
            for name in ("q_gain", "k_gain"):
                sp.dma_start(c[name][:, :], small_inputs[name].rearrange("a d -> d a"),
                             allow_slow_non_contiguous=True).then_inc(qk_gains_loaded, 16)
            load_x(2)
            load(0, 3)
            load_x(3)
            for p in range(3):
                load(1, p)
            for i in range(4, TILES):
                load_x(i)
            load(1, 3)
            sp.dma_start(c["o_gain"][:, :], small_inputs["o_gain"].rearrange("a d -> d a"),
                         allow_slow_non_contiguous=True).then_inc(small_loaded, 16)
            for layer in range(2):
                sp.dma_start(c["logits"][:, layer, :],
                             small_inputs["logits"][layer].rearrange("(h d) -> d h", d=P),
                             allow_slow_non_contiguous=True).then_inc(small_loaded, 16)
            for p in range(4):
                load(2, p)
            store(0, 0)
            for p in range(4):
                load(3, p)
            with sp.Fori(0, 2) as pair:
                for b in (1, 0):
                    store(pair * 2 + 2 - b, b)
                    for p in range(4):
                        load(pair * 2 + 5 - b, p)
            store(HEADS - 3, 1)
            for r in range(4):
                load_out(r)
            store(HEADS - 2, 0)
            for i in range(2):
                load_mixed_early(i)
            load_out(4)
            load_out(5)
            load_out(6)
            load_out(7)
            store(HEADS - 1, 1)

        @block.scalar
        def _(act):
            def split_hi(h, p):
                if not known_first(h):
                    act.wait_ge(proj_done, USES * (h - 1) + (NAT if p < 3 else USES))
                act.wait_ge(w_loaded[p], 16 * h + 16)
                dst = w_qkv_hi[:, :, p, :] if p < 3 else w_gate_hi[:, :, :]
                act.activation(dst, stage[p][:, :, :], ACT.Copy).then_inc(w_hi_ready[p], 1)

            def square_x(i):
                act.wait_ge(x_loaded[i % 2], 16 * (i // 2 + 1))
                if i >= 1:
                    act.wait_ge(x_sum_ready, i)
                if i >= 2:
                    act.wait_ge(x_mean_ready, i - 1)
                act.activation(x_squares, x_tile[i % 2][:, :], ACT.Square,
                               accum_out=x_sum_sq[i % 2][:, :]).then_inc(x_sum_ready, 1)

            def stream_hi(i):
                for half in range(2):
                    use = 2 * i + half
                    act.wait_ge(x_turned, use + 1)
                    act.activation(ut_hi[:, 4 * half:4 * half + 4, i * P:(i + 1) * P],
                                   p_z[use % 3][:, :].rearrange("p (a b) -> p a b", a=4),
                                   ACT.Copy).then_inc(ut_hi_ready, 1)

            def step(h, b, attends, projects):
                n, nb = h + 1, 1 - b
                for i in range(USES):
                    if known_first(h) and attends and i == 0:
                        act.wait_ge(normed_ready, TILES)
                        act.wait_ge(x_turned, 2 * TILES)
                    if known_first(n) and i + 1 < TILES:
                        stream_hi(i + 1)
                    if known_first(n) and i + 2 < TILES:
                        square_x(i + 2)
                    if attends and i < TILES:
                        for u in range(Z_UNITS[i]):
                            width = min(HALF, (i + 1) * P - u * HALF)
                            unit = ENDS[i] - Z_UNITS[i] + u
                            act.wait_ge(z_done, UNITS * h + unit + 1)
                            if u == 0:
                                act.wait_ge(rms_ready, TILES * h + i + 1)
                                if i >= 2:
                                    act.wait_ge(weights_turned, UNITS * h + ENDS[i - 2])
                                elif not known_first(h):
                                    act.wait_ge(weights_turned, UNITS * (h - 1) + ENDS[i + 6])
                            cols = slice(u * HALF, u * HALF + width)
                            act.activation(skip[i % 2][:, cols], p_z[unit % 3][:, 0:width], ACT.Sigmoid,
                                           scale=inv_rms[b][i][:, 2:3])
                            act.activation(beta[i % 2][:, cols], p_z[unit % 3][:, 0:width], ACT.Sigmoid,
                                           scale=inv_rms[b][i][:, 0:1]).then_inc(sigmoids_ready, 1)
                    if projects and i >= 3 and i % 2 == 1:
                        m = (i - 3) // 2
                        act.wait_ge(qk_turned, PAIRS * n + m + 1)
                        if known_first(n) and m == 0:
                            act.wait_ge(dve_made, 1)
                        if not (isinstance(n, int) and n < 2):
                            act.wait_ge(z_done, UNITS * (n - 1))
                        turn = (turn_of if attends else turn_alone)[("qk", m)] % 2
                        cols = slice(2 * m * P, (2 * m + 2) * P)
                        act.activation(qt_hi[nb][:, cols], p_turn[turn][:, 0:2, :].rearrange("p a b -> p (a b)"),
                                       ACT.Copy)
                        act.activation(kt_hi[nb][:, cols], p_turn[turn][:, 2:4, :].rearrange("p a b -> p (a b)"),
                                       ACT.Copy, scale=c["qk_gain"][:, 0:1]).then_inc(qk_hi_ready, 1)
                    if projects and i < NAT:
                        act.wait_ge(proj_done, USES * n + i + 1)
                        if i >= 4 or not known_first(n):
                            act.wait_ge(qk_turned, PAIRS * n + (i - 4) // 2 + 1)
                            act.wait_ge(v_ready, NAT * n + i - 3)
                        act.activation(raw[i % 4][:, :, :],
                                       p_proj[i % 2][:, 0:3, :],
                                       ACT.Copy).then_inc(raw_ready, 1)
                    if projects and i == 3:
                        split_hi(n, 3)
                    if projects and i == 8 and not (isinstance(n, int) and n == HEADS - 1):
                        for p in range(3):
                            split_hi(n + 1, p)
                    if attends and 1 <= i <= TILES:
                        j = i - 1
                        for u in range(Z_UNITS[j]):
                            unit = ENDS[j] - Z_UNITS[j] + u
                            act.wait_ge(weights_turned, UNITS * h + unit + 1)
                            if not (known_first(h) and j < 2):
                                act.wait_ge(o_done, PAIRS * h + j // 2)
                            nb_blocks = min(4, j + 1 - 4 * u)
                            act.activation(wt_hi[:, 4 * u:4 * u + nb_blocks, j % 2, :],
                                           w_bank(unit, projects)[:, 0:nb_blocks, :], ACT.Copy).then_inc(wt_hi_ready, 1)
                    if known_first(n) and i == NAT:
                        act.wait_ge(dve_made, 3)
                        act.activation(c["lower"][:, :], c["logit_gap"][:, :], ACT.Sigmoid).then_inc(act_made, 1)
                        act.activation(c["one_minus_lower"][:, :], c["logit_gap"][:, :], ACT.Sigmoid,
                                       scale=-1.0).then_inc(act_made, 1)
                    if projects and i >= NAT:
                        half = i - NAT
                        act.wait_ge(proj_done, USES * n + i + 1)
                        if not (isinstance(n, int) and n < 2):
                            act.wait_ge(o_stored, 16 * (n - 1))
                        act.activation(gated[nb][:, half * HALF:(half + 1) * HALF], p_wide[i % 2],
                                       ACT.Sigmoid).then_inc(gate_sigmoid, 1)
                    if not projects and i in M_AT:
                        split_mixed_hi(act, m_in, w_qkv_hi, link, M_AT.index(i))

            square_x(0)
            split_hi(0, 0)
            stream_hi(0)
            split_hi(0, 1)
            split_hi(0, 2)
            square_x(1)
            heads(act, step)

        @block.vector
        def _(dve):
            def split_w_out_hi(r):
                dve.wait_ge(proj_done, USES * HEADS)
                dve.wait_ge(link["w_loaded"][r % 4], 16 * (r // 4) + 16)
                dve.tensor_copy(ut_hi[:, r, :], stage[r % 4][:, :, :].rearrange("p k c -> p (k c)")
                                ).then_inc(w_out_hi_ready, 1)

            def split_lo(h, p):
                if not known_first(h):
                    dve.wait_ge(proj_done, USES * (h - 1) + (NAT if p < 3 else USES))
                dve.wait_ge(w_hi_ready[p], h + 1)
                hi = w_qkv_hi[:, :, p, :] if p < 3 else w_gate_hi[:, :, :]
                lo = w_qkv_lo[:, :, p, :] if p < 3 else w_gate_lo[:, :, :]
                dve.tensor_tensor(lo, stage[p][:, :, :], hi.bitcast(F32), ALU.subtract).then_inc(w_ready[p], 1)

            def norm_x(i):
                if i == 0:
                    dve.wait_ge(gain_loaded, 16)
                dve.wait_ge(x_rms_ready, i + 1)
                dve.wait_ge(x_loaded[i % 2], 16 * (i // 2 + 1))
                if i >= 2:
                    dve.wait_ge(x_turned, 2 * (i - 1))
                dve.scalar_tensor_tensor(out=normed[i % 2][:, 0:D_MODEL], in0=x_tile[i % 2][:, :],
                                         scalar=x_inv_rms[i % 2][:, 0:1], in1=gain_rows,
                                         op0=ALU.mult, op1=ALU.mult).then_inc(normed_ready, 1)

            def stream_lo(i):
                for half in range(2):
                    use = 2 * i + half
                    dve.wait_ge(ut_hi_ready, use + 1)
                    part = (slice(None), slice(4 * half, 4 * half + 4), slice(i * P, (i + 1) * P))
                    dve.tensor_tensor(ut_lo[part], p_z[use % 3][:, :].rearrange("p (a b) -> p a b", a=4),
                                      ut_hi[part].bitcast(F32), ALU.subtract).then_inc(ut_ready, 1)

            def gate_outputs(h, b, i):
                g = (i - 3) // 2
                dve.wait_ge(o_done, PAIRS * h + g + 1)
                dve.wait_ge(gate_ready, GATE * h + GATE)
                cols = slice(2 * g * P, (2 * g + 2) * P)
                dve.tensor_tensor(gated[b][:, cols], gated[b][:, cols],
                                  p_o[:, :, :].rearrange("p a b -> p (a b)"),
                                  ALU.mult).then_inc(o_gated, 1)

            def step(h, b, attends, projects):
                n, nb = h + 1, 1 - b
                for i in range(USES):
                    if known_first(n) and i + 1 < TILES:
                        stream_lo(i + 1)
                    if known_first(n) and i + 2 < TILES:
                        norm_x(i + 2)
                    if known_first(n) and i == 1:
                        dve.wait_ge(qk_gains_loaded, 16 * 2)
                        dve.scalar_tensor_tensor(out=c["qk_gain"][:, :], in0=c["q_gain"][:, :],
                                                 scalar=float(P) ** 0.5, in1=c["k_gain"][:, :],
                                                 op0=ALU.mult, op1=ALU.mult).then_inc(dve_made, 1)
                        dve.wait_ge(pool_made, 4)
                        dve.tensor_copy(c["ident_bf"][:, :], c["ident"][:, :]).then_inc(dve_made, 1)
                    if known_first(n) and i == NAT:
                        dve.wait_ge(small_loaded, 16 * 3)
                        dve.tensor_scalar(c["o_scale"][:, :], c["o_gain"][:, :], float(P) ** 0.5, None,
                                          ALU.mult)
                        dve.tensor_tensor(c["logit_gap"][:, :], c["logits"][:, 1, :], c["logits"][:, 0, :],
                                          ALU.subtract).then_inc(dve_made, 1)
                    if attends and i < TILES:
                        width = (i + 1) * P
                        if known_first(h) and i == 0:
                            dve.wait_ge(skip_set, 2)
                        dve.wait_ge(sigmoids_ready, UNITS * h + ENDS[i])
                        chain = skip[i % 2][:, 0:width][:, ::-1]
                        dve.tensor_tensor_scan(chain, chain, chain, 1.0, ALU.mult, ALU.min).then_inc(scan_done, 1)
                        dve.wait_ge(scan_done, TILES * h + i + 1)
                        dve.tensor_tensor(beta[i % 2][:, 0:width], beta[i % 2][:, 0:width],
                                          skip[i % 2][:, 1:width + 1], ALU.mult).then_inc(weights_ready, 1)
                    if projects and i >= 3 and i % 2 == 1:
                        m = (i - 3) // 2
                        dve.wait_ge(qk_hi_ready, PAIRS * n + m + 1)
                        if not (isinstance(n, int) and n < 2):
                            dve.wait_ge(z_done, UNITS * (n - 1))
                        turn = (turn_of if attends else turn_alone)[("qk", m)] % 2
                        cols = slice(2 * m * P, (2 * m + 2) * P)
                        dve.tensor_tensor(qt_lo[nb][:, cols], p_turn[turn][:, 0:2, :].rearrange("p a b -> p (a b)"),
                                          qt_hi[nb][:, cols].bitcast(F32), ALU.subtract)
                        dve.scalar_tensor_tensor(out=kt_lo[nb][:, cols],
                                                 in0=p_turn[turn][:, 2:4, :].rearrange("p a b -> p (a b)"),
                                                 scalar=c["qk_gain"][:, 0:1], in1=kt_hi[nb][:, cols].bitcast(F32),
                                                 op0=ALU.mult, op1=ALU.subtract).then_inc(qk_ready, 1)
                    if projects and i < NAT:
                        dve.wait_ge(raw_ready, NAT * n + i + 1)
                        if i >= 2 or not known_first(n):
                            dve.wait_ge(mean_ready, NAT * n + i - 1)
                        if i >= 1 or not known_first(n):
                            dve.wait_ge(sums_ready, 2 * (NAT * n + i))
                        for part in range(2):
                            dve.tensor_tensor_reduce(squares[part][:, :], raw[i % 4][:, part, :],
                                                     raw[i % 4][:, part, :], 1.0, 0.0, ALU.mult, ALU.add,
                                                     sum_sq[i % 2][:, part:part + 1]).then_inc(sums_ready, 1)
                        if not (isinstance(n, int) and n < 2):
                            dve.wait_ge(o_done, PAIRS * (n - 1))
                        dve.tensor_copy(v_hi[nb][:, i, :], raw[i % 4][:, 2, :]).then_inc(v_hi_ready, 1)
                        dve.wait_ge(v_hi_ready, NAT * n + i + 1)
                        dve.tensor_tensor(v_lo[nb][:, i, :], raw[i % 4][:, 2, :], v_hi[nb][:, i, :].bitcast(F32),
                                          ALU.subtract).then_inc(v_ready, 1)
                    if projects and i == 3:
                        split_lo(n, 3)
                    if projects and i == 8 and not (isinstance(n, int) and n == HEADS - 1):
                        for p in range(3):
                            split_lo(n + 1, p)
                    if not projects:
                        for r in W_OUT_AT.get(i, []):
                            split_w_out_hi(r)
                    if attends and i >= 3 and i % 2 == 1 and projects:
                        gate_outputs(h, b, i)
                    if attends and 1 <= i <= TILES:
                        j = i - 1
                        for u in range(Z_UNITS[j]):
                            unit = ENDS[j] - Z_UNITS[j] + u
                            dve.wait_ge(wt_hi_ready, UNITS * h + unit + 1)
                            if not (known_first(h) and j < 2):
                                dve.wait_ge(o_done, PAIRS * h + j // 2)
                            nb_blocks = min(4, j + 1 - 4 * u)
                            dve.tensor_tensor(wt_lo[:, 4 * u:4 * u + nb_blocks, j % 2, :],
                                              w_bank(unit, projects)[:, 0:nb_blocks, :],
                                              wt_hi[:, 4 * u:4 * u + nb_blocks, j % 2, :].bitcast(F32),
                                              ALU.subtract).then_inc(wt_ready, 1)
                    if attends and i >= 3 and i % 2 == 1 and not projects:
                        gate_outputs(h, b, i)
                    if projects and i >= NAT:
                        half = i - NAT
                        cols = slice(half * HALF, (half + 1) * HALF)
                        dve.wait_ge(gate_sigmoid, GATE * n + half + 1)
                        dve.tensor_tensor(gated[nb][:, cols], gated[nb][:, cols], p_wide[i % 2],
                                          ALU.mult).then_inc(gate_ready, 1)
                    if not projects and i in M_AT:
                        split_mixed_lo(dve, m_in, w_qkv_hi, w_qkv_lo, link, M_AT.index(i))

            norm_x(0)
            split_lo(0, 0)
            stream_lo(0)
            split_lo(0, 1)
            split_lo(0, 2)
            norm_x(1)
            heads(dve, step)

        @block.gpsimd
        def _(pool):
            def rms_of_x(i):
                pool.wait_ge(x_sum_ready, i + 1)
                pool.tensor_scalar(x_mean_sq[i % 2][:, :], x_sum_sq[i % 2][:, :], 1.0 / D_MODEL, RMS_EPS,
                                   ALU.mult, ALU.add).then_inc(x_mean_ready, 1)
                pool.wait_ge(x_mean_ready, i + 1)
                if i >= 2:
                    pool.wait_ge(normed_ready, i - 1)
                pool.tensor_tensor(x_inv_rms[i % 2][:, :], x_mean_sq[i % 2][:, :], c["minus_half"][:, 0:1],
                                   ALU.pow).then_inc(x_rms_ready, 1)

            pool.memset(c["minus_half"][:, :], -0.5).then_inc(pool_made, 1)
            pool.memset(c["ident"][:, :], 0.0).then_inc(pool_made, 1)
            pool.memset(c["causal_neg"][:, :], 0.0).then_inc(pool_made, 1)
            pool.wait_ge(pool_made, 3)
            pool.affine_select(out=c["ident"][:, :], in_=c["ident"][:, :], compare_op=ALU.not_equal, fill=1.0,
                               base=0, pattern=[[-1, P]], channel_multiplier=1).then_inc(pool_made, 1)
            rms_of_x(0)
            pool.affine_select(out=c["causal_neg"][:, :], in_=c["causal_neg"][:, :], compare_op=ALU.is_gt, fill=NEG,
                               base=0, pattern=[[-1, P]], channel_multiplier=1).then_inc(pool_made, 1)
            pool.memset(c["minus_one"][:, :], -1.0)
            pool.memset(c["head_eps"][:, :], RMS_EPS * P)
            pool.memset(c["ones_col"][:, :], 1.0).then_inc(pool_made, 1)
            for i in range(2):
                pool.memset(skip[i][:, SEQ:SEQ + 1], 1.0).then_inc(skip_set, 1)
            rms_of_x(1)

            def step(h, b, attends, projects):
                n, nb = h + 1, 1 - b
                if not projects:
                    for r in range(HEADS):
                        pool.wait_ge(w_out_hi_ready, r + 1)
                        pool.tensor_tensor(ut_lo[:, r, :], stage[r % 4][:, :, :].rearrange("p k c -> p (k c)"),
                                           ut_hi[:, r, :].bitcast(F32), ALU.subtract).then_inc(w_out_ready, 1)
                    return
                for i in range(NAT):
                    if known_first(n) and i + 2 < TILES:
                        rms_of_x(i + 2)
                    rms = inv_rms[nb][i]
                    pool.wait_ge(sums_ready, 2 * (NAT * n + i) + 2)
                    if i >= 2 or not known_first(n):
                        pool.wait_ge(rms_ready, NAT * n + i - 1)
                    pool.tensor_tensor(mean_sq[i % 2][:, :], sum_sq[i % 2][:, :], c["head_eps"][:, 0:2],
                                       ALU.add).then_inc(mean_ready, 1)
                    pool.wait_ge(mean_ready, NAT * n + i + 1)
                    if not (isinstance(n, int) and n < 2):
                        pool.wait_ge(sigmoids_ready, UNITS * (n - 1))
                    pool.tensor_tensor(rms[:, 0:2], mean_sq[i % 2][:, :], c["minus_half"][:, 0:2],
                                       ALU.pow).then_inc(k_ready, 1)
                    pool.wait_ge(k_ready, 2 * (NAT * n + i) + 1)
                    pool.tensor_tensor(rms[:, 2:3], rms[:, 0:1], c["minus_one"][:, :], ALU.mult).then_inc(rms_ready, 1)
                    pool.wait_ge(raw_ready, NAT * n + i + 1)
                    if i >= 4 or not known_first(n):
                        pool.wait_ge(qk_turned, PAIRS * n + (i - 4) // 2 + 1)
                    pool.tensor_tensor(k_scaled[i % 4][:, :], raw[i % 4][:, 1, :], rms[:, 1:2].to_broadcast([P, P]),
                                       ALU.mult).then_inc(k_ready, 1)

            heads(pool, step)

        @block.tensor
        def _(pe):
            def bank_is_read(h, attends, kind, which):
                if not attends:
                    if which >= 2:
                        pe.wait_ge(qk_ready, PAIRS * (h + 1) + which - 1)
                    return
                at = turn_of[(kind, which)]
                if at < 2:
                    pe.wait_ge(qk_ready, PAIRS * (h + 1))
                    if not known_first(h):
                        pe.wait_ge(wt_ready, UNITS * h)
                    return
                before, w = next(key for key, value in turn_of.items() if value == at - 2)
                if before == "w":
                    pe.wait_ge(wt_ready, UNITS * h + w + 1)
                elif not (isinstance(h, int) and h == HEADS - 1):
                    pe.wait_ge(qk_ready, PAIRS * (h + 1) + w + 1)

            def turn_x(i):
                pe.wait_ge(normed_ready, i + 1)
                for half in range(2):
                    use = 2 * i + half
                    if use >= 3:
                        pe.wait_ge(ut_ready, use - 2)
                    for q in range(4):
                        kt = 4 * half + q
                        last = pe.transpose(p_z[use % 3][:, q * P:(q + 1) * P], normed[i % 2][:, kt * P:(kt + 1) * P],
                                            c["ident"][:, :])
                    last.then_inc(x_turned, 1)

            def turn_qk(h, m, attends):
                n = h + 1
                pe.wait_ge(k_ready, 2 * (NAT * n + 2 * m + 2))
                bank_is_read(h, attends, "qk", m)
                bank = p_turn[(turn_of if attends else turn_alone)[("qk", m)] % 2]
                for t in range(2):
                    pe.transpose(bank[:, t, :], raw[(2 * m + t) % 4][:, 0, :], c["ident"][:, :])
                    last = pe.transpose(bank[:, 2 + t, :], k_scaled[(2 * m + t) % 4][:, :], c["ident"][:, :])
                last.then_inc(qk_turned, 1)

            def scores(h, b, i):
                pe.wait_ge(qk_ready, PAIRS * h + i // 2 + 1)
                rows = slice(i * P, (i + 1) * P)
                for u in range(Z_UNITS[i]):
                    width = min(HALF, (i + 1) * P - u * HALF)
                    unit = ENDS[i] - Z_UNITS[i] + u
                    bank = p_z[unit % 3]
                    if unit >= 3 or not known_first(h):
                        pe.wait_ge(sigmoids_ready, UNITS * h + unit - 2)
                    z = bank[:, 0:width]
                    cols = slice(u * HALF, u * HALF + width)
                    pe.matmul(z, qt_hi[b][:, rows], kt_hi[b][:, cols], start=True, stop=False,
                              skip_group_check=True)
                    if u == Z_UNITS[i] - 1:
                        pe.matmul(bank[:, width - P:width], c["ident_bf"][:, :],
                                  c["causal_neg"][:, :], start=False, stop=False, skip_group_check=True)
                    pe.matmul(z, qt_hi[b][:, rows], kt_lo[b][:, cols], start=False, stop=False,
                              skip_group_check=True)
                    pe.matmul(z, qt_lo[b][:, rows], kt_hi[b][:, cols], start=False, stop=True,
                              skip_group_check=True).then_inc(z_done, 1)

            def outputs(h, b, i):
                g = (i - 3) // 2
                pe.wait_ge(wt_ready, UNITS * h + ENDS[2 * g + 1])
                pe.wait_ge(v_ready, NAT * h + NAT)
                if g >= 1 or not known_first(h):
                    pe.wait_ge(o_gated, PAIRS * h + g)
                for s in range(2 * g + 2):
                    o = p_o[:, :, :] if s <= 2 * g else p_o[:, 1, :]
                    w_h = wt_hi[:, s, :, :] if s <= 2 * g else wt_hi[:, s, 1, :]
                    w_l = wt_lo[:, s, :, :] if s <= 2 * g else wt_lo[:, s, 1, :]
                    last = matmul_exact(pe, o, v_hi[b][:, s, :], v_lo[b][:, s, :], w_h, w_l,
                                        s == 0, s == 2 * g + 1)
                last.then_inc(o_done, 1)

            def step(h, b, attends, projects):
                n, nb = h + 1, 1 - b
                for i in range(USES):
                    if known_first(h) and attends and i == 0:
                        pe.wait_ge(ut_ready, 2 * TILES)
                        pe.wait_ge(dve_made, 2)
                        pe.wait_ge(pool_made, 6)
                    if attends and projects and i < TILES:
                        scores(h, b, i)
                    if attends and not projects:
                        for tile in ([0, 1] if i == 0 else [i + 1] if i + 1 < TILES else []):
                            scores(h, b, tile)
                    if projects:
                        if i >= 2:
                            pe.wait_ge(raw_ready, NAT * n + i - 1)
                        elif not known_first(n):
                            pe.wait_ge(gate_ready, GATE * (n - 1) + i + 1)
                        if i == 0:
                            for p in range(3):
                                pe.wait_ge(w_ready[p], n + 1)
                        if i == NAT:
                            pe.wait_ge(w_ready[3], n + 1)
                        if known_first(n) and i < TILES:
                            pe.wait_ge(ut_ready, 2 * i + 2)
                        for kt in range(KT):
                            if i >= 3 and i % 2 == 1 and kt == 2:
                                turn_qk(h, (i - 3) // 2, attends)
                            if known_first(n) and i + 1 < TILES and kt == KT // 2:
                                turn_x(i + 1)
                            if i < NAT:
                                rows = slice(i * P, (i + 1) * P)
                                last = matmul_exact(pe, p_proj[i % 2][:, 0:3, :].rearrange("p a b -> p (a b)"),
                                                    ut_hi[:, kt, rows], ut_lo[:, kt, rows],
                                                    w_qkv_hi[:, kt, :, :].rearrange("p a b -> p (a b)"),
                                                    w_qkv_lo[:, kt, :, :].rearrange("p a b -> p (a b)"),
                                                    kt == 0, kt == KT - 1)
                            else:
                                cols = slice((i - NAT) * HALF, (i - NAT + 1) * HALF)
                                last = matmul_exact(pe, p_wide[i % 2], w_gate_hi[:, kt, :],
                                                    w_gate_lo[:, kt, :], ut_hi[:, kt, cols], ut_lo[:, kt, cols],
                                                    kt == 0, kt == KT - 1)
                        last.then_inc(proj_done, 1)
                    if attends and i >= 3 and i % 2 == 1 and projects:
                        outputs(h, b, i)
                    if attends and 1 <= i <= TILES:
                        j = i - 1
                        pe.wait_ge(weights_ready, TILES * h + j + 1)
                        for u in range(Z_UNITS[j]):
                            unit = ENDS[j] - Z_UNITS[j] + u
                            if projects:
                                bank_is_read(h, attends, "w", unit)
                            elif unit >= 2:
                                pe.wait_ge(wt_ready, UNITS * h + unit - 1)
                            else:
                                pe.wait_ge(wt_ready, UNITS * h)
                                pe.wait_ge(qk_ready, PAIRS * HEADS)
                            for s in range(4 * u, min(4 * u + 4, j + 1)):
                                last = pe.transpose(w_bank(unit, projects)[:, s - 4 * u, :],
                                                    beta[j % 2][:, s * P:(s + 1) * P], c["ident"][:, :])
                            last.then_inc(weights_turned, 1)
                    if not projects and i in START_AT:
                        pe.wait_ge(gate_ready, GATE * HEADS)
                        start_output_tile(pe, p_proj, w_qkv_hi, w_qkv_lo, ut_hi, ut_lo, link["m_ready"],
                                          w_out_ready, START_AT[i])
                    if attends and i >= 3 and i % 2 == 1 and not projects:
                        outputs(h, b, i)

            pe.wait_ge(pool_made, 4)
            turn_x(0)
            heads(pe, step)


def build_output_projection(nc, tag, c, m_in, link, mixed, w_hi, w_lo, residual, dst,
                            m_hi, m_lo, p_proj, gain, ut_hi, ut_lo,
                            next_weights):
    def split_count(i, part):
        return 2 * part + i + 1 if i < 2 else i + 3

    if next_weights is not None:
        stage, w_in, w, w_qf_hi, w_qf_lo = next_weights

    with ExitStack() as ctx:
        def sb(name, shape, dt=F32):
            return ctx.enter_context(nc.sbuf_tensor(f"{tag}_{name}", shape, dt))

        def sem(name):
            return ctx.enter_context(nc.semaphore(f"{tag}_{name}"))

        last_in = sb("last_in", [P, 2, P])
        h_tile = [sb(f"h_tile{i}", [P, D_MODEL]) for i in range(2)]
        p_y = [bank[:, :, :].rearrange("p a b -> p (a b)") for bank in p_proj]
        p_y += [ctx.enter_context(nc.psum_tensor(f"{tag}_p_y{i}", [P, HALF], F32))[:, :] for i in range(2)]
        if gain is not None:
            gain_rows = sb("gain_rows", [P, D_MODEL])
            squares = sb("squares", [P, D_MODEL])
            normed = [sb(f"normed{i}", [P, D_MODEL]) for i in range(2)]
            sum_sq = [sb(f"sum_sq{i}", [P, 1]) for i in range(2)]
            mean_sq = [sb(f"mean_sq{i}", [P, 1]) for i in range(2)]
            inv_rms = [sb(f"inv_rms{i}", [P, 1]) for i in range(2)]
            turned = [ctx.enter_context(nc.psum_tensor(f"{tag}_turned{i}", [P, 4, P], F32)) for i in range(2)]

        gain_loaded = sem("gain_loaded")
        m_loaded = link["m_loaded"]
        last_loaded = [sem(f"last_loaded{i}") for i in range(2)]
        m_hi_ready = link["m_hi_ready"]
        m_ready = link["m_ready"]
        r_loaded = [sem(f"r_loaded{i}") for i in range(2)]
        y_done = sem("y_done")
        h_ready = sem("h_ready")
        stored = sem("stored")
        sum_ready = sem("sum_ready")
        mean_ready = sem("mean_ready")
        rms_ready = sem("rms_ready")
        normed_ready = sem("normed_ready")
        turned_ready = sem("turned_ready")
        hi_ready = sem("hi_ready")
        lo_ready = sem("lo_ready")

        block = ctx.enter_context(nc.Block())

        @block.sync
        def _(sp):
            def load_residual(i):
                if i >= 2:
                    sp.wait_ge(stored, 16 * (i - 1))
                    if gain is not None:
                        sp.wait_ge(normed_ready, i - 1)
                sp.dma_start(h_tile[i % 2][:, :], residual[i * P:(i + 1) * P, :]).then_inc(r_loaded[i % 2], 16)

            def load_tile(i):
                if i >= 4:
                    sp.wait_ge(m_ready, split_count(i - 2, 1))
                load_mixed(sp, m_in, mixed, i, slice(0, HEADS)).then_inc(m_loaded[i % 2], 16)

            sp.wait_ge(link["stored"], 16 * HEADS)
            for i in range(2):
                sp.dma_start(last_in[:, i, :], mixed[HEADS - 1, :, i * P:(i + 1) * P]).then_inc(last_loaded[i], 16)
            sp.wait_ge(m_ready, split_count(1, 0))
            load_tile(2)
            load_residual(0)
            load_residual(1)
            if gain is not None:
                sp.dma_start(gain_rows[:, :], gain[0:1, :].to_broadcast([P, D_MODEL])).then_inc(gain_loaded, 16)
            load_tile(3)
            for i in range(TILES):
                if 2 <= i < TILES - 2:
                    load_tile(i + 2)
                sp.wait_ge(h_ready, 2 * i + 2)
                sp.dma_start(dst[i * P:(i + 1) * P, :], h_tile[i % 2][:, :]).then_inc(stored, 16)
                if i + 2 < TILES:
                    load_residual(i + 2)
                if 1 <= i <= 4 and next_weights is not None:
                    load_columns(sp, stage, w_in, 0, i - 1).then_inc(w["w_loaded"][i - 1], 16)
            sp.wait_ge(stored, 16 * TILES)

        @block.scalar
        def _(act):
            def mixed_hi(i):
                if i >= 2:
                    act.wait_ge(y_done, 2 * (i - 1))
                if i < 2:
                    act.wait_ge(last_loaded[i], 16)
                    act.activation(m_hi[:, HEADS - 1, i, :], last_in[:, i, :], ACT.Copy).then_inc(m_hi_ready, 1)
                    return
                act.wait_ge(m_loaded[i % 2], 16 * (i // 2 + 1))
                act.activation(m_hi[:, :, i % 2, :], m_in[i % 2][:, :, :], ACT.Copy).then_inc(m_hi_ready, 1)

            mixed_hi(0)
            mixed_hi(1)
            for i in range(TILES + 1):
                if i + 2 < TILES:
                    mixed_hi(i + 2)
                if gain is not None and i < TILES:
                    act.wait_ge(h_ready, 2 * i + 2)
                    if i >= 1:
                        act.wait_ge(sum_ready, i)
                    if i >= 2:
                        act.wait_ge(mean_ready, i - 1)
                    act.activation(squares[:, :], h_tile[i % 2][:, :], ACT.Square,
                                   accum_out=sum_sq[i % 2][:, :]).then_inc(sum_ready, 1)
                if next_weights is not None and i in (5, 6):
                    act.wait_ge(w["w_loaded"][i - 5], 16)
                    act.activation(w_qf_hi[:, :, i - 5, :], stage[i - 5][:, :, :],
                                   ACT.Copy).then_inc(w["w_hi_ready"][i - 5], 1)
                if gain is not None and i >= 1:
                    j = i - 1
                    for half in range(2):
                        act.wait_ge(turned_ready, 2 * j + half + 1)
                        act.activation(ut_hi[:, 4 * half:4 * half + 4, j * P:(j + 1) * P],
                                       turned[half][:, :, :], ACT.Copy).then_inc(hi_ready, 1)

        @block.vector
        def _(dve):
            def mixed_lo(i):
                if i >= 2:
                    dve.wait_ge(y_done, 2 * (i - 1))
                heads, source = (slice(HEADS - 1, HEADS), last_in[:, i:i + 1, :]) if i < 2 else (
                    slice(0, HEADS), m_in[i % 2][:, :, :])
                dve.wait_ge(m_hi_ready, split_count(i, 1))
                dve.tensor_tensor(m_lo[:, heads, i % 2, :], source, m_hi[:, heads, i % 2, :].bitcast(F32),
                                  ALU.subtract).then_inc(m_ready, 1)

            mixed_lo(0)
            mixed_lo(1)
            for i in range(TILES + 1):
                if i < TILES:
                    dve.wait_ge(r_loaded[i % 2], 16 * (i // 2 + 1))
                    for half in range(2):
                        cols = slice(half * HALF, (half + 1) * HALF)
                        dve.wait_ge(y_done, 2 * i + half + 1)
                        dve.tensor_tensor(h_tile[i % 2][:, cols], h_tile[i % 2][:, cols],
                                          p_y[(2 * i + half) % 4], ALU.add).then_inc(h_ready, 1)
                if i + 2 < TILES:
                    mixed_lo(i + 2)
                if next_weights is not None and i in (5, 6):
                    dve.wait_ge(w["w_hi_ready"][i - 5], 1)
                    dve.tensor_tensor(w_qf_lo[:, :, i - 5, :], stage[i - 5][:, :, :],
                                      w_qf_hi[:, :, i - 5, :].bitcast(F32),
                                      ALU.subtract).then_inc(w["w_ready"][i - 5], 1)
                if gain is not None and i < TILES:
                    if i == 0:
                        dve.wait_ge(gain_loaded, 16)
                    dve.wait_ge(rms_ready, i + 1)
                    dve.wait_ge(h_ready, 2 * i + 2)
                    if i >= 2:
                        dve.wait_ge(turned_ready, 2 * (i - 1))
                    dve.scalar_tensor_tensor(out=normed[i % 2][:, :], in0=h_tile[i % 2][:, :],
                                             scalar=inv_rms[i % 2][:, 0:1], in1=gain_rows[:, :],
                                             op0=ALU.mult, op1=ALU.mult).then_inc(normed_ready, 1)
                if gain is not None and i >= 1:
                    j = i - 1
                    for half in range(2):
                        dve.wait_ge(hi_ready, 2 * j + half + 1)
                        dve.tensor_tensor(ut_lo[:, 4 * half:4 * half + 4, j * P:(j + 1) * P], turned[half][:, :, :],
                                          ut_hi[:, 4 * half:4 * half + 4, j * P:(j + 1) * P].bitcast(F32),
                                          ALU.subtract).then_inc(lo_ready, 1)

        @block.gpsimd
        def _(pool):
            if gain is None:
                return
            for i in range(TILES):
                pool.wait_ge(sum_ready, i + 1)
                pool.tensor_scalar(mean_sq[i % 2][:, :], sum_sq[i % 2][:, :], 1.0 / D_MODEL, RMS_EPS,
                                   ALU.mult, ALU.add).then_inc(mean_ready, 1)
                pool.wait_ge(mean_ready, i + 1)
                if i >= 2:
                    pool.wait_ge(normed_ready, i - 1)
                pool.tensor_tensor(inv_rms[i % 2][:, :], mean_sq[i % 2][:, :], c["minus_half"][:, 0:1],
                                   ALU.pow).then_inc(rms_ready, 1)

        @block.tensor
        def _(pe):
            def product(i, half, heads):
                cols = slice(half * HALF, (half + 1) * HALF)
                for h in heads:
                    last = matmul_exact(pe, p_y[(2 * i + half) % 4], m_hi[:, h, i % 2, :], m_lo[:, h, i % 2, :],
                                        w_hi[:, h, cols], w_lo[:, h, cols], h == 0, h == HEADS - 1)
                return last

            def turn_tile(j):
                pe.wait_ge(normed_ready, j + 1)
                for half in range(2):
                    if j >= 1:
                        pe.wait_ge(lo_ready, 2 * (j - 1) + half + 1)
                    for q in range(4):
                        kt = 4 * half + q
                        last = pe.transpose(turned[half][:, q, :], normed[j % 2][:, kt * P:(kt + 1) * P],
                                            c["ident"][:, :])
                    last.then_inc(turned_ready, 1)

            pe.wait_ge(m_ready, split_count(1, 0))
            product(1, 0, range(HEADS - 1))
            pe.wait_ge(m_ready, split_count(0, 1))
            for half in range(2):
                product(0, half, [HEADS - 1]).then_inc(y_done, 1)
            product(1, 1, range(HEADS - 1))
            pe.wait_ge(m_ready, split_count(1, 1))
            for half in range(2):
                product(1, half, [HEADS - 1]).then_inc(y_done, 1)
            for i in range(2, TILES):
                pe.wait_ge(m_ready, split_count(i, 1))
                for half in range(2):
                    pe.wait_ge(h_ready, 2 * i + half - 3)
                    product(i, half, range(HEADS)).then_inc(y_done, 1)
                    if gain is not None and half == 0:
                        turn_tile(i - 2)
            if gain is not None:
                turn_tile(TILES - 2)
                turn_tile(TILES - 1)


def build_hgrn(nc, c, stage, m_in, link, w, w_in, w_out, ut_hi, ut_lo,
               w_qf_hi, w_qf_lo, p_proj, mixed):
    L = len(LEVELS)
    MASKED = L - 1
    W_OUT_AT = {0: [0, 1], 1: [2, 3], 2: [4], 3: [5], 4: [6], 5: [7]}
    M_AT = [4, 5]
    START_AT = {4: [0, 1], 6: range(2, HEADS - 1)}
    HALVES = SEQ // 2
    USES = 8

    with ExitStack() as ctx:
        def sb(name, shape, dt=F32):
            return ctx.enter_context(nc.sbuf_tensor("g_" + name, shape, dt))

        def psum(name, shape):
            return ctx.enter_context(nc.psum_tensor("g_" + name, shape, F32))

        def sem(name):
            return ctx.enter_context(nc.semaphore("g_" + name))

        w_ig_hi = sb("w_ig_hi", [P, KT, 2, P], F32R)
        w_ig_lo = sb("w_ig_lo", [P, KT, 2, P], F32R)
        q = [sb(f"q{b}", [P, SEQ]) for b in range(2)]
        k = [sb(f"k{b}", [P, SEQ]) for b in range(2)]
        prefix = [sb(f"prefix{b}", [P, SEQ]) for b in range(2)]
        suffix = sb("suffix", [P, SEQ])
        value = [sb(f"value{b}", [P, TILES, P]) for b in range(2)]
        gate = [sb(f"gate{b}", [P, TILES, P]) for b in range(2)]
        q_right = [sb(f"q_right{i}", [P, HALVES]) for i in range(2)]
        k_left = [sb(f"k_left{i}", [P, SEQ]) for i in range(2)]
        scores = [sb(f"scores{b}", [P, TILES, P]) for b in range(2)]
        q_chunk = sb("q_chunk", [P, SEQ])
        k_chunk = sb("k_chunk", [P, SEQ])
        qk = sb("qk", [P, SEQ])
        self_score = sb("self_score", [P, TILES])
        k_turned = sb("k_turned", [P, TILES, P])
        state = sb("state", [P, TILES, P])
        o = sb("o", [P, TILES, P])
        squares = [sb(f"squares{i}", [P, P]) for i in range(2)]
        sum_sq = sb("sum_sq", [P, TILES])
        sum_eps = sb("sum_eps", [P, TILES])
        inv_rms = sb("inv_rms", [P, TILES])
        out_turned = sb("out_turned", [P, SEQ])
        waits_taken = sb("waits_taken", [P, 1])

        p_wide = [bank[:, :, :].rearrange("p a b -> p (a b)") for bank in p_proj]
        p_level = [psum(f"p_level{i}", [P, HALF]) for i in range(2)]
        p_misc = [psum(f"p_misc{i}", [P, 4, P]) for i in range(4)]

        w_out_hi_ready = sem("w_out_hi_ready")
        w_out_ready = sem("w_out_ready")
        w_loaded, w_hi_ready, w_ready = w["w_loaded"], w["w_hi_ready"], w["w_ready"]
        proj_done = sem("proj_done")
        q_sigmoid = sem("q_sigmoid")
        q_ready = sem("q_ready")
        f_sigmoid = sem("f_sigmoid")
        fk_ready = sem("fk_ready")
        ig_copied = sem("ig_copied")
        gate_ready = sem("gate_ready")
        zeroed = sem("zeroed")
        masks_made = sem("masks_made")
        k_prepared = sem("k_prepared")
        prepared = sem("prepared")
        doubled = sem("doubled")
        level_done = sem("level_done")
        level_placed = sem("level_placed")
        last_placed = sem("last_placed")
        k_chunk_ready = sem("k_chunk_ready")
        chunk_ready = sem("chunk_ready")
        self_done = sem("self_done")
        self_ready = sem("self_ready")
        k_turned_done = sem("k_turned_done")
        k_turned_ready = sem("k_turned_ready")
        update_done = sem("update_done")
        state_ready = sem("state_ready")
        o_done = sem("o_done")
        o_ready = sem("o_ready")
        sums_ready = sem("sums_ready")
        eps_added = sem("eps_added")
        rms_ready = sem("rms_ready")
        o_gated = sem("o_gated")
        o_turned = sem("o_turned")
        out_ready = sem("out_ready")
        out_stored = link["stored"]

        def heads(eng, step):
            step(-1, 1, False, True)
            step(0, 0, True, True)
            with eng.Fori(0, (HEADS - 4) // 2) as pair:
                step(pair * 2 + 1, 1, True, True)
                step(pair * 2 + 2, 0, True, True)
            step(HEADS - 3, 1, True, True)
            step(HEADS - 2, 0, True, True)
            step(HEADS - 1, 1, True, False)

        def level_bank(level, projects):
            return p_level[level % 2] if projects or level < L - 2 else p_wide[level - (L - 2)]

        def known_first(h):
            return isinstance(h, int) and h <= 0

        block = ctx.enter_context(nc.Block())

        @block.sync
        def _(sp):
            def load_out(r):
                if r < 4:
                    sp.wait_ge(w_ready[r], HEADS)
                else:
                    sp.wait_ge(w_out_ready, r - 3)
                load_w_out(sp, stage, w_out, r).then_inc(link["w_loaded"][r % 4], 16)

            def load_mixed_early(i):
                sp.wait_ge(out_stored, 16 * (HEADS - 1))
                load_mixed(sp, m_in, mixed, i, slice(0, HEADS - 1)).then_inc(link["m_loaded"][i], 16)

            def load(h, p):
                if not known_first(h):
                    sp.wait_ge(w_ready[p], h)
                load_columns(sp, stage, w_in, h, p).then_inc(w_loaded[p], 16)

            def store(h):
                sp.wait_ge(out_ready, 2 * h + 2)
                sp.dma_start(mixed[bass.ds(h, 1), :, :].rearrange("o p s -> p (o s)"),
                             out_turned[:, :]).then_inc(out_stored, 16)

            for h in range(1, 3):
                for p in range(4):
                    load(h, p)
            with sp.Fori(0, HEADS - 3) as h:
                store(h)
                for p in range(4):
                    load(h + 3, p)
            store(HEADS - 3)
            for r in range(4):
                load_out(r)
            store(HEADS - 2)
            for i in range(2):
                load_mixed_early(i)
            load_out(4)
            load_out(5)
            load_out(6)
            load_out(7)
            store(HEADS - 1)

        @block.scalar
        def _(act):
            def split_w_out_hi(r):
                act.wait_ge(proj_done, USES * HEADS)
                act.wait_ge(link["w_loaded"][r % 4], 16 * (r // 4) + 16)
                act.activation(ut_hi[:, r, :], stage[r % 4][:, :, :].rearrange("p k c -> p (k c)"),
                               ACT.Copy).then_inc(w_out_hi_ready, 1)

            def split_hi(h, p):
                if not known_first(h):
                    act.wait_ge(proj_done, USES * (h - 1) + (4 if p < 2 else USES))
                act.wait_ge(w_loaded[p], 16 * h + 16)
                dst = (w_qf_hi if p < 2 else w_ig_hi)[:, :, p % 2, :]
                act.activation(dst, stage[p][:, :, :], ACT.Copy).then_inc(w_hi_ready[p], 1)

            def place_last(h, b, projects):
                act.wait_ge(level_placed, MASKED * h + MASKED)
                act.wait_ge(level_done, L * h + L)
                act.activation(scores[b][0:P // 2, :, P // 2:P],
                               level_bank(L - 1, projects)[0:P // 2, :].rearrange("p (m t) -> p m t", m=TILES),
                               ACT.Copy).then_inc(last_placed, 1)

            def step(h, b, mixes, projects):
                n, nb = h + 1, 1 - b
                early = isinstance(n, int) and n < 2
                last_head = isinstance(n, int) and n == HEADS - 1
                for i in range(USES):
                    if projects and i in (1, 2):
                        split_hi(n, i + 1)
                    if projects and i in (4, 5) and not last_head:
                        split_hi(n + 1, i - 4)
                    if mixes and projects and i == 3:
                        place_last(h, b, projects)
                    if mixes and i == 4:
                        for u in range(2):
                            act.wait_ge(k_turned_done, 2 * h + u + 1)
                            if not known_first(h):
                                act.wait_ge(update_done, 2 * h)
                            act.activation(k_turned[:, 4 * u:4 * u + 4, :], p_misc[u][:, :, :],
                                           ACT.Copy).then_inc(k_turned_ready, 1)
                    if mixes and not projects and i == 4:
                        place_last(h, b, projects)
                    if not projects and i in M_AT:
                        split_mixed_hi(act, m_in, w_qf_hi, link, M_AT.index(i))
                    if not projects:
                        for r in W_OUT_AT.get(i, []):
                            split_w_out_hi(r)
                    if mixes and i == 6:
                        for m in range(TILES):
                            act.wait_ge(o_ready, TILES * h + m + 1)
                            if m >= 2 or not known_first(h):
                                act.wait_ge(sums_ready, TILES * h + m - 1)
                            if m == 0 and not known_first(h):
                                act.wait_ge(eps_added, h)
                            act.activation(squares[m % 2][:, :], o[:, m, :], ACT.Square,
                                           accum_out=sum_sq[:, m:m + 1]).then_inc(sums_ready, 1)
                    if projects:
                        act.wait_ge(proj_done, USES * n + i + 1)
                        cols = slice((i % 2) * HALF, (i % 2 + 1) * HALF)
                        if i == 0 and not early:
                            act.wait_ge(state_ready, (TILES - 1) * (n - 1))
                            act.wait_ge(o_gated, n - 1)
                            act.wait_ge(chunk_ready, n - 1)
                        if i < 2:
                            act.activation(q[nb][:, cols], p_wide[i % 2][:, :], ACT.Sigmoid).then_inc(q_sigmoid, 1)
                        elif i < 4:
                            act.activation(prefix[nb][:, cols], p_wide[i % 2][:, :], ACT.Sigmoid)
                            act.activation(k[nb][:, cols], p_wide[i % 2][:, :], ACT.Sigmoid,
                                           scale=-1.0).then_inc(f_sigmoid, 1)
                        else:
                            both = p_wide[i % 2][:, :].rearrange("p (t a v) -> p t a v", t=2, a=2)
                            tiles = slice(2 * (i - 4), 2 * (i - 4) + 2)
                            act.activation(value[nb][:, tiles, :], both[:, :, 0, :], ACT.Copy)
                            act.activation(gate[nb][:, tiles, :], both[:, :, 1, :],
                                           ACT.Sigmoid).then_inc(ig_copied, 1)
                    if mixes and i == 7:
                        for u in range(2):
                            act.wait_ge(o_turned, 2 * h + u + 1)
                            if u == 0 and not known_first(h):
                                act.wait_ge(out_stored, 16 * h)
                            act.activation(out_turned[:, u * HALF:(u + 1) * HALF],
                                           p_misc[2 + u][:, :, :].rearrange("p a b -> p (a b)"), ACT.Copy,
                                           scale=c["o_scale"][:, 0:1]).then_inc(out_ready, 1)

            heads(act, step)

        @block.vector
        def _(dve):

            def split_lo(h, p):
                if not known_first(h):
                    dve.wait_ge(proj_done, USES * (h - 1) + (4 if p < 2 else USES))
                dve.wait_ge(w_hi_ready[p], h + 1)
                hi = (w_qf_hi if p < 2 else w_ig_hi)[:, :, p % 2, :]
                lo = (w_qf_lo if p < 2 else w_ig_lo)[:, :, p % 2, :]
                dve.tensor_tensor(lo, stage[p][:, :, :], hi.bitcast(F32), ALU.subtract).then_inc(w_ready[p], 1)

            def by_halves(t, half):
                return t[:, :].rearrange("p (b two r) -> p b two r", two=2, r=half)

            def prepare(h, b, level):
                half = LEVELS[level]
                blocks = SEQ // (2 * half)
                pre, suf = by_halves(prefix[b], half), by_halves(suffix, half)
                if level == 0:
                    dve.wait_ge(fk_ready, 2 * h + 2)
                    dve.wait_ge(q_ready, 2 * h + 2)
                    if known_first(h):
                        dve.wait_ge(zeroed, 5)
                    else:
                        dve.wait_ge(chunk_ready, h)
                else:
                    dve.wait_ge(doubled, 2 * (L * h + level) - 1)
                if level >= 2:
                    dve.wait_ge(level_done, L * h + level - 1)
                elif not known_first(h):
                    dve.wait_ge(level_done, L * h)
                q_out = q_right[level % 2][:, :].rearrange("p (b r) -> p b r", r=half)
                k_out = by_halves(k_left[level % 2], half)[:, :, 0, :]
                k_in = by_halves(k[b], half)[:, :, 0, :]
                if level == 0:
                    dve.tensor_copy(k_out, k_in).then_inc(k_prepared, 1)
                else:
                    dve.tensor_tensor(k_out, k_in, suf[:, :, 0, :], ALU.mult).then_inc(k_prepared, 1)
                    dve.wait_ge(doubled, 2 * (L * h + level))
                dve.tensor_tensor(q_out, by_halves(q[b], half)[:, :, 1, :], pre[:, :, 1, :],
                                  ALU.mult).then_inc(prepared, 1)
                dve.wait_ge(k_prepared, L * h + level + 1)
                if level == 0:
                    dve.tensor_copy(suf[:, :, 0, :], pre[:, :, 1, :])
                    dve.memset(suf[:, :, 1, :], 1.0).then_inc(doubled, 1)
                else:
                    dve.tensor_tensor(suf[:, :, 0, :], suf[:, :, 0, :],
                                      pre[:, :, 1, half - 1:half].to_broadcast([P, blocks, half]),
                                      ALU.mult).then_inc(doubled, 1)
                dve.wait_ge(prepared, L * h + level + 1)
                dve.wait_ge(doubled, 2 * (L * h + level) + 1)
                dve.tensor_tensor(pre[:, :, 1, :], pre[:, :, 1, :],
                                  pre[:, :, 0, half - 1:half].to_broadcast([P, blocks, half]),
                                  ALU.mult).then_inc(doubled, 1)

            def place(h, b, level, bank):
                half = LEVELS[level]
                blocks = P // (2 * half)
                dve.wait_ge(level_done, L * h + level + 1)
                if level == 0 and not (isinstance(h, int) and h < 2):
                    dve.wait_ge(o_done, 2 * (h - 1))
                if level >= 1:
                    dve.wait_ge(level_placed, MASKED * h + level)
                dve.memset(waits_taken[:, :], 0.0)
                dve.wait_ge(masks_made, 1 + 2 * L)
                dst = scores[b][:, :, :].rearrange("p m (b two r) -> p m b two r", two=2, r=half)[:, :, :, 1, :]
                mask = c["level_mask"][:, level, :].bitcast(I32).rearrange("p (b r) -> p b r", r=half)
                dve.copy_predicated(dst, mask.unsqueeze(1).to_broadcast([P, TILES, blocks, half]),
                                    bank[:, :].rearrange("p (m b r) -> p m b r", m=TILES, r=half)
                                    ).then_inc(level_placed, 1)

            def chunk_operands(h, b):
                dve.wait_ge(doubled, 2 * L * (h + 1))
                if not known_first(h):
                    dve.wait_ge(o_done, 2 * h)
                    dve.wait_ge(k_turned_done, 2 * h)
                    dve.wait_ge(self_done, h)
                dve.tensor_tensor(k_chunk[:, :], k[b][:, :], suffix[:, :], ALU.mult).then_inc(k_chunk_ready, 1)
                dve.tensor_tensor(qk[:, :], q[b][:, :], k[b][:, :], ALU.mult)
                dve.tensor_tensor(q_chunk[:, :], q[b][:, :], prefix[b][:, :], ALU.mult).then_inc(chunk_ready, 1)

            def states(h, b):
                for m in range(TILES - 1):
                    bank = p_misc[2 + m // 4][:, m % 4, :]
                    dve.wait_ge(update_done, 2 * h + m // 4 + 1)
                    if m == 0:
                        if not known_first(h):
                            dve.wait_ge(o_done, 2 * h)
                        dve.tensor_copy(state[:, 1, :], bank).then_inc(state_ready, 1)
                    else:
                        dve.wait_ge(state_ready, (TILES - 1) * h + m)
                        dve.scalar_tensor_tensor(out=state[:, m + 1, :], in0=state[:, m, :],
                                                 scalar=prefix[b][:, m * P + P - 1:m * P + P], in1=bank,
                                                 op0=ALU.mult, op1=ALU.add).then_inc(state_ready, 1)

            def outputs(h, b):
                dve.wait_ge(self_ready, h + 1)
                if not known_first(h):
                    dve.wait_ge(o_turned, 2 * h)
                for m in range(TILES):
                    dve.wait_ge(o_done, 2 * h + m // 4 + 1)
                    dve.scalar_tensor_tensor(out=o[:, m, :], in0=value[b][:, m, :], scalar=self_score[:, m:m + 1],
                                             in1=p_misc[m // 4][:, m % 4, :], op0=ALU.mult,
                                             op1=ALU.add).then_inc(o_ready, 1)

            def gate_outputs(h, b):
                dve.wait_ge(rms_ready, h + 1)
                dve.wait_ge(gate_ready, 4 * h + 4)
                for m in range(TILES):
                    ins = dve.scalar_tensor_tensor(out=o[:, m, :], in0=o[:, m, :], scalar=inv_rms[:, m:m + 1],
                                                   in1=gate[b][:, m, :], op0=ALU.mult, op1=ALU.mult)
                ins.then_inc(o_gated, 1)

            def step(h, b, mixes, projects):
                n, nb = h + 1, 1 - b
                last_head = isinstance(n, int) and n == HEADS - 1
                for i in range(USES):
                    if mixes and i < 3:
                        prepare(h, b, 4 + i)
                        if projects:
                            place(h, b, 3 + i, level_bank(3 + i, projects))
                    if mixes and i == 3:
                        chunk_operands(h, b)
                        if not projects:
                            for level in range(3, L - 1):
                                place(h, b, level, level_bank(level, projects))
                    if mixes and i == 4:
                        dve.wait_ge(self_done, h + 1)
                        if not known_first(h):
                            dve.wait_ge(o_ready, TILES * h)
                        dve.tensor_copy(self_score[:, :], p_level[1][:, 0:TILES]).then_inc(self_ready, 1)
                    if projects and i >= 4:
                        prepare(n, nb, i - 4)
                    if not projects and i in M_AT:
                        split_mixed_lo(dve, m_in, w_qf_hi, w_qf_lo, link, M_AT.index(i))
                    if mixes and i == 5:
                        states(h, b)
                    if mixes and i == 6:
                        outputs(h, b)
                    if projects and i >= 5:
                        place(n, nb, i - 5, level_bank(i - 5, True))
                    if mixes and i == 7:
                        gate_outputs(h, b)
                    if projects and i in (1, 2):
                        split_lo(n, i + 1)
                    if projects and i in (4, 5) and not last_head:
                        split_lo(n + 1, i - 4)
                    if projects:
                        cols = slice((i % 2) * HALF, (i % 2 + 1) * HALF)
                        if i < 2:
                            dve.wait_ge(q_sigmoid, 2 * n + i + 1)
                            dve.tensor_tensor(q[nb][:, cols], q[nb][:, cols], p_wide[i % 2][:, :],
                                              ALU.mult).then_inc(q_ready, 1)
                        elif i < 4:
                            dve.wait_ge(f_sigmoid, 2 * n + i - 1)
                            scale = c["one_minus_lower"][:, bass.ds(n, 1)]
                            dve.tensor_scalar(prefix[nb][:, cols], prefix[nb][:, cols], scale,
                                              c["lower"][:, bass.ds(n, 1)], ALU.mult, ALU.add)
                            dve.tensor_scalar(k[nb][:, cols], k[nb][:, cols], scale, None,
                                              ALU.mult).then_inc(fk_ready, 1)
                        else:
                            dve.wait_ge(ig_copied, 4 * n + i - 3)
                            tiles = slice(2 * (i - 4), 2 * (i - 4) + 2)
                            both = p_wide[i % 2][:, :].rearrange("p (t a v) -> p t a v", t=2, a=2)
                            dve.tensor_tensor(gate[nb][:, tiles, :], gate[nb][:, tiles, :], both[:, :, 1, :],
                                              ALU.mult).then_inc(gate_ready, 1)

            heads(dve, step)

        @block.gpsimd
        def _(pool):
            pool.memset(suffix[:, :], 1.0).then_inc(zeroed, 1)
            for i in range(2):
                pool.memset(k_left[i][:, :], 0.0).then_inc(zeroed, 1)
                pool.memset(scores[i][:, :, :], 0.0).then_inc(zeroed, 1)
            pool.memset(c["level_mask"][:, :, :], 1.0).then_inc(masks_made, 1)
            pool.wait_ge(masks_made, 1)
            for n, half in enumerate(LEVELS):
                mask = c["level_mask"][:, n, :].rearrange("p (b r) -> p b r", r=half)
                pool.affine_select(out=mask, in_=mask, compare_op=ALU.is_ge, fill=0.0, base=0,
                                   pattern=[[-2 * half, P // 2 // half], [0, half]],
                                   channel_multiplier=1).then_inc(masks_made, 1)
                pool.wait_ge(masks_made, 2 + 2 * n)
                pool.affine_select(out=mask, in_=mask, compare_op=ALU.is_gt, fill=0.0, base=half,
                                   pattern=[[2 * half, P // 2 // half], [0, half]],
                                   channel_multiplier=-1).then_inc(masks_made, 1)

            def step(h, b, mixes, projects):
                if not mixes:
                    return
                if not projects:
                    for r in range(HEADS):
                        pool.wait_ge(w_out_hi_ready, r + 1)
                        pool.tensor_tensor(ut_lo[:, r, :], stage[r % 4][:, :, :].rearrange("p k c -> p (k c)"),
                                           ut_hi[:, r, :].bitcast(F32), ALU.subtract).then_inc(w_out_ready, 1)
                pool.wait_ge(sums_ready, TILES * h + TILES)
                if not known_first(h):
                    pool.wait_ge(rms_ready, h)
                pool.tensor_tensor(sum_eps[:, :], sum_sq[:, :], c["head_eps"][:, :], ALU.add).then_inc(eps_added, 1)
                pool.wait_ge(eps_added, h + 1)
                if not known_first(h):
                    pool.wait_ge(o_gated, h)
                pool.tensor_tensor(inv_rms[:, :], sum_eps[:, :], c["minus_half"][:, :], ALU.pow).then_inc(rms_ready, 1)

            heads(pool, step)

        @block.tensor
        def _(pe):
            def multiply_level(h, level, projects):
                pe.wait_ge(prepared, L * h + level + 1)
                if level >= L - 2 and not projects:
                    pe.wait_ge(gate_ready, 4 * HEADS)
                elif level >= 2:
                    pe.wait_ge(level_placed, MASKED * h + level - 1)
                elif level == 0 and not known_first(h):
                    pe.wait_ge(last_placed, h)
                elif level == 1 and not known_first(h):
                    pe.wait_ge(self_ready, h)
                rows = P if level < L - 1 else P // 2
                for m in range(TILES):
                    last = pe.matmul(level_bank(level, projects)[0:rows, m * (P // 2):(m + 1) * (P // 2)],
                                     k_left[level % 2][:, m * P:m * P + rows],
                                     q_right[level % 2][:, m * (P // 2):(m + 1) * (P // 2)], start=True, stop=True)
                last.then_inc(level_done, 1)

            def step(h, b, mixes, projects):
                n, nb = h + 1, 1 - b
                for i in range(USES):
                    if projects:
                        if i in (0, 1) and not known_first(n):
                            pe.wait_ge(gate_ready, 4 * (n - 1) + 3 + i)
                        if i in (2, 3):
                            pe.wait_ge(q_ready, 2 * n + i - 1)
                        if i in (4, 5):
                            pe.wait_ge(f_sigmoid, 2 * n + i - 3)
                        if i in (6, 7):
                            pe.wait_ge(gate_ready, 4 * n + i - 5)
                        if i in (0, 2):
                            pe.wait_ge(w_ready[i // 2], n + 1)
                        if i == 4:
                            pe.wait_ge(w_ready[2], n + 1)
                            pe.wait_ge(w_ready[3], n + 1)
                        if i < 4:
                            cols = slice((i % 2) * HALF, (i % 2 + 1) * HALF)
                            for kt in range(KT):
                                last = matmul_exact(pe, p_wide[i % 2][:, :], w_qf_hi[:, kt, i // 2, :],
                                                    w_qf_lo[:, kt, i // 2, :], ut_hi[:, kt, cols],
                                                    ut_lo[:, kt, cols], kt == 0, kt == KT - 1)
                        else:
                            for t in range(2):
                                tile = 2 * (i - 4) + t
                                rows = slice(tile * P, (tile + 1) * P)
                                for kt in range(KT):
                                    last = matmul_exact(pe, p_wide[i % 2][:, t * 2 * P:(t + 1) * 2 * P],
                                                        ut_hi[:, kt, rows], ut_lo[:, kt, rows],
                                                        w_ig_hi[:, kt, :, :].rearrange("p a b -> p (a b)"),
                                                        w_ig_lo[:, kt, :, :].rearrange("p a b -> p (a b)"),
                                                        kt == 0, kt == KT - 1)
                        last.then_inc(proj_done, 1)
                    if mixes and i < 3:
                        multiply_level(h, 4 + i, projects)
                    if mixes and i == 3:
                        pe.wait_ge(k_chunk_ready, h + 1)
                        if not known_first(h):
                            pe.wait_ge(o_ready, TILES * h)
                        for u in range(2):
                            for m in range(4):
                                last = pe.transpose(p_misc[u][:, m, :],
                                                    k_chunk[:, (4 * u + m) * P:(4 * u + m + 1) * P],
                                                    c["ident"][:, :])
                            last.then_inc(k_turned_done, 1)
                        pe.wait_ge(chunk_ready, h + 1)
                        pe.wait_ge(level_placed, MASKED * h + (MASKED if projects else 4))
                        for m in range(TILES):
                            last = pe.matmul(p_level[1][:, m:m + 1], qk[:, m * P:(m + 1) * P],
                                             c["ones_col"][:, :], start=True, stop=True)
                        last.then_inc(self_done, 1)
                    if projects and i >= 4:
                        multiply_level(n, i - 4, True)
                    if mixes and i == 4:
                        if not known_first(h):
                            pe.wait_ge(out_ready, 2 * h)
                        for u in range(2):
                            pe.wait_ge(k_turned_ready, 2 * h + u + 1)
                            for m in range(4 * u, min(4 * u + 4, TILES - 1)):
                                last = pe.matmul(p_misc[2 + u][:, m % 4, :], k_turned[:, m, :], value[b][:, m, :],
                                                 start=True, stop=True)
                            last.then_inc(update_done, 1)
                    if mixes and i == 5:
                        pe.wait_ge(last_placed, h + 1)
                        for u in range(2):
                            for m in range(4 * u, 4 * u + 4):
                                dst = p_misc[u][:, m % 4, :]
                                last = pe.matmul(dst, scores[b][:, m, :], value[b][:, m, :], start=True,
                                                 stop=(m == 0))
                                if m > 0:
                                    pe.wait_ge(state_ready, (TILES - 1) * h + m)
                                    last = pe.matmul(dst, q_chunk[:, m * P:(m + 1) * P], state[:, m, :],
                                                     start=False, stop=True)
                            last.then_inc(o_done, 1)
                    if mixes and not projects and i in START_AT:
                        pe.wait_ge(level_placed, MASKED * HEADS)
                        pe.wait_ge(last_placed, HEADS)
                        start_output_tile(pe, p_proj, w_qf_hi, w_qf_lo, ut_hi, ut_lo, link["m_ready"],
                                          w_out_ready, START_AT[i])
                    if mixes and i == 7:
                        pe.wait_ge(o_gated, h + 1)
                        for u in range(2):
                            pe.wait_ge(state_ready, (TILES - 1) * (h + 1))
                            for m in range(4):
                                last = pe.transpose(p_misc[2 + u][:, m, :], o[:, 4 * u + m, :], c["ident"][:, :])
                            last.then_inc(o_turned, 1)

            heads(pe, step)


_INS = ["x", "sb_norm", "sb_w_in", "sb_q_gain", "sb_k_gain", "sb_w_out",
        "hg_norm", "hg_w_in", "hg_o_gain", "hg_w_out", "hg_lb_logits"]


def kernel(**inputs):
    import numpy as _np
    import concourse.bacc as _bacc
    from concourse import mybir as _mybir
    from concourse.bass_utils import run_bass_kernel_spmd as _run

    nc = _bacc.Bacc("TRN2", target_bir_lowering=False, num_devices=1, dynamic_dma_scratch_size=1024)
    arrays, args = {}, []
    for name in _INS:
        a = _np.ascontiguousarray(inputs[name])
        arrays[f"in_{name}_dram"] = a
        args.append(nc.dram_tensor(f"in_{name}_dram", a.shape, _mybir.dt.from_np(a.dtype), kind="ExternalInput").ap())
    result = nc.dram_tensor("out_0_dram", inputs["x"].shape, _mybir.dt.float32, kind="ExternalOutput").ap()
    build_trunk(nc, *args, result)
    r = _run(nc, [arrays], core_ids=[0])
    return r.results[0]["out_0_dram"]
```
